# Optimizing a Trainium2 kernel written in Bass

```python
import math, functools
import jax, jax.numpy as jnp
from jax import lax
import numpy as np

D_MODEL = 1024
BATCH = 1
SEQ = 2048
DEPTH = 1
DEC_BATCH = 8
DEC_SEQ = 16
PAST_LEN = 512

CHUNK = 64
HEAD_DIM = 64
N_FOX_HEADS = 8
FOX_WIDTH = N_FOX_HEADS * HEAD_DIM
SSM_CH_PER_GROUP = 16
SSM_GROUPS = 16
SSM_WIDTH = SSM_GROUPS * SSM_CH_PER_GROUP
SSM_STATE = 64
N_MEM_HEADS = 4
MEM_WIDTH = N_MEM_HEADS * HEAD_DIM
N_MEM = 256
MIX_WIDTH = FOX_WIDTH + SSM_WIDTH + MEM_WIDTH
Q_BLOCK = 128
EPS = 1e-6
IN_SIZES = (FOX_WIDTH, FOX_WIDTH, FOX_WIDTH, FOX_WIDTH, N_FOX_HEADS, SSM_WIDTH, SSM_WIDTH, MEM_WIDTH, MEM_WIDTH)
IN_COLS = 4 * FOX_WIDTH + N_FOX_HEADS + 2 * SSM_WIDTH + 2 * MEM_WIDTH

kernel_name = "hybrid_fox_s5_memory_stream_step"

def rms_norm(x, g):
    xf = x.astype(jnp.float32)
    y = xf * lax.rsqrt(jnp.mean(xf * xf, axis=-1, keepdims=True) + EPS)
    return (y * g.astype(jnp.float32)).astype(x.dtype)

def split_columns(z):
    offs = []
    o = 0
    for s in IN_SIZES[:-1]:
        o += s
        offs.append(o)
    return jnp.split(z, offs, axis=-1)

def fox_block(q, k, v, cq, ck, q_pos, k_pos):
    s = jnp.einsum('bqhd,bkhd->bhqk', q, k).astype(jnp.float32) * (HEAD_DIM ** -0.5)
    s = s + jnp.swapaxes(cq, 1, 2)[..., :, None] - jnp.swapaxes(ck, 1, 2)[..., None, :]
    mask = k_pos[None, :] <= q_pos[:, None]
    p = jax.nn.softmax(jnp.where(mask, s, -jnp.inf), axis=-1)
    return jnp.einsum('bhqk,bkhd->bqhd', p.astype(v.dtype), v)

def fox_attention_prompt(q, k, v, logf):
    B, T, H, Dh = q.shape
    nb = T // Q_BLOCK
    c = jnp.cumsum(logf, axis=1)
    qb = jnp.swapaxes(q.reshape(B, nb, Q_BLOCK, H, Dh), 0, 1)
    cb = jnp.swapaxes(c.reshape(B, nb, Q_BLOCK, H), 0, 1)
    pos = jnp.arange(T)
    pb = pos.reshape(nb, Q_BLOCK)
    out = lax.map(lambda a: fox_block(a[0], k, v, a[1], c, a[2], pos), (qb, cb, pb))
    return jnp.swapaxes(out, 0, 1).reshape(B, T, H, Dh)

def fox_attention_sample(q, k, v, logf, cache_k, cache_v, cache_logf):
    P = cache_k.shape[1]
    T = q.shape[1]
    k_all = jnp.concatenate([cache_k.astype(k.dtype), k], axis=1)
    v_all = jnp.concatenate([cache_v.astype(v.dtype), v], axis=1)
    c_all = jnp.cumsum(jnp.concatenate([cache_logf.astype(jnp.float32), logf], axis=1), axis=1)
    return fox_block(q, k_all, v_all, c_all[:, P:], c_all, P + jnp.arange(T), jnp.arange(P + T))

def _complex_affine_combine(e1, e2):
    a1r, a1i, b1r, b1i = e1
    a2r, a2i, b2r, b2i = e2
    ar = a2r * a1r - a2i * a1i
    ai = a2r * a1i + a2i * a1r
    br = a2r * b1r - a2i * b1i + b2r
    bi = a2r * b1i + a2i * b1r + b2i
    return (ar, ai, br, bi)

def s5_mixer(u, h0_re, h0_im, a_re, a_im, log_dt, b_re, b_im, c_re, c_im, d, w_glu, b_glu):
    f32 = jnp.float32
    B, T, _ = u.shape
    uf = u.astype(f32).reshape(B, T, SSM_GROUPS, SSM_CH_PER_GROUP)
    dt = jnp.exp(log_dt.astype(f32))[:, None]
    ar, ai = a_re.astype(f32), a_im.astype(f32)
    mag = jnp.exp(dt * ar)
    abar_re = mag * jnp.cos(dt * ai)
    abar_im = mag * jnp.sin(dt * ai)
    den = ar * ar + ai * ai
    zr = ((abar_re - 1.0) * ar + abar_im * ai) / den
    zi = (abar_im * ar - (abar_re - 1.0) * ai) / den
    br, bi = b_re.astype(f32), b_im.astype(f32)
    bbar_re = zr[..., None] * br - zi[..., None] * bi
    bbar_im = zr[..., None] * bi + zi[..., None] * br
    bu_re = jnp.einsum('btgp,gnp->btgn', uf, bbar_re)
    bu_im = jnp.einsum('btgp,gnp->btgn', uf, bbar_im)
    a_seq_re = jnp.broadcast_to(abar_re, bu_re.shape)
    a_seq_im = jnp.broadcast_to(abar_im, bu_im.shape)
    acum_re, acum_im, h_re, h_im = lax.associative_scan(
        _complex_affine_combine, (a_seq_re, a_seq_im, bu_re, bu_im), axis=1)
    h0r = h0_re.astype(f32)[:, None]
    h0i = h0_im.astype(f32)[:, None]
    h_re = h_re + acum_re * h0r - acum_im * h0i
    h_im = h_im + acum_re * h0i + acum_im * h0r
    y = (jnp.einsum('gpn,btgn->btgp', c_re.astype(f32), h_re)
         - jnp.einsum('gpn,btgn->btgp', c_im.astype(f32), h_im)
         + d.astype(f32) * uf).reshape(B, T, SSM_WIDTH)
    g = jax.nn.gelu(y)
    out = g * jax.nn.sigmoid(g @ w_glu.astype(f32) + b_glu.astype(f32))
    return out.astype(u.dtype), h_re[:, -1], h_im[:, -1]

def memory_attention(q, mk, mv):
    s = jnp.einsum('bqhd,bkhd->bhqk', q, mk.astype(q.dtype)).astype(jnp.float32) * (HEAD_DIM ** -0.5)
    p = jax.nn.softmax(s, axis=-1)
    return jnp.einsum('bhqk,bkhd->bqhd', p.astype(q.dtype), mv.astype(q.dtype))

def memory_kv(mem, mem_norm, w_mem_kv, mem_k_norm):
    B, M, _ = mem.shape
    kv = rms_norm(mem, mem_norm) @ w_mem_kv
    mk, mv = jnp.split(kv, 2, axis=-1)
    mk = rms_norm(mk.reshape(B, M, N_MEM_HEADS, HEAD_DIM), mem_k_norm)
    return mk, mv.reshape(B, M, N_MEM_HEADS, HEAD_DIM)

def mixer_layer(x, w, fox_attend, h0_re, h0_im, mem_k, mem_v):
    (norm_g, w_in, b_forget, fox_q_norm, fox_k_norm, a_re, a_im, log_dt, b_re, b_im,
     c_re, c_im, d, w_glu, b_glu, mem_q_norm, w_out) = w
    B, T, _ = x.shape
    h = rms_norm(x, norm_g)
    fq, fk, fv, fg, ff, su, sg, mq, mg = split_columns(h @ w_in)
    fq = rms_norm(fq.reshape(B, T, N_FOX_HEADS, HEAD_DIM), fox_q_norm)
    fk = rms_norm(fk.reshape(B, T, N_FOX_HEADS, HEAD_DIM), fox_k_norm)
    fv = fv.reshape(B, T, N_FOX_HEADS, HEAD_DIM)
    logf = jax.nn.log_sigmoid(ff.astype(jnp.float32) + b_forget.astype(jnp.float32))
    fox_out = fox_attend(fq, fk, fv, logf).reshape(B, T, FOX_WIDTH) * jax.nn.silu(fg)
    ssm_y, h_re, h_im = s5_mixer(su, h0_re, h0_im, a_re, a_im, log_dt, b_re, b_im, c_re, c_im, d, w_glu, b_glu)
    ssm_out = ssm_y * jax.nn.silu(sg)
    mq = rms_norm(mq.reshape(B, T, N_MEM_HEADS, HEAD_DIM), mem_q_norm)
    mem_out = memory_attention(mq, mem_k, mem_v).reshape(B, T, MEM_WIDTH) * jax.nn.silu(mg)
    mix = jnp.concatenate([fox_out, ssm_out, mem_out], axis=-1) @ w_out
    return x + mix, fk, fv, logf, h_re, h_im

def setup_inputs(seed: int = 0) -> dict:
    key = jax.random.key(seed)
    ks = jax.random.split(key, 40)
    f32 = jnp.float32

    def nrm(k, shape, scale):
        return scale * jax.random.normal(k, shape, f32)

    inp = {}
    inp["x_prompt"] = nrm(ks[0], (BATCH, SEQ, D_MODEL), 1.0)
    inp["x_sample"] = nrm(ks[1], (DEC_BATCH, DEC_SEQ, D_MODEL), 1.0)
    inp["mem_prompt"] = nrm(ks[2], (BATCH, N_MEM, D_MODEL), 1.0)
    inp["cache_fox_k"] = nrm(ks[3], (DEPTH, DEC_BATCH, PAST_LEN, N_FOX_HEADS, HEAD_DIM), 1.0)
    inp["cache_fox_v"] = nrm(ks[4], (DEPTH, DEC_BATCH, PAST_LEN, N_FOX_HEADS, HEAD_DIM), 1.0)
    inp["cache_fox_logf"] = jax.nn.log_sigmoid(3.0 + nrm(ks[5], (DEPTH, DEC_BATCH, PAST_LEN, N_FOX_HEADS), 1.0))
    inp["state_ssm_re"] = nrm(ks[6], (DEPTH, DEC_BATCH, SSM_GROUPS, SSM_STATE), 0.5)
    inp["state_ssm_im"] = nrm(ks[7], (DEPTH, DEC_BATCH, SSM_GROUPS, SSM_STATE), 0.5)
    inp["cache_mem_k"] = nrm(ks[8], (DEPTH, DEC_BATCH, N_MEM, N_MEM_HEADS, HEAD_DIM), 1.0)
    inp["cache_mem_v"] = nrm(ks[9], (DEPTH, DEC_BATCH, N_MEM, N_MEM_HEADS, HEAD_DIM), 1.0)
    inp["norm_g"] = 1.0 + nrm(ks[10], (DEPTH, D_MODEL), 0.02)
    inp["w_in"] = nrm(ks[11], (DEPTH, D_MODEL, IN_COLS), D_MODEL ** -0.5)
    inp["b_forget"] = jnp.linspace(1.0, 6.0, N_FOX_HEADS, dtype=f32)[None, :] + nrm(ks[12], (DEPTH, N_FOX_HEADS), 0.1)
    inp["fox_q_norm"] = 1.0 + nrm(ks[13], (DEPTH, HEAD_DIM), 0.02)
    inp["fox_k_norm"] = 1.0 + nrm(ks[14], (DEPTH, HEAD_DIM), 0.02)
    inp["ssm_a_re"] = -0.5 + nrm(ks[15], (DEPTH, SSM_GROUPS, SSM_STATE), 0.01)
    inp["ssm_a_im"] = (math.pi * jnp.arange(SSM_STATE, dtype=f32))[None, None, :] + nrm(ks[16], (DEPTH, SSM_GROUPS, SSM_STATE), 0.01)
    inp["ssm_log_dt"] = jax.random.uniform(ks[17], (DEPTH, SSM_GROUPS), f32, math.log(1e-3), math.log(1e-1))
    inp["ssm_b_re"] = nrm(ks[18], (DEPTH, SSM_GROUPS, SSM_STATE, SSM_CH_PER_GROUP), (2 * SSM_CH_PER_GROUP) ** -0.5)
    inp["ssm_b_im"] = nrm(ks[19], (DEPTH, SSM_GROUPS, SSM_STATE, SSM_CH_PER_GROUP), (2 * SSM_CH_PER_GROUP) ** -0.5)
    inp["ssm_c_re"] = nrm(ks[20], (DEPTH, SSM_GROUPS, SSM_CH_PER_GROUP, SSM_STATE), SSM_STATE ** -0.5)
    inp["ssm_c_im"] = nrm(ks[21], (DEPTH, SSM_GROUPS, SSM_CH_PER_GROUP, SSM_STATE), SSM_STATE ** -0.5)
    inp["ssm_d"] = nrm(ks[22], (DEPTH, SSM_GROUPS, SSM_CH_PER_GROUP), 0.5)
    inp["w_glu"] = nrm(ks[23], (DEPTH, SSM_WIDTH, SSM_WIDTH), SSM_WIDTH ** -0.5)
    inp["b_glu"] = nrm(ks[24], (DEPTH, SSM_WIDTH), 0.01)
    inp["mem_norm"] = 1.0 + nrm(ks[25], (DEPTH, D_MODEL), 0.02)
    inp["w_mem_kv"] = nrm(ks[26], (DEPTH, D_MODEL, 2 * MEM_WIDTH), D_MODEL ** -0.5)
    inp["mem_q_norm"] = 1.0 + nrm(ks[27], (DEPTH, HEAD_DIM), 0.02)
    inp["mem_k_norm"] = 1.0 + nrm(ks[28], (DEPTH, HEAD_DIM), 0.02)
    inp["w_out"] = nrm(ks[29], (DEPTH, MIX_WIDTH, D_MODEL), MIX_WIDTH ** -0.5)
    return inp

def reference(x_prompt, x_sample, mem_prompt, cache_fox_k, cache_fox_v, cache_fox_logf,
              state_ssm_re, state_ssm_im, cache_mem_k, cache_mem_v,
              norm_g, w_in, b_forget, fox_q_norm, fox_k_norm, ssm_a_re, ssm_a_im, ssm_log_dt,
              ssm_b_re, ssm_b_im, ssm_c_re, ssm_c_im, ssm_d, w_glu, b_glu,
              mem_norm, w_mem_kv, mem_q_norm, mem_k_norm, w_out):
    xp, xs = x_prompt, x_sample
    pk, pv, pf, pre, pim, pmk, pmv = [], [], [], [], [], [], []
    sk, sv, sf, sre, sim = [], [], [], [], []
    for l in range(DEPTH):
        w = (norm_g[l], w_in[l], b_forget[l], fox_q_norm[l], fox_k_norm[l], ssm_a_re[l], ssm_a_im[l],
             ssm_log_dt[l], ssm_b_re[l], ssm_b_im[l], ssm_c_re[l], ssm_c_im[l], ssm_d[l], w_glu[l], b_glu[l],
             mem_q_norm[l], w_out[l])
        mk, mv = memory_kv(mem_prompt, mem_norm[l], w_mem_kv[l], mem_k_norm[l])
        h0 = jnp.zeros((xp.shape[0], SSM_GROUPS, SSM_STATE), jnp.float32)
        xp, k, v, lf, hr, hi = mixer_layer(xp, w, fox_attention_prompt, h0, h0, mk, mv)
        pk.append(k); pv.append(v); pf.append(lf); pre.append(hr); pim.append(hi)
        pmk.append(mk); pmv.append(mv)
        fox_sample = functools.partial(fox_attention_sample, cache_k=cache_fox_k[l],
                                       cache_v=cache_fox_v[l], cache_logf=cache_fox_logf[l])
        xs, k, v, lf, hr, hi = mixer_layer(xs, w, fox_sample, state_ssm_re[l], state_ssm_im[l],
                                           cache_mem_k[l], cache_mem_v[l])
        sk.append(k); sv.append(v); sf.append(lf); sre.append(hr); sim.append(hi)
    y_prompt, y_sample = xp, xs
    fox_k_prompt, fox_v_prompt, fox_logf_prompt = jnp.stack(pk), jnp.stack(pv), jnp.stack(pf)
    ssm_re_prompt, ssm_im_prompt = jnp.stack(pre), jnp.stack(pim)
    mem_k_prompt, mem_v_prompt = jnp.stack(pmk), jnp.stack(pmv)
    fox_k_sample, fox_v_sample, fox_logf_sample = jnp.stack(sk), jnp.stack(sv), jnp.stack(sf)
    ssm_re_sample, ssm_im_sample = jnp.stack(sre), jnp.stack(sim)
    return (y_prompt, y_sample, fox_k_prompt, fox_v_prompt, fox_logf_prompt, ssm_re_prompt, ssm_im_prompt,
            mem_k_prompt, mem_v_prompt, fox_k_sample, fox_v_sample, fox_logf_sample, ssm_re_sample, ssm_im_sample)


_drawn_inputs = setup_inputs


def setup_inputs(seed=0):
    import zlib

    import numpy as np

    out = dict(_drawn_inputs(seed))
    spreads = {}
    factors = {'cache_fox_logf': 4.755,
     'norm_g': 2.862,
     'fox_q_norm': 8.0,
     'fox_k_norm': 2.923,
     'ssm_a_re': 16.203,
     'w_glu': 3.486,
     'b_glu': 64.0,
     'mem_norm': 2.776,
     'mem_q_norm': 8.0,
     'mem_k_norm': 2.693}
    for name, (base, spread) in spreads.items():
        noise = np.random.default_rng([zlib.crc32(name.encode()), seed]).standard_normal(out[name].shape)
        drawn = base * np.exp(spread * noise) if base else spread * noise
        out[name] = __import__('jax').numpy.asarray(drawn.astype(out[name].dtype))
    for name, factor in factors.items():
        out[name] = (out[name] * factor).astype(out[name].dtype)
    return out
```

```python
from contextlib import ExitStack

import numpy as np

import concourse.bass as bass
from concourse import mybir

P = 128
D_MODEL = 1024
KC = D_MODEL // P
SEQ = 2048
DEC_BATCH = 8
DEC_SEQ = 16
TOKENS = SEQ + DEC_BATCH * DEC_SEQ
TILES = TOKENS // P
PROMPT_TILES = SEQ // P
PAST = 512
HD = 64
FOX_HEADS = 8
FOX = FOX_HEADS * HD
GROUPS = 16
CH = 16
SSM = GROUPS * CH
STATE = 64
MEM_HEADS = 4
MEM = MEM_HEADS * HD
N_MEM = 256
EPS = 1e-6
MASKED = -1e30

C_FQ, C_FK, C_FV, C_FG = 0, FOX, 2 * FOX, 3 * FOX
C_FF = 4 * FOX
C_SU = C_FF + FOX_HEADS
C_SG = C_SU + SSM
C_MQ = C_SG + SSM
C_MG = C_MQ + MEM
C_END = C_MG + MEM

F32 = mybir.dt.float32
F32R = mybir.dt.float32r
BF16 = mybir.dt.bfloat16
ALU = mybir.AluOpType
ACT = mybir.ActivationFunctionType
AX = mybir.AxisListType


class Place:

    def __init__(self, nc, stack, prefix):
        self.nc, self.stack, self.prefix, self.sems = nc, stack, prefix, []
        stack.callback(self.clear)

    def clear(self):
        if self.sems:
            self.nc.clear_and_free_semaphores(self.sems)
            self.nc.all_engine_barrier()

    def sb(self, name, shape, dt=F32):
        return self.stack.enter_context(self.nc.sbuf_tensor(f"{self.prefix}_{name}", shape, dt))

    def ps(self, name, shape, dt=F32):
        return self.stack.enter_context(self.nc.psum_tensor(f"{self.prefix}_{name}", shape, dt))

    def sem(self, name):
        self.sems.append(self.nc.alloc_semaphore(name=f"{self.prefix}_{name}"))
        return self.sems[-1]


def fl(ap):
    return ap.bitcast(F32)


def hold(eng, sem, value, s_held):
    eng.wait_ge(sem, value)
    eng.sem_inc(s_held, 1)


def constants_phase(nc, K):
    with ExitStack() as stack:
        a = Place(nc, stack, "cst")
        s_set = a.sem("set")
        block = stack.enter_context(nc.Block())

        @block.gpsimd
        def _(pool):
            nc.gpsimd.memset(K.ident[:, :], 0.0).then_inc(s_set, 1)
            nc.gpsimd.memset(K.identb[:, :], 0.0).then_inc(s_set, 1)
            nc.gpsimd.memset(K.causal[:, :], 0.0).then_inc(s_set, 1)
            nc.gpsimd.memset(K.neghalf[:, :], -0.5).then_inc(s_set, 1)
            nc.gpsimd.memset(K.one[:, :], 1.0).then_inc(s_set, 1)
            pool.wait_ge(s_set, 5)
            nc.gpsimd.affine_select(out=K.ident[:, :], in_=K.ident[:, :], compare_op=ALU.not_equal, fill=1.0,
                                    base=0, pattern=[[-1, P]], channel_multiplier=1).then_inc(s_set, 1)
            nc.gpsimd.affine_select(out=K.identb[:, :], in_=K.identb[:, :], compare_op=ALU.not_equal, fill=1.0,
                                    base=0, pattern=[[-1, P]], channel_multiplier=1).then_inc(s_set, 1)
            nc.gpsimd.affine_select(out=K.causal[:, :], in_=K.causal[:, :], compare_op=ALU.is_ge, fill=MASKED,
                                    base=0, pattern=[[-1, P]], channel_multiplier=1).then_inc(s_set, 1)


class Piece:

    def __init__(self, kind, n, nat=None, last=None, gain=None, scale=1.0, scratch=None, bias=None):
        self.kind, self.n, self.nat, self.last = kind, n, nat, last
        self.gain, self.scale, self.scratch, self.bias = gain, scale, scratch, bias
        self.heads = n // HD


def project(nc, K, name, sources, w_runs, w_dram, gain_dram, groups, schedule, banks_turned):
    ntiles = sum(n for _, n in sources)
    ncols = sum(n for _, n in w_runs)
    nruns = len(w_runs)
    looped = (sources[0][1] - 2) // 2 * 2 if ntiles > 4 else 0
    KT = banks_turned
    with ExitStack() as stack:
        a = Place(nc, stack, name)
        wh, wl = a.sb("wh", [P, KC, ncols], F32R), a.sb("wl", [P, KC, ncols], F32R)
        raw, gain = a.sb("raw", [P, 2, ncols]), a.sb("gain", [P, KC])
        x = a.sb("x", [P, 2, D_MODEL])
        xth, xtl = a.sb("xth", [P, 2, KC, P], F32R), a.sb("xtl", [P, 2, KC, P], F32R)
        ssq, var = a.sb("ssq", [P, 2]), a.sb("var", [P, 2])
        rstd, half = a.sb("rstd", [P, 2]), a.sb("half", [P, 2])
        squares = a.sb("squares", [P, D_MODEL])
        xt_ps = [a.ps(f"xt{i}", [P, 4, P]) for i in range(2)]
        g_ps = [a.ps(f"g{i}", [P, 512]) for i in range(len(groups))]
        tr_ps = [a.ps(f"tr{i}", [P, 4, P]) for i in range(2)]
        s_held_sp, s_held_pool = a.sem("held_sp"), a.sem("held_pool")
        s_w = [a.sem(f"w{i}") for i in range(2)]
        s_x = [a.sem(f"x{i}") for i in range(2)]
        s_wh, s_wl, s_gain = a.sem("w_hi"), a.sem("w_lo"), a.sem("gain")
        s_xt, s_xth, s_xtl = a.sem("x_turned"), a.sem("x_hi"), a.sem("x_lo")
        s_ssq, s_pool, s_rstd = a.sem("ssq"), a.sem("pool_chain"), a.sem("rstd")
        s_g = [a.sem(f"g{i}") for i in range(len(groups))]
        s_tr, s_tev = a.sem("turned"), a.sem("turned_read")
        act_reads, dve_reads = [[] for _ in groups], [[] for _ in groups]
        parts_gain = []
        for g, pieces in enumerate(groups):
            at = 0
            for i, p in enumerate(pieces):
                tag = f"{g}{i}"
                p.at, at = at, at + p.n
                p.s_stage = a.sem("stage" + tag)
                p.s_out = [a.sem(f"stored{tag}{b}") for b in range(2)]
                if p.kind in ("gate", "turned"):
                    m = p.n if p.kind == "gate" else p.n // 2
                    p.th, p.z = a.sb("th" + tag, [P, m]), a.sb("z" + tag, [P, m])
                    p.s_th, p.s_z = a.sem("tanh" + tag), a.sem("z" + tag)
                    act_reads[g].append(p.s_th)
                    dve_reads[g].append(p.s_z)
                if p.kind == "turned":
                    p.stage, p.s_su = a.sb("stage" + tag, [P, 4, P]), a.sem("su" + tag)
                if p.kind in ("gate", "plain", "heads"):
                    p.stage = a.sb("stage" + tag, [P, 2, p.n])
                if p.kind == "plain":
                    act_reads[g].append(p.s_stage)
                if p.kind == "heads":
                    p.sq, p.qn = a.sb("sq" + tag, [P, p.n]), a.sb("qn" + tag, [P, p.n])
                    p.hs, p.hv, p.hr = (a.sb(k + tag, [P, p.heads]) for k in ("hs", "hv", "hr"))
                    p.parts = a.sb("parts" + tag, [P, p.heads, 2 * HD])
                    p.turned = a.sb("turned" + tag, [P, 2, p.heads, P])
                    p.s_tout = [a.sem(f"tstored{tag}{b}") for b in range(2)]
                    p.s_sq, p.s_hs, p.s_hr, p.s_qn, p.s_hi, p.s_lo = (
                        a.sem(k + tag) for k in ("sq", "hsum", "hrstd", "qn", "hi", "lo"))
                    act_reads[g].append(p.s_sq)
                    dve_reads[g].append(p.s_qn)
                    p.gain_sb = a.sb("hgain" + tag, [P, HD])
                    parts_gain.append((p.gain_sb, p.gain))
                if p.kind == "logits":
                    p.bias_sb = a.sb("bias" + tag, [P, p.n])
                    dve_reads[g].append(p.s_stage)
                    parts_gain.append((p.bias_sb, p.bias))
        first, nbanks = {}, {}
        for step in schedule:
            if step[0] == "T":
                first[step[1]] = sum(nbanks.values())
                nbanks[step[1]] = sum(2 * p.n if p.kind == "heads" else p.n for p in groups[step[1]]
                                      if p.kind in ("heads", "turned")) // 512
        assert sum(nbanks.values()) == KT

        def rows(t):
            if isinstance(t, int) and t >= sources[0][1]:
                return sources[1][0]
            return sources[0][0][bass.ts(t, P), :]

        def tiles(eng, body):
            for t in range(2):
                body(t, t)
            if looped:
                with eng.Fori(1, looped // 2) as i:
                    for u in range(2):
                        body(i * 2 + u, u)
            for t in range(max(looped, 2), ntiles):
                body(t, t % 2)

        def last_tile(t):
            return isinstance(t, int) and t == ntiles - 1

        def bank(t, k):
            return k % 2 if KT % 2 == 0 else (t * KT + k) % 2

        def turned_pieces(g):
            return [p for p in groups[g] if p.kind in ("heads", "turned")]

        block = stack.enter_context(nc.Block())

        @block.sync
        def _(sp):
            sp.dma_start(gain[:, :], gain_dram.rearrange("(c p) -> p c", p=P), allow_slow_non_contiguous=True).then_inc(s_gain, 16)
            for dst, src in parts_gain:
                sp.dma_start(dst[:, :], src.partition_broadcast(P)).then_inc(s_gain, 16)
            for t in range(2):
                sp.dma_start(x[:, t, :], rows(t)).then_inc(s_x[t], 16)
            for c in range(KC):
                if c >= 2:
                    sp.wait_ge(s_wh, c - 1)
                    sp.wait_ge(s_wl, c - 1)
                at = 0
                for c0, n in w_runs:
                    sp.dma_start(raw[:, c % 2, at:at + n],
                                 w_dram[c * P:(c + 1) * P, c0:c0 + n]).then_inc(s_w[c % 2], 16)
                    at += n
            for pieces in groups:
                for p in pieces:
                    for b in range(2):
                        if p.nat:
                            sp.sem_inc(p.s_out[b], 16)
                        if p.kind == "heads":
                            sp.sem_inc(p.s_tout[b], 16)

            def body(t, u):
                if not isinstance(t, int) or t + 2 < ntiles:
                    sp.wait_ge(s_xt, (t + 1) * 2)
                    sp.wait_ge(s_ssq, t + 1)
                    sp.dma_start(x[:, u, :], rows(t + 2)).then_inc(s_x[u], 16)
                for step in schedule:
                    if step[0] == "G":
                        for p in groups[step[1]]:
                            if p.nat:
                                sp.wait_ge(p.s_stage, t + 1)
                                sp.dma_start(p.nat(t), p.stage[:, u, :]).then_inc(p.s_out[u], 16)
                            if p.last is not None and last_tile(t):
                                sp.wait_ge(p.s_stage, t + 1)
                                sp.dma_start(p.last, p.stage[:, u, :]).then_inc(p.s_out[u], 16)
                    if step[0] == "T":
                        for p in groups[step[1]]:
                            if p.kind == "heads":
                                hold(sp, s_tev, t * KT + first[step[1]] + nbanks[step[1]] + 1, s_held_sp)
                                sp.dma_start(p.scratch[:, :, bass.ts(t, P)].rearrange("h p t -> p h t"),
                                             p.turned[:, u, :, :]).then_inc(p.s_tout[u], 16)

            tiles(sp, body)
            for pieces in groups:
                for p in pieces:
                    for b in range(2):
                        if p.nat:
                            sp.wait_ge(p.s_out[b], 16 * (1 + (ntiles + 1 - b) // 2))
                        if p.kind == "heads":
                            sp.wait_ge(p.s_tout[b], 16 * (1 + (ntiles + 1 - b) // 2))
                    if p.last is not None:
                        sp.wait_ge(p.s_out[(ntiles - 1) % 2], 16)

        @block.tensor
        def _(pe):
            def turn_x(t, u):
                pe.wait_ge(s_x[u], (t - u) * 8 + 16)
                pe.wait_ge(s_xtl, t * 2)
                for h in range(2):
                    for c in range(4):
                        at = (4 * h + c) * P
                        last = nc.tensor.transpose(xt_ps[h][:, c, :], x[:, u, at:at + P], K.ident[:, :])
                    last.then_inc(s_xt, 1)

            def body(t, u):
                for step in schedule:
                    if step[0] == "X" and not last_tile(t):
                        turn_x(t + 1, 1 - u)
                    if step[0] == "G":
                        g = step[1]
                        at = sum(p.n for ps in groups[:g] for p in ps)
                        n = sum(p.n for p in groups[g])
                        pe.wait_ge(s_xtl, (t + 1) * 2)
                        for s in act_reads[g] + dve_reads[g]:
                            pe.wait_ge(s, t)
                        for c in range(KC):
                            for k, (xs, ws) in enumerate(((xth, wh), (xtl, wh), (xth, wl))):
                                last = nc.tensor.matmul(g_ps[g][:, 0:n], xs[:, u, c, :], ws[:, c, at:at + n],
                                                        start=(c == 0 and k == 0), stop=(c == KC - 1 and k == 2))
                        last.then_inc(s_g[g], 1)
                    if step[0] == "T":
                        g = step[1]
                        k = first[g]
                        for p in turned_pieces(g):
                            if p.kind == "heads":
                                pe.wait_ge(p.s_lo, t + 1)
                                blocks = [p.parts[:, j, :] for j in range(p.heads)]
                            else:
                                pe.wait_ge(p.s_su, t + 1)
                                pe.wait_ge(p.s_stage, t + 1)
                                blocks = [p.stage[:, j, :] for j in range(4)]
                            for j, b in enumerate(blocks):
                                if j % 4 == 0:
                                    pe.wait_ge(s_tev, t * KT + k)
                                last = nc.tensor.transpose(tr_ps[bank(t, k)][:, j % 4, :], b, K.ident[:, :])
                                if j % 4 == 3:
                                    last.then_inc(s_tr, 1)
                                    k += 1

            pe.sem_inc(s_tr, KT)
            turn_x(0, 0)
            pe.wait_ge(s_wl, KC)
            tiles(pe, body)

        @block.scalar
        def _(act):
            act.wait_ge(s_gain, 16 * (1 + len(parts_gain)))
            for c in range(KC):
                act.wait_ge(s_w[c % 2], 16 * nruns * (c // 2 + 1))
                nc.scalar.activation(wh[:, c, :], raw[:, c % 2, :], ACT.Copy, scale=gain[:, c:c + 1]).then_inc(s_wh, 1)
            act.sem_inc(s_tev, 1)

            def split_x(t, u):
                for h in range(2):
                    act.wait_ge(s_xt, t * 2 + h + 1)
                    nc.scalar.activation(xth[:, u, 4 * h:4 * h + 4, :], xt_ps[h][:, :, :], ACT.Copy).then_inc(s_xth, 1)
                act.wait_ge(s_x[u], (t - u) * 8 + 16)
                act.wait_ge(s_ssq, t)
                nc.scalar.activation(squares[:, :], x[:, u, :], ACT.Square, accum_out=ssq[:, u:u + 1]).then_inc(s_ssq, 1)

            def body(t, u):
                for step in schedule:
                    if step[0] == "X" and not last_tile(t):
                        split_x(t + 1, 1 - u)
                    if step[0] == "G":
                        g = step[1]
                        act.wait_ge(s_g[g], t + 1)
                        act.wait_ge(s_rstd, t + 1)
                        for p in groups[g]:
                            src = g_ps[g][:, p.at:p.at + p.n]
                            if p.kind in ("gate", "turned"):
                                act.wait_ge(p.s_stage, t)
                                nc.scalar.activation(p.th[:, :], src[:, p.n // 2:] if p.kind == "turned" else src,
                                                     ACT.Tanh, scale=half[:, u:u + 1]).then_inc(p.s_th, 1)
                            if p.kind == "plain":
                                act.wait_ge(p.s_out[u], (t - u) * 8 + 16)
                                nc.scalar.activation(p.stage[:, u, :], src, ACT.Copy,
                                                     scale=rstd[:, u:u + 1]).then_inc(p.s_stage, 1)
                            if p.kind == "heads":
                                act.wait_ge(p.s_hs, t)
                                nc.scalar.activation(p.sq[:, :], src, ACT.Square,
                                                     scale=rstd[:, u:u + 1]).then_inc(p.s_sq, 1)
                        for p in groups[g]:
                            if p.kind == "heads":
                                act.wait_ge(p.s_stage, t + 1)
                                act.wait_ge(s_tr, t * KT + first[g] + nbanks[g])
                                nc.scalar.activation(p.parts[:, :, 0:HD].bitcast(F32R),
                                                     p.stage[:, u, :].rearrange("p (h d) -> p h d", d=HD),
                                                     ACT.Copy).then_inc(p.s_hi, 1)
                    if step[0] == "T":
                        g = step[1]
                        k = first[g]
                        for p in turned_pieces(g):
                            if p.kind == "heads":
                                act.wait_ge(p.s_tout[u], (t - u) * 8 + 16)
                                for j in range(p.heads // 4):
                                    act.wait_ge(s_tr, t * KT + KT + k + 1)
                                    nc.scalar.activation(p.turned[:, u, 4 * j:4 * j + 4, :], tr_ps[bank(t, k)][:, :, :],
                                                         ACT.Copy).then_inc(s_tev, 1)
                                    k += 1
                            else:
                                act.wait_ge(s_tr, t * KT + KT + k + 1)
                                for c in range(2):
                                    nc.scalar.activation(
                                        K.su[:, c, :, bass.ts(t, P // 8)],
                                        tr_ps[bank(t, k)][:, c, :].rearrange("p (j s) -> p s j", s=8), ACT.Copy)
                                nc.scalar.activation(K.sg[:, :, :, bass.ts(t, P // 8)].rearrange("p c s j -> p c j s"),
                                                     tr_ps[bank(t, k)][:, 2:4, :].rearrange("p c (j s) -> p c j s", s=8),
                                                     ACT.Copy).then_inc(s_tev, 1)
                                k += 1

            split_x(0, 0)
            tiles(act, body)

        @block.vector
        def _(dve):
            dve.wait_ge(s_gain, 16 * (1 + len(parts_gain)))
            for c in range(KC):
                dve.wait_ge(s_wh, c + 1)
                nc.vector.scalar_tensor_tensor(wl[:, c, :], raw[:, c % 2, :], gain[:, c:c + 1], fl(wh[:, c, :]),
                                               ALU.mult, ALU.subtract).then_inc(s_wl, 1)

            def split_x(t, u):
                for h in range(2):
                    dve.wait_ge(s_xth, t * 2 + h + 1)
                    nc.vector.tensor_tensor(xtl[:, u, 4 * h:4 * h + 4, :], xt_ps[h][:, :, :],
                                            fl(xth[:, u, 4 * h:4 * h + 4, :]), ALU.subtract).then_inc(s_xtl, 1)

            def body(t, u):
                for step in schedule:
                    if step[0] == "X" and not last_tile(t):
                        split_x(t + 1, 1 - u)
                    if step[0] != "G":
                        continue
                    g = step[1]
                    dve.wait_ge(s_g[g], t + 1)
                    dve.wait_ge(s_rstd, t + 1)
                    for s in act_reads[g]:
                        dve.wait_ge(s, t + 1)
                    for p in groups[g]:
                        src = g_ps[g][:, p.at:p.at + p.n]
                        if p.kind == "gate":
                            nc.vector.tensor_scalar(p.z[:, :], src, half[:, u:u + 1], None, ALU.mult).then_inc(p.s_z, 1)
                            dve.wait_ge(p.s_z, t + 1)
                            dve.wait_ge(p.s_th, t + 1)
                            dve.wait_ge(p.s_out[u], (t - u) * 8 + 16)
                            nc.vector.scalar_tensor_tensor(p.stage[:, u, :], p.th[:, :], 1.0, p.z[:, :],
                                                           ALU.add, ALU.mult).then_inc(p.s_stage, 1)
                        if p.kind == "turned":
                            dve.wait_ge(s_tr, t * KT + first[g] + nbanks[g])
                            n = p.n // 2
                            nc.vector.tensor_scalar(p.stage[:, 0:2, :], src[:, 0:n].rearrange("p (c n) -> p c n", c=2),
                                                    rstd[:, u:u + 1], None, ALU.mult).then_inc(p.s_su, 1)
                            nc.vector.tensor_scalar(p.z[:, :], src[:, n:], half[:, u:u + 1], None,
                                                    ALU.mult).then_inc(p.s_z, 1)
                            dve.wait_ge(p.s_z, t + 1)
                            dve.wait_ge(p.s_th, t + 1)
                            nc.vector.scalar_tensor_tensor(p.stage[:, 2:4, :],
                                                           p.th[:, :].rearrange("p (c n) -> p c n", c=2), 1.0,
                                                           p.z[:, :].rearrange("p (c n) -> p c n", c=2),
                                                           ALU.add, ALU.mult).then_inc(p.s_stage, 1)
                        if p.kind == "logits":
                            nc.vector.scalar_tensor_tensor(K.logits[:, bass.ts(t, FOX_HEADS)], src, rstd[:, u:u + 1],
                                                           p.bias_sb[:, :], ALU.mult, ALU.add).then_inc(p.s_stage, 1)
                        if p.kind == "heads":
                            by_head = "p (h d) -> p h d"
                            dve.wait_ge(p.s_sq, t + 1)
                            dve.wait_ge(p.s_hr, t)
                            nc.vector.tensor_reduce(p.hs[:, :], p.sq[:, :].rearrange(by_head, d=HD), AX.X,
                                                    ALU.add).then_inc(p.s_hs, 1)
                            dve.wait_ge(p.s_hr, t + 1)
                            nc.vector.tensor_tensor(p.qn[:, :].rearrange(by_head, d=HD), src.rearrange(by_head, d=HD),
                                                    p.hr[:, :, None].to_broadcast([P, p.heads, HD]),
                                                    ALU.mult).then_inc(p.s_qn, 1)
                            dve.wait_ge(p.s_qn, t + 1)
                            if p.nat:
                                dve.wait_ge(p.s_out[u], (t - u) * 8 + 16)
                            nc.vector.tensor_tensor(p.stage[:, u, :].rearrange(by_head, d=HD),
                                                    p.qn[:, :].rearrange(by_head, d=HD),
                                                    p.gain_sb[:, None, :].to_broadcast([P, p.heads, HD]),
                                                    ALU.mult).then_inc(p.s_stage, 1)
                            dve.wait_ge(p.s_hi, t + 1)
                            nc.vector.tensor_tensor(p.parts[:, :, HD:2 * HD].bitcast(F32R),
                                                    p.stage[:, u, :].rearrange(by_head, d=HD), p.parts[:, :, 0:HD],
                                                    ALU.subtract).then_inc(p.s_lo, 1)

            split_x(0, 0)
            tiles(dve, body)

        @block.gpsimd
        def _(pool):
            heads = [p for ps in groups for p in ps if p.kind == "heads"]
            per_tile = 2 + 2 * len(heads)

            def row_rms(t, u, base):
                hold(pool, s_ssq, t + 1, s_held_pool)
                nc.gpsimd.tensor_scalar(var[:, 0:1], ssq[:, u:u + 1], 1.0 / D_MODEL, EPS, ALU.mult,
                                        ALU.add).then_inc(s_pool, 1)
                pool.wait_ge(s_pool, base + 1)
                nc.gpsimd.tensor_tensor(rstd[:, u:u + 1], var[:, 0:1], K.neghalf[:, 0:1], ALU.pow).then_inc(s_pool, 1)
                hold(pool, s_pool, base + 2, s_held_pool)
                nc.gpsimd.tensor_scalar(half[:, u:u + 1], rstd[:, u:u + 1], 0.5, None, ALU.mult).then_inc(s_rstd, 1)

            def body(t, u):
                n = 0
                for step in schedule:
                    base = t * per_tile + 2 + n
                    if step[0] == "X" and not last_tile(t):
                        for s in sum(dve_reads, []):
                            pool.wait_ge(s, t)
                        row_rms(t + 1, 1 - u, base)
                        n += 2
                    if step[0] == "G":
                        for p in groups[step[1]]:
                            if p.kind != "heads":
                                continue
                            base = t * per_tile + 2 + n
                            hold(pool, p.s_hs, t + 1, s_held_pool)
                            nc.gpsimd.tensor_scalar(p.hs[:, :], p.hs[:, :], 1.0 / HD, EPS, ALU.mult,
                                                    ALU.add).then_inc(s_pool, 1)
                            pool.wait_ge(s_pool, base + 1)
                            nc.gpsimd.tensor_tensor(p.hv[:, :], p.hs[:, :], K.neghalf[:, 0:p.heads],
                                                    ALU.pow).then_inc(s_pool, 1)
                            pool.wait_ge(p.s_qn, t)
                            hold(pool, s_pool, base + 2, s_held_pool)
                            nc.gpsimd.tensor_scalar(p.hr[:, :], p.hv[:, :], rstd[:, u:u + 1], p.scale,
                                                    ALU.mult, ALU.mult).then_inc(p.s_hr, 1)
                            n += 2

            row_rms(0, 0, 0)
            tiles(pool, body)


def decay_phase(nc, K, D):
    NG = TILES * FOX_HEADS
    with ExitStack() as stack:
        a = Place(nc, stack, "decay")
        e, ab, lf = a.sb("exp", [P, NG]), a.sb("abs", [P, NG]), a.sb("logf", [P, NG])
        cache = a.sb("cache", [P, PAST // P, DEC_BATCH, FOX_HEADS])
        rows = a.sb("rows", [FOX_HEADS, SEQ])
        csum = a.sb("csum", [FOX_HEADS, SEQ])
        ones = a.sb("ones", [DEC_BATCH * FOX_HEADS, SEQ])
        hi, lo = a.sb("hi", [FOX_HEADS, SEQ], F32R), a.sb("lo", [FOX_HEADS, SEQ], F32R)
        srows = a.sb("srows", [DEC_BATCH * FOX_HEADS, PAST + DEC_SEQ])
        ssum = a.sb("ssum", [DEC_BATCH * FOX_HEADS, PAST + DEC_SEQ])
        ps = [a.ps(f"t{i}", [P, 4, P]) for i in range(5)]
        s_cache, s_abs, s_e, s_ln, s_lf = (a.sem(k) for k in ("cache", "abs", "exp", "ln", "logf"))
        s_out, s_back, s_t, s_rows, s_ones = (a.sem(k) for k in ("stored", "back", "turned", "rows", "ones"))
        s_sum, s_hi, s_parts, s_end = (a.sem(k) for k in ("sum", "hi", "parts", "end"))
        block = stack.enter_context(nc.Block())
        C = FOX_HEADS
        NS = DEC_BATCH * C

        @block.sync
        def _(sp):
            for k in range(PAST // P):
                sp.dma_start(cache[:, k, :, :], D.cache_logf[:, k * P:(k + 1) * P, :].rearrange("b p h -> p b h"))\
                    .then_inc(s_cache, 16)
            sp.wait_ge(s_lf, 1)
            sp.dma_start(D.o_logf.rearrange("(t p) h -> p t h", p=P),
                         lf[:, 0:PROMPT_TILES * C].rearrange("p (t h) -> p t h", h=C)).then_inc(s_out, 16)
            sp.dma_start(D.o_logf_s, lf[:, PROMPT_TILES * C:NG]).then_inc(s_back, 16)
            sp.wait_ge(s_back, 16)
            for b in range(DEC_BATCH):
                sp.dma_start(srows[b * C:(b + 1) * C, PAST:],
                             D.o_logf_s[b * DEC_SEQ:(b + 1) * DEC_SEQ, :].rearrange("t h -> h t"),
                             allow_slow_non_contiguous=True).then_inc(s_back, 16)
            sp.wait_ge(s_parts, 1)
            for part, src in ((0, hi), (1, lo)):
                sp.dma_start(D.decay[:, part, :], fl(src[:, :])).then_inc(s_out, 16)
            sp.wait_ge(s_sum, 2)
            sp.dma_start(D.decay_s.rearrange("b h t -> (b h) t"), ssum[:, :]).then_inc(s_out, 16)
            sp.wait_ge(s_out, 64)

        @block.gpsimd
        def _(pool):
            nc.gpsimd.memset(ones[:, :], 1.0).then_inc(s_ones, 1)

        @block.scalar
        def _(act):
            act.wait_ge(s_abs, 1)
            nc.scalar.activation(e[:, :], ab[:, :], ACT.Exp, scale=-1.0).then_inc(s_e, 1)
            act.wait_ge(s_e, 1)
            nc.scalar.activation(ab[:, :], e[:, :], ACT.Ln, bias=K.one[:, 0:1]).then_inc(s_ln, 1)
            act.wait_ge(s_sum, 1)
            nc.scalar.activation(hi[:, :], csum[:, :], ACT.Copy).then_inc(s_hi, 1)

        @block.vector
        def _(dve):
            nc.vector.scalar_tensor_tensor(ab[:, :], K.logits[:, :], -1.0, K.logits[:, :], ALU.mult, ALU.max).then_inc(s_abs, 1)
            dve.wait_ge(s_ln, 1)
            nc.vector.scalar_tensor_tensor(lf[:, :], K.logits[:, :], 0.0, ab[:, :], ALU.min,
                                           ALU.subtract).then_inc(s_lf, 1)
            for i in range(4):
                dve.wait_ge(s_t, i + 1)
                nc.vector.tensor_copy(rows[:, i * 512:(i + 1) * 512], ps[i][0:C, :, :].rearrange("p a b -> p (a b)"))\
                    .then_inc(s_rows, 1)
            dve.wait_ge(s_ones, 1)
            dve.wait_ge(s_rows, 4)
            nc.vector.tensor_tensor_scan(csum[:, :], ones[0:C, :], rows[:, :], 0.0, ALU.mult,
                                         ALU.subtract).then_inc(s_sum, 1)
            dve.wait_ge(s_t, 5)
            nc.vector.tensor_copy(srows[:, 0:PAST], ps[4][0:NS, :, :].rearrange("p a b -> p (a b)")).then_inc(s_rows, 1)
            dve.wait_ge(s_rows, 5)
            dve.wait_ge(s_back, 16 * (1 + DEC_BATCH))
            nc.vector.tensor_tensor_scan(ssum[:, :], ones[0:NS, 0:PAST + DEC_SEQ], srows[:, :], 0.0, ALU.mult,
                                         ALU.subtract).then_inc(s_sum, 1)
            dve.wait_ge(s_hi, 1)
            nc.vector.tensor_tensor(lo[:, :], csum[:, :], fl(hi[:, :]), ALU.subtract).then_inc(s_parts, 1)

        @block.tensor
        def _(pe):
            pe.wait_ge(s_lf, 1)
            for i in range(4):
                for j in range(4):
                    last = nc.tensor.transpose(ps[i][0:C, j, :], lf[:, (4 * i + j) * C:(4 * i + j + 1) * C],
                                               K.ident[:, :])
                last.then_inc(s_t, 1)
            pe.wait_ge(s_cache, 16 * (PAST // P))
            for k in range(PAST // P):
                last = nc.tensor.transpose(ps[4][0:NS, k, :], cache[:, k, :, :].rearrange("p b h -> p (b h)"),
                                           K.ident[:, :])
            last.then_inc(s_t, 1)


def ssm_phase(nc, K, D, I, O):
    L = 16
    PAIRS = GROUPS // 2
    NB = SEQ // L
    NBS = NB + DEC_BATCH
    J = TOKENS // 8
    PAD = 7 * CH
    LEVELS = NB.bit_length() - 1
    NS = PAIRS * DEC_BATCH
    c1 = 6.28125
    c2 = round((2 * np.pi - c1) * 2 ** 21) / 2 ** 21
    c3 = 2 * np.pi - c1 - c2
    ROUND = 12582912.0
    RE, IM = 0, 1

    with ExitStack() as stack:
        a = Place(nc, stack, "ssm")
        prm = a.sb("prm", [P, 3, PAIRS])
        are, aim, log_dt = (prm[:, k, :] for k in range(3))
        dt, decay, theta, turns, ang, ang2, mag, cos, sin, den, rden, am1, zr, zi, x1, x2 = (
            a.sb(k, [P, PAIRS])[:, :] for k in ("dt", "decay", "theta", "turns", "ang", "ang2", "mag", "cos", "sin",
                                                "den", "rden", "am1", "zr", "zi", "x1", "x2"))
        braw = a.sb("braw", [P, 2, PAIRS, CH])
        craw = a.sb("craw", [P, 2, P])
        ct = a.sb("ct", [P, 2, PAIRS, CH])
        bbar = a.sb("bbar", [P, 2, PAIRS, CH])
        pw, pw_rev = a.sb("pw", [P, 2, L + 1, PAIRS]), a.sb("pw_rev", [P, 2, L, PAIRS])
        lvl = a.sb("lvl", [P, 2, LEVELS, PAIRS])
        wb = a.sb("wb", [P, 2, PAIRS, L, CH])
        wbt = a.sb("wbt", [P, PAIRS, 2, 2, P])
        ca = a.sb("ca", [P, 2, PAIRS, L + 1, CH])
        t1, t2 = a.sb("t1", [P, PAIRS * (L + 1) * CH]), a.sb("t2", [P, PAIRS * (L + 1) * CH])
        kern_mem = a.sb("kern", [P, GROUPS * (PAD + L * CH)])
        kern = kern_mem[0:CH, :].rearrange("p (g n) -> p g n", g=GROUPS)
        final = kern_mem[:, 0:2 * 8 * J].rearrange("p (m j s) -> p m j s", m=2, s=8)
        skip = a.sb("skip", [CH, GROUPS, CH])
        toep = a.sb("toep", [P, GROUPS, L * CH])
        u = a.sb("u", [P, GROUPS, J])
        hraw = a.sb("hraw", [NS, 2, P])
        scan = [a.sb("scan0", [P, 2, PAIRS, NBS]), a.sb("scan1", [P, 2, PAIRS, NB])]
        before = a.sb("before", [P, 2, PAIRS, NBS])
        end_p, end_s = a.sb("end_p", [P, 2, PAIRS]), a.sb("end_s", [P, 2, NS])
        out_p, out_s = a.sb("out_p", [PAIRS, 2, P]), a.sb("out_s", [NS, 2, P])
        wglu, bglu, bhalf = a.sb("wglu", [P, 2, SSM]), a.sb("bglu", [P, 2]), a.sb("bhalf", [P, 2])
        gt = a.sb("gt", [P, 2, J])
        ps = [a.ps(f"p{i}", [P, 512]) for i in range(8)]
        (s_load, s_exp, s_prm, s_trig, s_wb, s_wbt, s_mats, s_ct, s_bc, s_kern, s_kread, s_kdone, s_toep, s_uin, s_h0,
         s_drive, s_dread, s_before, s_y, s_yread, s_sq, s_poly, s_tanh, s_gelu, s_yt, s_glu, s_gtanh, s_final, s_ends,
         s_eread, s_state, s_stored, s_dve) = (a.sem(k) for k in (
             "load exp prm trig wb wbt mats ct bc kern kread kdone toep uin h0 drive dread before y yread sq poly "
             "tanh gelu yt glu gtanh final ends eread state stored dve").split())
        NLOAD = 2 + 2 + 1 + 2 + 2 * PAIRS + 1 + 2 * PAIRS + 2
        CHUNK = GROUPS // 4 * J
        block = stack.enter_context(nc.Block())

        def ys(k):
            return u[:, 4 * k:4 * k + 4, :].rearrange("p g j -> p (g j)")

        def channels(g, s):
            return K.su[g % 8 * CH:(g % 8 + 1) * CH, g // 8, s, :]

        @block.sync
        def _(sp):
            def load(dst, src):
                sp.dma_start(dst, src).then_inc(s_load, 16)

            with nc.allow_non_contiguous_dma(reason="parameters: a thousand words each"):
                load(are, I["ssm_a_re"][0].rearrange("(g r) n -> (r n) g", r=2))
                load(aim, I["ssm_a_im"][0].rearrange("(g r) n -> (r n) g", r=2))
                for r in range(2):
                    load(prm[r * STATE:(r + 1) * STATE, 2, :],
                         I["ssm_log_dt"][0].rearrange("(g r) -> r g", r=2)[r, :].partition_broadcast(STATE))
                load(bglu[:, :], I["b_glu"][0].rearrange("(c p) -> p c", p=P))
            for k, b in enumerate((I["ssm_b_re"], I["ssm_b_im"])):
                load(braw[:, k, :, :], b[0].rearrange("(g r) n q -> (r n) g q", r=2))
            for k, c in enumerate((I["ssm_c_re"], I["ssm_c_im"])):
                for g in range(PAIRS):
                    load(craw[g * CH:(g + 1) * CH, k, :].rearrange("p (r n) -> p r n", r=2),
                         c[0, 2 * g:2 * g + 2, :, :].rearrange("r p n -> p r n"))
            load(skip[:, :, :].rearrange("q g p -> q (g p)"),
                 I["ssm_d"][0].rearrange("g p -> (g p)").partition_broadcast(CH))
            for k, h in enumerate((I["state_ssm_re"], I["state_ssm_im"])):
                for g in range(PAIRS):
                    load(hraw[g * DEC_BATCH:(g + 1) * DEC_BATCH, k, :],
                         h[0, :, 2 * g:2 * g + 2, :].rearrange("b r n -> b (r n)"))
            for c in range(2):
                load(wglu[:, c, :], I["w_glu"][0, c * P:(c + 1) * P, :])
            for s in range(8):
                for g in range(GROUPS):
                    sp.dma_start(u[s * CH:(s + 1) * CH, g, :], channels(g, s)).then_inc(s_uin, 16)
            sp.wait_ge(s_kdone, 1)
            for s in range(8):
                sp.dma_start(toep[s * CH:(s + 1) * CH, :, :],
                             kern[:, :, PAD - s * CH:PAD - s * CH + L * CH]).then_inc(s_toep, 16)
            sp.wait_ge(s_uin, 16 * 8 * GROUPS)
            sp.wait_ge(s_gelu, 4)
            for s in range(8):
                for g in range(GROUPS):
                    sp.dma_start(channels(g, s), u[s * CH:(s + 1) * CH, g, :]).then_inc(s_yt, 16)
            sp.wait_ge(s_eread, 4)
            for k, (po, so) in enumerate((("ssm_re_prompt", "ssm_re_sample"), ("ssm_im_prompt", "ssm_im_sample"))):
                sp.dma_start(O[po][0, 0].rearrange("(g r) n -> g (r n)", r=2), out_p[:, k, :]).then_inc(s_stored, 16)
                for g in range(PAIRS):
                    sp.dma_start(O[so][0, :, 2 * g:2 * g + 2, :].rearrange("b r n -> b (r n)"),
                                 out_s[g * DEC_BATCH:(g + 1) * DEC_BATCH, k, :]).then_inc(s_stored, 16)
            for m in range(2):
                sp.wait_ge(s_final, 8 * (m + 1))
                sp.dma_start(D.ssm[m * P:(m + 1) * P, :], final[:, m, :, :].rearrange("p j s -> p (j s)"))\
                    .then_inc(s_stored, 16)
            sp.wait_ge(s_stored, 16 * (2 * (1 + PAIRS) + 2))

        @block.scalar
        def _(act):
            act.wait_ge(s_load, 16 * NLOAD)
            nc.scalar.activation(dt, log_dt, ACT.Exp).then_inc(s_exp, 1)
            act.wait_ge(s_prm, 1)
            nc.scalar.activation(mag, decay, ACT.Exp).then_inc(s_trig, 1)
            nc.scalar.activation(sin, ang, ACT.Sin).then_inc(s_trig, 1)
            nc.scalar.activation(cos, ang2, ACT.Sin).then_inc(s_trig, 1)
            for g in range(PAIRS):
                act.wait_ge(s_wbt, g + 1)
                nc.scalar.activation(wbt[:, g, :, :, :].rearrange("p a b c -> p (a b c)"), ps[g % 2][:, :],
                                     ACT.Copy).then_inc(s_mats, 1)
            for k in range(4):
                act.wait_ge(s_yread, 4 * (k + 1))
                act.wait_ge(s_gelu, k)
                nc.scalar.activation(t1[:, 0:CHUNK], ys(k), ACT.Square).then_inc(s_sq, 1)
                act.wait_ge(s_poly, k + 1)
                nc.scalar.activation(t1[:, 0:CHUNK], t2[:, 0:CHUNK], ACT.Tanh,
                                     scale=float(np.sqrt(2 / np.pi))).then_inc(s_tanh, 1)
            for n in range(16):
                act.wait_ge(s_glu, n + 1)
                if n >= 2:
                    act.wait_ge(s_final, n - 1)
                nc.scalar.activation(gt[:, n % 2, :], ps[n % 2][:, 0:J], ACT.Tanh, scale=0.25,
                                     bias=bhalf[:, n // 8:n // 8 + 1]).then_inc(s_gtanh, 1)

        @block.vector
        def _(dve):
            steps = [0]

            def do(ins):
                steps[0] += 1
                ins.then_inc(s_dve, 1)
                dve.wait_ge(s_dve, steps[0])

            V = nc.vector

            def mul(o, x, y):
                do(V.tensor_tensor(o, x, y, ALU.mult))

            def cmul(o_re, o_im, x_re, x_im, y_re, y_im, p, q):
                mul(p, x_re, y_re)
                mul(q, x_im, y_im)
                do(V.tensor_tensor(o_re, p, q, ALU.subtract))
                mul(p, x_re, y_im)
                mul(q, x_im, y_re)
                do(V.tensor_tensor(o_im, p, q, ALU.add))

            dve.wait_ge(s_load, 16 * NLOAD)
            do(V.tensor_scalar(bhalf[:, :], bglu[:, :], 0.5, None, ALU.mult))
            dve.wait_ge(s_exp, 1)
            mul(decay, dt, are)
            mul(theta, dt, aim)
            do(V.tensor_scalar(turns, theta, 1.0 / (2 * np.pi), ROUND, ALU.mult, ALU.add))
            do(V.tensor_scalar(turns, turns, ROUND, None, ALU.subtract))
            do(V.scalar_tensor_tensor(x1, turns, -c1, theta, ALU.mult, ALU.add))
            do(V.scalar_tensor_tensor(x2, turns, -c2, x1, ALU.mult, ALU.add))
            do(V.scalar_tensor_tensor(x1, turns, -c3, x2, ALU.mult, ALU.add))
            do(V.tensor_scalar(ang, x1, 3.1415925, -3.1415925, ALU.min, ALU.max))
            do(V.scalar_tensor_tensor(x2, ang, -1.0, ang, ALU.mult, ALU.max))
            V.tensor_scalar(ang2, x2, -1.0, np.pi / 2, ALU.mult, ALU.add).then_inc(s_prm, 1)
            dve.wait_ge(s_trig, 3)
            a_re, a_im = pw[:, RE, 1, :], pw[:, IM, 1, :]
            mul(a_re, mag, cos)
            mul(a_im, mag, sin)
            mul(x1, are, are)
            mul(x2, aim, aim)
            do(V.tensor_tensor(den, x1, x2, ALU.add))
            do(V.reciprocal(rden, den))
            do(V.tensor_scalar(am1, a_re, 1.0, None, ALU.subtract))
            mul(x1, am1, are)
            mul(x2, a_im, aim)
            do(V.tensor_tensor(x1, x1, x2, ALU.add))
            mul(zr, x1, rden)
            mul(x1, a_im, are)
            mul(x2, am1, aim)
            do(V.tensor_tensor(x1, x1, x2, ALU.subtract))
            mul(zi, x1, rden)
            n = PAIRS * CH

            def by_pair(x):
                return x.rearrange("p (g q) -> p g q", g=PAIRS)

            z_re, z_im = (z[:, :, None].to_broadcast([P, PAIRS, CH]) for z in (zr, zi))
            cmul(bbar[:, RE, :, :], bbar[:, IM, :, :], braw[:, RE, :, :], braw[:, IM, :, :], z_re, z_im,
                 by_pair(t1[:, 0:n]), by_pair(t2[:, 0:n]))
            do(V.memset(pw[:, RE, 0, :], 1.0))
            do(V.memset(pw[:, IM, 0, :], 0.0))
            m = 1
            while m < L:
                bc = [pw[:, k, m:m + 1, :].to_broadcast([P, m, PAIRS]) for k in (RE, IM)]
                tt = [t[:, 0:m * PAIRS].rearrange("p (t g) -> p t g", g=PAIRS) for t in (t1, t2)]
                cmul(pw[:, RE, m + 1:2 * m + 1, :], pw[:, IM, m + 1:2 * m + 1, :],
                     pw[:, RE, 1:m + 1, :], pw[:, IM, 1:m + 1, :], bc[0], bc[1], tt[0], tt[1])
                m *= 2
            do(V.tensor_copy(lvl[:, :, 0, :], pw[:, :, L, :]))
            for k in range(1, LEVELS):
                cmul(lvl[:, RE, k, :], lvl[:, IM, k, :], lvl[:, RE, k - 1, :], lvl[:, IM, k - 1, :],
                     lvl[:, RE, k - 1, :], lvl[:, IM, k - 1, :], x1, x2)
            for s in range(L):
                do(V.tensor_copy(pw_rev[:, :, s, :], pw[:, :, L - 1 - s, :]))
            full = [P, PAIRS, L, CH]
            n = PAIRS * L * CH
            tt = [t[:, 0:n].rearrange("p (g s q) -> p g s q", g=PAIRS, s=L) for t in (t1, t2)]
            rev = [pw_rev[:, k, :, :].rearrange("p s g -> p g s")[:, :, :, None].to_broadcast(full) for k in (RE, IM)]
            bb = [bbar[:, k, :, None, :].to_broadcast(full) for k in (RE, IM)]
            cmul(wb[:, RE, :, :, :], wb[:, IM, :, :, :], rev[0], rev[1], bb[0], bb[1], tt[0], tt[1])
            dve.sem_inc(s_wb, 1)
            dve.wait_ge(s_ct, 1)
            do(V.tensor_copy(ct[:, :, :, :].rearrange("p k g q -> p (k g q)"), ps[7][:, 0:2 * P]))
            full = [P, PAIRS, L + 1, CH]
            tt = [t[:, :].rearrange("p (g s q) -> p g s q", g=PAIRS, s=L + 1) for t in (t1, t2)]
            fw = [pw[:, k, :, :].rearrange("p s g -> p g s")[:, :, :, None].to_broadcast(full) for k in (RE, IM)]
            cc = [ct[:, k, :, None, :].to_broadcast(full) for k in (RE, IM)]
            mul(tt[0], fw[0], cc[0])
            mul(tt[1], fw[1], cc[1])
            flat = "p g s q -> p (g s q)"
            do(V.tensor_tensor(ca[:, RE, :, :, :].rearrange(flat), t1[:, :], t2[:, :], ALU.subtract))
            mul(tt[0], fw[0], cc[1])
            mul(tt[1], fw[1], cc[0])
            V.scalar_tensor_tensor(ca[:, IM, :, :, :].rearrange(flat), t1[:, :], -1.0, t2[:, :], ALU.mult,
                                   ALU.subtract).then_inc(s_bc, 1)
            do(V.memset(kern[:, :, 0:PAD], 0.0))
            for k in range(PAIRS):
                dve.wait_ge(s_kern, k + 1)
                for r in range(2):
                    V.tensor_copy(kern[:, 2 * k + r, PAD:], ps[2 + 2 * r + k % 2][0:CH, 0:L * CH]).then_inc(s_kread, 1)
            tt16 = t1[0:CH, 0:GROUPS * CH].rearrange("p (g q) -> p g q", g=GROUPS)
            mul(tt16, skip[:, :, :], K.ident[0:CH, None, 0:CH].to_broadcast([CH, GROUPS, CH]))
            dve.wait_ge(s_kread, 2 * PAIRS)
            V.tensor_tensor(kern[:, :, PAD:PAD + CH], kern[:, :, PAD:PAD + CH], tt16, ALU.add).then_inc(s_kdone, 1)
            for g in range(PAIRS):
                dve.wait_ge(s_drive, g + 1)
                V.tensor_copy(scan[0][:, :, g, :], ps[2 + g % 2][:, 0:2 * NBS].rearrange("p (k c) -> p k c", k=2))\
                    .then_inc(s_dread, 1)
            dve.wait_ge(s_h0, 1)
            do(V.tensor_copy(before[:, :, :, NB:], ps[6][:, 0:2 * NS].rearrange("p (k g b) -> p k g b", k=2, b=DEC_BATCH)))
            do(V.memset(before[:, :, :, 0:1], 0.0))
            dve.wait_ge(s_dread, PAIRS)
            full = [P, PAIRS, DEC_BATCH]
            tt = [t[:, 0:NS].rearrange("p (g b) -> p g b", g=PAIRS) for t in (t1, t2)]
            lv = [lvl[:, k, 0, :, None].to_broadcast(full) for k in (RE, IM)]
            es = [end_s[:, k, :].rearrange("p (g b) -> p g b", g=PAIRS) for k in (RE, IM)]
            h0 = [before[:, k, :, NB:] for k in (RE, IM)]
            cmul(es[0], es[1], h0[0], h0[1], lv[0], lv[1], tt[0], tt[1])
            for k in (RE, IM):
                do(V.tensor_tensor(es[k], es[k], scan[0][:, k, :, NB:], ALU.add))
            for k in range(LEVELS):
                x, y = scan[k % 2], scan[(k + 1) % 2]
                d = 1 << k
                w = NB - d
                full = [P, PAIRS, w]
                tt = [t[:, 0:PAIRS * w].rearrange("p (g c) -> p g c", g=PAIRS) for t in (t1, t2)]
                lv = [lvl[:, r, k, :, None].to_broadcast(full) for r in (RE, IM)]
                cmul(y[:, RE, :, d:NB], y[:, IM, :, d:NB], x[:, RE, :, 0:w], x[:, IM, :, 0:w], lv[0], lv[1], tt[0], tt[1])
                for r in (RE, IM):
                    do(V.tensor_tensor(y[:, r, :, d:NB], y[:, r, :, d:NB], x[:, r, :, d:NB], ALU.add))
                    do(V.tensor_copy(y[:, r, :, 0:d], x[:, r, :, 0:d]))
            done = scan[LEVELS % 2]
            for r in (RE, IM):
                do(V.tensor_copy(before[:, r, :, 1:NB], done[:, r, :, 0:NB - 1]))
            V.tensor_copy(end_p[:, :, :], done[:, :, :, NB - 1]).then_inc(s_before, 1)
            for k in range(4):
                for g in range(4 * k, 4 * k + 4):
                    dve.wait_ge(s_y, g + 1)
                    V.tensor_copy(u[:, g, :].rearrange("p (c b) -> p b c", b=2),
                                  ps[g % 4][:, 0:2 * NBS].rearrange("p (b c) -> p b c", b=2)).then_inc(s_yread, 1)
                dve.wait_ge(s_yread, 4 * (k + 1))
                dve.wait_ge(s_sq, k + 1)
                do(V.tensor_scalar(t1[:, 0:CHUNK], t1[:, 0:CHUNK], 0.044715, 1.0, ALU.mult, ALU.add))
                V.tensor_tensor(t2[:, 0:CHUNK], t1[:, 0:CHUNK], ys(k), ALU.mult).then_inc(s_poly, 1)
                dve.wait_ge(s_tanh, k + 1)
                V.scalar_tensor_tensor(ys(k), t1[:, 0:CHUNK], 1.0, ys(k), ALU.add, ALU.mult).then_inc(s_gelu, 1)
            dve.wait_ge(s_ends, 1)
            for k in range(2):
                V.tensor_copy(out_p[:, k, :], ps[4][0:PAIRS, k * P:(k + 1) * P]).then_inc(s_eread, 1)
                V.tensor_copy(out_s[:, k, :], ps[5][0:NS, k * P:(k + 1) * P]).then_inc(s_eread, 1)
            dve.wait_ge(s_yt, 16 * 8 * GROUPS)
            dve.wait_ge(s_toep, 16 * 8)
            for n in range(16):
                m, s = n // 8, n % 8
                w = t2[:, (n % 2) * J:(n % 2 + 1) * J]
                do(V.scalar_tensor_tensor(w, K.su[:, m, s, :], 0.25, K.sg[:, m, s, :], ALU.mult, ALU.mult))
                dve.wait_ge(s_gtanh, n + 1)
                V.scalar_tensor_tensor(final[:, m, :, s], gt[:, n % 2, :], 1.0, w, ALU.add, ALU.mult).then_inc(s_final, 1)

        @block.tensor
        def _(pe):
            T = nc.tensor
            pe.wait_ge(s_load, 16 * NLOAD)
            for k in range(2):
                last = T.transpose(ps[7][:, k * P:(k + 1) * P], craw[:, k, :], K.ident[:, :])
            last.then_inc(s_ct, 1)
            for k in range(2):
                last = T.transpose(ps[6][:, k * NS:(k + 1) * NS], hraw[:, k, :], K.ident[0:NS, 0:NS])
            last.then_inc(s_h0, 1)
            pe.wait_ge(s_wb, 1)
            for g in range(PAIRS):
                if g >= 2:
                    pe.wait_ge(s_mats, g - 1)
                for b in range(2):
                    for r in (RE, IM):
                        at = (2 * b + r) * P
                        last = T.transpose(ps[g % 2][:, at:at + P],
                                           wb[:, r, g, 8 * b:8 * b + 8, :].rearrange("p s q -> p (s q)"), K.ident[:, :])
                last.then_inc(s_wbt, 1)
            pe.wait_ge(s_bc, 1)
            for k in range(PAIRS):
                if k >= 2:
                    pe.wait_ge(s_kread, 2 * (k - 1))
                for r in range(2):
                    rows = slice(r * STATE, (r + 1) * STATE)
                    for c in (RE, IM):
                        last = T.matmul(ps[2 + 2 * r + k % 2][0:CH, 0:L * CH], bbar[rows, c, k, :],
                                        ca[rows, c, k, 0:L, :].rearrange("p t q -> p (t q)"),
                                        start=c == RE, stop=c == IM)
                last.then_inc(s_kern, 1)
            pe.wait_ge(s_kread, 2 * PAIRS)
            pe.wait_ge(s_uin, 16 * 8 * GROUPS)
            pe.wait_ge(s_mats, PAIRS)
            for g in range(PAIRS):
                if g >= 2:
                    pe.wait_ge(s_dread, g - 1)
                for r in range(2):
                    for c in (RE, IM):
                        for b in range(2):
                            last = T.matmul(ps[2 + g % 2][r * STATE:(r + 1) * STATE, c * NBS:(c + 1) * NBS],
                                            wbt[:, g, b, c, r * STATE:(r + 1) * STATE],
                                            u[:, 2 * g + r, :].rearrange("p (c b) -> p b c", b=2)[:, b, :],
                                            start=b == 0, stop=b == 1)
                last.then_inc(s_drive, 1)
            pe.wait_ge(s_toep, 16 * 8)
            pe.wait_ge(s_before, 1)
            for g in range(GROUPS):
                if g >= 4:
                    pe.wait_ge(s_yread, g - 3)
                rows = slice(g % 2 * STATE, (g % 2 + 1) * STATE)
                halves = u[:, g, :].rearrange("p (c b) -> p b c", b=2)
                for b in range(2):
                    out = ps[g % 4][:, b * NBS:(b + 1) * NBS]
                    for k in range(b + 1):
                        T.matmul(out, toep[:, g, (b - k) * P:(b - k + 1) * P], halves[:, k, :], start=k == 0, stop=False)
                    for c in (RE, IM):
                        last = T.matmul(out, ca[rows, c, g // 2, 1 + 8 * b:9 + 8 * b, :].rearrange("p t q -> p (t q)"),
                                        before[rows, c, g // 2, :], start=False, stop=c == IM)
                last.then_inc(s_y, 1)
            for k in range(2):
                T.transpose(ps[4][0:PAIRS, k * P:(k + 1) * P], end_p[:, k, :], K.ident[:, :])
                last = T.transpose(ps[5][0:NS, k * P:(k + 1) * P], end_s[:, k, :], K.ident[:, :])
            last.then_inc(s_ends, 1)
            pe.wait_ge(s_yt, 16 * 8 * GROUPS)
            for n in range(16):
                m, s = n // 8, n % 8
                if n >= 2:
                    pe.wait_ge(s_gtanh, n - 1)
                for c in range(2):
                    last = T.matmul(ps[n % 2][:, 0:J], wglu[:, c, m * P:(m + 1) * P], K.su[:, c, s, :],
                                    start=c == 0, stop=c == 1)
                last.then_inc(s_glu, 1)


def prompt_attention(nc, K, D):
    HEADS_PAIR = 2
    NPAIR = FOX_HEADS // HEADS_PAIR
    MT = PROMPT_TILES // HEADS_PAIR
    kinds = []
    for t in range(PROMPT_TILES):
        kinds.append(("fox", t))
        if t % 2:
            kinds.append(("mem", t // 2))

    class Unit:
        pass

    units, nu, ng = [], 0, 0
    for h in range(HEADS_PAIR):
        for kind, t in kinds:
            u = Unit()
            u.h, u.kind, u.t, u.n = h, kind, t, nu
            keys = (t + 1) * P if kind == "fox" else N_MEM
            u.groups = [(ng + j, k0, min(512, keys - k0)) for j, k0 in enumerate(range(0, keys, 512))]
            ng += len(u.groups)
            nu += 1
            units.append(u)
    UPH, UNITS, GROUPS_PAIR = nu // HEADS_PAIR, nu, ng
    assert GROUPS_PAIR % 8 == 0 and UNITS % 4 == 0

    with ExitStack() as stack:
        a = Place(nc, stack, "attn")
        qa = [a.sb(f"qa{h}", [P, SEQ], F32R) for h in range(2)]
        qb = [a.sb(f"qb{h}", [HD + 2, SEQ], F32R) for h in range(2)]
        ka = [a.sb(f"ka{h}", [P, SEQ], F32R) for h in range(2)]
        kb = [a.sb(f"kb{h}", [HD + 2, SEQ], F32R) for h in range(2)]
        v = [a.sb(f"v{h}", [P, PROMPT_TILES, HD + 1]) for h in range(2)]
        mqa = [a.sb(f"mqa{h}", [P, MT * P], F32R) for h in range(2)]
        mka = [a.sb(f"mka{h}", [P, N_MEM], F32R) for h in range(2)]
        mkb = [a.sb(f"mkb{h}", [HD, N_MEM], F32R) for h in range(2)]
        mv = [a.sb(f"mv{h}", [P, N_MEM // P, HD + 1]) for h in range(2)]
        probs = a.sb("probs", [P, 8, 512])
        probs_t = a.sb("probs_t", [P, 4, 512])
        top, negmax, rden = a.sb("top", [P, 4]), a.sb("negmax", [P, 4]), a.sb("rden", [P, 2])
        out = a.sb("out", [P, 2, UPH, HD])
        s_ps = [a.ps(f"s{i}", [P, 512]) for i in range(4)]
        t_ps = [a.ps(f"t{i}", [P, 512]) for i in range(2)]
        o_ps = [a.ps(f"o{i}", [P, 512]) for i in range(2)]
        s_ones = a.sem("ones")
        s_load = [a.sem(f"load{h}") for h in range(2)]
        s_score, s_top, s_negmax, s_exp = a.sem("scores"), a.sem("top"), a.sem("negmax"), a.sem("exp")
        s_turn, s_read = a.sem("turned"), [a.sem("turned_read_dve"), a.sem("turned_read_act")]
        s_pv, s_rden, s_o = a.sem("pv"), a.sem("rden"), a.sem("out")
        s_store = [a.sem(f"stored{h}") for h in range(2)]
        LOADS = 12
        block = stack.enter_context(nc.Block())

        def slots():
            return [(u, units[u.n + 1] if u.n + 1 < UNITS else None) for u in units]

        @block.sync
        def _(sp):
            with sp.Fori(0, NPAIR) as i:
                for h in range(2):
                    head = i * 2 + h

                    def load(dst, src):
                        sp.dma_start(dst, src).then_inc(s_load[h], 16)

                    def row(x, lo, hi, c=None):
                        return x[bass.ds(head, 1), lo:hi, 0:SEQ].rearrange("o p t -> (o p) t")

                    sp.wait_ge(s_pv, (head + 1) * UPH)
                    load(fl(qa[h][:, :]), row(D.q, 0, P))
                    load(fl(ka[h][0:HD, :]), row(D.k, 0, HD))
                    load(fl(ka[h][HD:P, :]), row(D.k, 0, HD))
                    load(fl(qb[h][0:HD, :]), row(D.q, 0, HD))
                    load(fl(kb[h][0:HD, :]), row(D.k, HD, P))
                    load(fl(kb[h][HD:HD + 2, :]), row(D.decay, 0, 2))
                    load(v[h][:, :, 0:HD], D.o_v[:, bass.ds(head * HD, HD)].rearrange("(k p) d -> p k d", p=P))
                    load(fl(mqa[h][:, :]), D.mq[bass.ds(i, 1), :, h * MT * P:(h + 1) * MT * P].rearrange("o p t -> (o p) t"))
                    load(fl(mka[h][0:HD, :]), D.mk[bass.ds(i, 1), 0:HD, :].rearrange("o p t -> (o p) t"))
                    load(fl(mka[h][HD:P, :]), D.mk[bass.ds(i, 1), 0:HD, :].rearrange("o p t -> (o p) t"))
                    load(fl(mkb[h][:, :]), D.mk[bass.ds(i, 1), HD:P, :].rearrange("o p t -> (o p) t"))
                    load(mv[h][:, :, 0:HD], D.o_mv[:, bass.ds(i * HD, HD)].rearrange("(k p) d -> p k d", p=P))

        @block.tensor
        def _(pe):
            pe.sem_inc(s_pv, 2 * UPH)
            pe.wait_ge(s_ones, 6)
            with pe.Fori(0, NPAIR) as i:
                g0, u0 = i * GROUPS_PAIR, i * UNITS

                def scores(u, j):
                    g, k0, n = u.groups[j]
                    if j == 0 and u.n % UPH == 0:
                        pe.wait_ge(s_load[u.h], (i + 1) * (16 * LOADS))
                    pe.wait_ge(s_exp, g0 + (g + 1))
                    bank = s_ps[g % 4]
                    q = slice(u.t * P, (u.t + 1) * P)
                    if u.kind == "fox":
                        nc.tensor.matmul(bank[:, 0:n], qa[u.h][:, q], ka[u.h][:, k0:k0 + n], start=True, stop=False)
                        if j == len(u.groups) - 1:
                            nc.tensor.matmul(bank[:, n - P:n], K.identb[:, :], K.causal[:, :], start=False, stop=False)
                        last = nc.tensor.matmul(bank[:, 0:n], qb[u.h][:, q], kb[u.h][:, k0:k0 + n],
                                                start=False, stop=True)
                    else:
                        nc.tensor.matmul(bank[:, 0:n], mqa[u.h][:, q], mka[u.h][:, 0:n], start=True, stop=False)
                        last = nc.tensor.matmul(bank[:, 0:n], mqa[u.h][0:HD, q], mkb[u.h][:, 0:n],
                                                start=False, stop=True)
                    last.then_inc(s_score, 1)

                def turn(u, j):
                    g, k0, n = u.groups[j]
                    pe.wait_ge(s_exp, g0 + (g + 5))
                    pe.wait_ge(s_read[g % 2], i * (GROUPS_PAIR // 2) + (g // 2 + 1))
                    for b in range(n // P):
                        last = nc.tensor.transpose(t_ps[g % 2][:, b * P:(b + 1) * P],
                                                   probs[:, g % 8, b * P:(b + 1) * P], K.ident[:, :])
                    last.then_inc(s_turn, 1)

                def values(u, j):
                    g, k0, n = u.groups[j]
                    pe.wait_ge(s_read[g % 2], i * (GROUPS_PAIR // 2) + (g // 2 + 2))
                    if j == 0:
                        pe.wait_ge(s_o, u0 + (u.n + 1))
                    vals = v[u.h] if u.kind == "fox" else mv[u.h]
                    for b in range(n // P):
                        done = j == len(u.groups) - 1 and b == n // P - 1
                        last = nc.tensor.matmul(o_ps[u.n % 2][:, 0:HD + 1], probs_t[:, g % 4, b * P:(b + 1) * P],
                                                vals[:, k0 // P + b, :], start=(j == 0 and b == 0), stop=done)
                    if done:
                        last.then_inc(s_pv, 1)

                scores(units[0], 0)
                for u, nxt in slots():
                    here, there = len(u.groups), len(nxt.groups) if nxt else 0
                    for j in range(max(here, there)):
                        if j < here:
                            turn(u, j)
                        if j < there:
                            scores(nxt, j)
                        if 0 < j < here:
                            values(u, j - 1)
                    values(u, here - 1)

        @block.scalar
        def _(act):
            act.sem_inc(s_exp, 4)
            act.sem_inc(s_read[1], 1)
            for h in range(2):
                act.sem_inc(s_store[h], 16 * 3)
            assert [u.kind for u in units[:UPH]] == ["fox", "fox", "mem"] * (UPH // 3)
            with act.Fori(0, NPAIR) as i:
                g0, u0 = i * GROUPS_PAIR, i * UNITS

                def exps(u):
                    act.wait_ge(s_negmax, u0 + (u.n + 1))
                    for g, k0, n in u.groups:
                        nc.scalar.activation(probs[:, g % 8, 0:n], s_ps[g % 4][:, 0:n], ACT.Exp,
                                             bias=negmax[:, u.n % 4:u.n % 4 + 1]).then_inc(s_exp, 1)

                def store(h):
                    head = i * 2 + h
                    by_three = out[:, h, :, :].rearrange("p (t o) d -> p t o d", o=3)
                    act.wait_ge(s_o, u0 + ((h + 1) * UPH + 2))
                    fox = D.fox[0:SEQ, bass.ds(head * HD, HD)].rearrange("(t o p) d -> p t o d", p=P, o=2)
                    for odd in range(2):
                        act.dma_start(fox[:, :, odd, :], by_three[:, :, odd, :]).then_inc(s_store[h], 16)
                    act.dma_start(D.mem[h * MT * P:(h + 1) * MT * P, bass.ds(i * HD, HD)]
                                  .rearrange("(t p) d -> p t d", p=P), by_three[:, :, 2, :]).then_inc(s_store[h], 16)

                exps(units[0])
                for u, nxt in slots():
                    if u.n == UPH + 2:
                        store(0)
                    for g, k0, n in u.groups:
                        if g % 2 == 1:
                            act.wait_ge(s_turn, g0 + (g + 1))
                            nc.scalar.activation(probs_t[:, g % 4, 0:n], t_ps[1][:, 0:n], ACT.Copy).then_inc(s_read[1], 1)
                    if nxt:
                        exps(nxt)
                store(1)
            for h in range(2):
                act.wait_ge(s_store[h], 16 * 3 * (1 + NPAIR))

        @block.vector
        def _(dve):
            for h in range(2):
                nc.vector.memset(fl(qb[h][HD:HD + 2, :]), 1.0).then_inc(s_ones, 1)
                nc.vector.memset(v[h][:, :, HD:HD + 1], 1.0).then_inc(s_ones, 1)
                nc.vector.memset(mv[h][:, :, HD:HD + 1], 1.0).then_inc(s_ones, 1)
            dve.sem_inc(s_o, 2)
            dve.sem_inc(s_read[0], 1)
            with dve.Fori(0, NPAIR) as i:
                g0, u0 = i * GROUPS_PAIR, i * UNITS
                multi = [u.n for u in units if len(u.groups) > 1]

                def maximum(u, j):
                    g, k0, n = u.groups[j]
                    dve.wait_ge(s_score, g0 + (g + 1))
                    col = negmax[:, u.n % 4:u.n % 4 + 1]
                    if len(u.groups) == 1:
                        nc.vector.tensor_reduce(col, s_ps[g % 4][:, 0:n], AX.X, ALU.max, negate=True).then_inc(s_negmax, 1)
                        return
                    nc.vector.tensor_reduce(top[:, j:j + 1], s_ps[g % 4][:, 0:n], AX.X, ALU.max).then_inc(s_top, 1)
                    if j == len(u.groups) - 1:
                        tops = sum(len(units[m].groups) for m in multi if m <= u.n)
                        dve.wait_ge(s_top, i * sum(len(units[m].groups) for m in multi) + tops)
                        nc.vector.tensor_reduce(col, top[:, 0:j + 1], AX.X, ALU.max, negate=True).then_inc(s_negmax, 1)

                def normalise(u):
                    dve.wait_ge(s_pv, u0 + (u.n + 1 + 2 * UPH))
                    nc.vector.reciprocal(rden[:, u.n % 2:u.n % 2 + 1], o_ps[u.n % 2][:, HD:HD + 1]).then_inc(s_rden, 1)
                    dve.wait_ge(s_rden, u0 + (u.n + 1))
                    if u.n % UPH == 0:
                        dve.wait_ge(s_store[u.h], (i + 1) * (16 * 3))
                    nc.vector.tensor_scalar(out[:, u.h, u.n % UPH, :], o_ps[u.n % 2][:, 0:HD],
                                            rden[:, u.n % 2:u.n % 2 + 1], None, ALU.mult).then_inc(s_o, 1)

                maximum(units[0], 0)
                for u, nxt in slots():
                    here, there = len(u.groups), len(nxt.groups) if nxt else 0
                    for j in range(max(here, there)):
                        if j < here and u.groups[j][0] % 2 == 0:
                            g, k0, n = u.groups[j]
                            dve.wait_ge(s_turn, g0 + (g + 1))
                            nc.vector.tensor_copy(probs_t[:, g % 4, 0:n], t_ps[0][:, 0:n]).then_inc(s_read[0], 1)
                        if j < there:
                            maximum(nxt, j)
                        if j == 0 and u.n > 0:
                            normalise(units[u.n - 1])
                normalise(units[-1])


def sample_attention(nc, K, D):
    B, T = DEC_BATCH, DEC_SEQ
    KT = PAST // P
    HP, MP = FOX_HEADS // 2, MEM_HEADS // 2
    MROWS = MEM_HEADS * T
    KEYS = PAST + T
    with ExitStack() as stack:
        a = Place(nc, stack, "smp")
        qn, kn, mqn = a.sb("qn", [P, FOX]), a.sb("kn", [P, FOX]), a.sb("mqn", [P, MEM])
        qt, knt, mqt = a.sb("qt", [P, HP, P]), a.sb("knt", [P, HP, P]), a.sb("mqt", [P, MP, P])
        qblk = [a.sb(f"qblk{u}", [P, 32 + HP * (P + 32)]) for u in range(2)]
        mqblk = [a.sb(f"mqblk{u}", [P, 32 + MP * (MROWS + 32)]) for u in range(2)]
        kc, vc = a.sb("kc", [P, 2, KT, FOX]), a.sb("vc", [P, 2, KT, FOX])
        mk, mv = a.sb("mk", [P, 2, N_MEM // P, MEM]), a.sb("mv", [P, 2, N_MEM // P, MEM])
        vn, dec = a.sb("vn", [P, 2, FOX]), a.sb("dec", [P, 2, KEYS])
        kt, mkt = a.sb("kt", [P, 2, HP, PAST]), a.sb("mkt", [P, 2, MP, N_MEM])
        sel, rep = a.sb("sel", [P, FOX_HEADS, T]), a.sb("rep", [P, FOX_HEADS, T], BF16)
        top, negmax, den, rden = (a.sb(k, [P, 2]) for k in ("top", "negmax", "den", "rden"))
        mneg, mden, mrden = (a.sb(k, [MROWS, 2]) for k in ("mneg", "mden", "mrden"))
        probs, mprobs = a.sb("probs", [P, KEYS]), a.sb("mprobs", [MROWS, N_MEM])
        pt, ptn, mpt = a.sb("pt", [P, KT, P]), a.sb("ptn", [P, P]), a.sb("mpt", [P, 2, MROWS])
        out, mout = a.sb("out", [P, 2, FOX]), a.sb("mout", [MROWS, 2, MEM])
        t_ps = [a.ps(f"t{i}", [P, 512]) for i in range(2)]
        p_ps, s_ps, n_ps, m_ps, o_ps, mo_ps = (a.ps(k, [P, 512]) for k in ("p", "s", "n", "m", "o", "mo"))
        wide, mwide = D.wide, D.mwide
        (s_q, s_turn0, s_qt, s_zero, s_sel, s_blk, s_turn, s_score, s_top, s_neg, s_exp, s_mexp, s_den, s_rden, s_pturn,
         s_pread, s_pread2, s_pv, s_out, s_mout, s_gather) = (a.sem(k) for k in (
             "q turn0 qt zero sel blk turn score top neg exp mexp den rden pturn pread pread2 pv out mout gather").split())
        s_load = [a.sem(f"load{u}") for u in range(2)]
        s_store = [a.sem(f"store{u}") for u in range(2)]
        s_read = [a.sem("read_dve"), a.sem("read_act")]
        LOADS = 6
        block = stack.enter_context(nc.Block())

        def streams(eng, body):
            for b in range(2):
                body(b, b, 0)
            with eng.Fori(1, B // 2 - 1) as i:
                for u in range(2):
                    body(i * 2 + u, u, i)
            for b in range(B - 2, B):
                body(b, b % 2, b // 2)

        def fills(b, u, i):
            return [(f, (5 * u + f) % 2, i * 5 + (5 * u + f) // 2) for f in range(5)]

        @block.sync
        def _(sp):
            sp.dma_start(qn[:, :], D.q_s).then_inc(s_q, 16)
            sp.dma_start(kn[:, :], D.o_k_s).then_inc(s_q, 16)
            sp.dma_start(mqn[:, :], D.mq_s).then_inc(s_q, 16)
            for u in range(2):
                sp.sem_inc(s_store[u], 32)
            sp.wait_ge(s_zero, 1)

            def load(b, u):
                def one(dst, src):
                    sp.dma_start(dst, src).then_inc(s_load[u], 16)
                if isinstance(b, int):
                    bb = slice(b, b + 1)
                else:
                    bb = bass.ds(b, 1)
                one(kc[:, u, :, :], D.cache_k[bb, :, :].rearrange("o (k p) c -> p (o k) c", p=P))
                one(mk[:, u, :, :], D.cache_mk[bb, :, :].rearrange("o (k p) c -> p (o k) c", p=P))
                one(dec[0:FOX_HEADS, u, :], D.decay_s[bb, :, :].rearrange("o h c -> (o h) c"))
                one(vc[:, u, :, :], D.cache_v[bb, :, :].rearrange("o (k p) c -> p (o k) c", p=P))
                one(mv[:, u, :, :], D.cache_mv[bb, :, :].rearrange("o (k p) c -> p (o k) c", p=P))
                one(vn[0:T, u, :], D.o_v_s.rearrange("(b t) c -> b t c", t=T)[bb, :, :].rearrange("o t c -> (o t) c"))

            load(0, 0)
            load(1, 1)

            def body(b, u, i):
                bb = slice(b, b + 1) if isinstance(b, int) else bass.ds(b, 1)
                sp.wait_ge(s_out, b + 2)
                sp.dma_start(wide[bb, :, :].rearrange("o r c -> (o r) c"), out[:, u, :]).then_inc(s_store[u], 16)
                sp.wait_ge(s_mout, b + 2)
                sp.dma_start(mwide[bb, :, :].rearrange("o r c -> (o r) c"), mout[:, u, :]).then_inc(s_store[u], 16)
                if not isinstance(b, int) or b + 2 < B:
                    load(b + 2, u)

            streams(sp, body)
            for u in range(2):
                sp.wait_ge(s_store[u], 32 * (1 + B // 2))
            for h in range(FOX_HEADS):
                sp.dma_start(D.fox[SEQ:, h * HD:(h + 1) * HD].rearrange("(b t) d -> b t d", t=T),
                             wide[:, h * T:(h + 1) * T, h * HD:(h + 1) * HD]).then_inc(s_gather, 16)
            for h in range(MEM_HEADS):
                sp.dma_start(D.mem[SEQ:, h * HD:(h + 1) * HD].rearrange("(b t) d -> b t d", t=T),
                             mwide[:, h * T:(h + 1) * T, h * HD:(h + 1) * HD]).then_inc(s_gather, 16)
            sp.wait_ge(s_gather, 16 * (FOX_HEADS + MEM_HEADS))

        @block.gpsimd
        def _(pool):
            nc.gpsimd.memset(sel[:, :, :], 0.0).then_inc(s_sel, 1)
            nc.gpsimd.memset(rep[:, :, :], 0.0).then_inc(s_sel, 1)
            pool.wait_ge(s_sel, 2)
            nc.gpsimd.affine_select(out=sel[:, :, :], in_=sel[:, :, :], compare_op=ALU.not_equal, fill=1.0, base=0,
                                    pattern=[[-1, FOX_HEADS], [0, T]], channel_multiplier=1).then_inc(s_sel, 1)
            nc.gpsimd.affine_select(out=rep[:, :, :], in_=rep[:, :, :], compare_op=ALU.not_equal, fill=1.0, base=0,
                                    pattern=[[0, FOX_HEADS], [-1, T]], channel_multiplier=1).then_inc(s_sel, 1)

        @block.tensor
        def _(pe):
            X = nc.tensor
            pe.wait_ge(s_q, 48)
            for dst, src, n in ((s_ps, qn, HP), (n_ps, kn, HP), (m_ps, mqn, MP)):
                for j in range(n):
                    last = X.transpose(dst[:, j * P:(j + 1) * P], src[:, j * P:(j + 1) * P], K.ident[:, :])
            last.then_inc(s_turn0, 1)
            pe.wait_ge(s_sel, 4)
            pe.wait_ge(s_zero, 1)
            pe.wait_ge(s_qt, 3)

            def turn_keys(b, u, i):
                pe.wait_ge(s_load[u], (i + 1) * (16 * LOADS))
                for f, bank, before in fills(b, u, i):
                    pe.wait_ge(s_read[bank], before + 1)
                    for j in range(4):
                        src = (kc[:, u, j, f * P:(f + 1) * P] if f < HP else mk[:, u, j % 2, (j // 2) * P:(j // 2 + 1) * P])
                        last = X.transpose(t_ps[bank][:, j * P:(j + 1) * P], src, K.ident[:, :])
                    last.then_inc(s_turn, 1)

            def body(b, u, i):
                for bank in range(2):
                    pe.wait_ge(s_read[bank], i * 5 + ((5 * (u + 1) + 1 - bank) // 2 + 1))
                pe.wait_ge(s_blk, b + 1)
                pe.wait_ge(s_exp, b * 2 + 1)
                pe.wait_ge(s_mexp, b + 1)
                q = [qblk[u][:, h * P:(h + 1) * P] for h in range(HP)]
                sel_h = sel[:, :, :].rearrange("p h t -> p (h t)")
                for h in range(HP):
                    X.matmul(s_ps[:, 0:PAST], q[h], kt[:, u, h, :], start=h == 0, stop=False)
                X.matmul(s_ps[:, 0:PAST], sel_h, dec[:, u, 0:PAST], start=False, stop=True).then_inc(s_score, 1)
                for h in range(HP):
                    X.matmul(n_ps[:, 0:T], q[h], knt[:, h, bass.ts(b, T)], start=h == 0, stop=False)
                X.matmul(n_ps[:, 0:T], rep[:, :, :].rearrange("p h t -> p (h t)"), K.causal[:, 0:T],
                         start=False, stop=False)
                X.matmul(n_ps[:, 0:T], sel_h, dec[:, u, PAST:KEYS], start=False, stop=True).then_inc(s_score, 1)
                for h in range(MP):
                    last = X.matmul(m_ps[0:MROWS, 0:N_MEM], mqblk[u][:, h * MROWS:(h + 1) * MROWS], mkt[:, u, h, :],
                                    start=h == 0, stop=h == MP - 1)
                last.then_inc(s_score, 1)
                if not isinstance(b, int) or b + 1 < B:
                    turn_keys(b + 1, 1 - u, i + u)
                pe.wait_ge(s_exp, b * 2 + 3)
                pe.wait_ge(s_pread2, b * 2 + 1)
                for j in range(KT):
                    last = X.transpose(p_ps[:, j * P:(j + 1) * P], probs[:, j * P:(j + 1) * P], K.ident[:, :])
                last.then_inc(s_pturn, 1)
                pe.wait_ge(s_mexp, b + 2)
                pe.wait_ge(s_pread, b + 2)
                X.transpose(p_ps[0:T, 0:P], probs[:, PAST:KEYS], K.ident[:, :])
                for j in range(2):
                    last = X.transpose(p_ps[:, P + j * MROWS:P + (j + 1) * MROWS], mprobs[:, j * P:(j + 1) * P],
                                       K.ident[0:MROWS, 0:MROWS])
                last.then_inc(s_pturn, 1)
                pe.wait_ge(s_mout, b + 1)
                pe.wait_ge(s_out, b + 1)
                for j in range(KT):
                    X.matmul(o_ps[:, :], pt[:, j, :], vc[:, u, j, :], start=j == 0, stop=False)
                pe.wait_ge(s_pread2, b * 2 + 3)
                X.matmul(o_ps[:, :], ptn[:, :], vn[:, u, :], start=False, stop=True).then_inc(s_pv, 1)
                for j in range(2):
                    last = X.matmul(mo_ps[0:MROWS, 0:MEM], mpt[:, j, :], mv[:, u, j, :], start=j == 0, stop=j == 1)
                last.then_inc(s_pv, 1)

            turn_keys(0, 0, 0)
            streams(pe, body)

        @block.scalar
        def _(act):
            act.sem_inc(s_read[1], 1)
            act.sem_inc(s_pread, 1)
            act.sem_inc(s_exp, 1)
            act.sem_inc(s_mexp, 1)
            act.sem_inc(s_out, 1)
            act.sem_inc(s_mout, 1)

            def keys(b, u, i):
                for f, bank, before in fills(b, u, i):
                    if bank == 1:
                        act.wait_ge(s_turn, b * 5 + (f + 1))
                        dst = kt[:, u, f, :] if f < HP else mkt[:, u, :, :].rearrange("p h k -> p (h k)")
                        nc.scalar.activation(dst, t_ps[1][:, :], ACT.Copy).then_inc(s_read[1], 1)

            def body(b, u, i):
                act.wait_ge(s_neg, b * 2 + 1)
                act.wait_ge(s_pturn, b * 2)
                nc.scalar.activation(probs[:, 0:PAST], s_ps[:, 0:PAST], ACT.Exp, bias=negmax[:, u:u + 1])
                nc.scalar.activation(probs[:, PAST:KEYS], n_ps[:, 0:T], ACT.Exp, bias=negmax[:, u:u + 1]).then_inc(s_exp, 2)
                act.wait_ge(s_neg, b * 2 + 2)
                nc.scalar.activation(mprobs[:, :], m_ps[0:MROWS, 0:N_MEM], ACT.Exp, bias=mneg[:, u:u + 1]).then_inc(s_mexp, 1)
                if not isinstance(b, int) or b + 1 < B:
                    keys(b + 1, 1 - u, i + u)
                act.wait_ge(s_pturn, b * 2 + 1)
                nc.scalar.activation(pt[:, :, :].rearrange("p k q -> p (k q)"), p_ps[:, :], ACT.Copy).then_inc(s_pread, 1)
                act.wait_ge(s_pv, b * 2 + 2)
                act.wait_ge(s_rden, b * 2 + 2)
                act.wait_ge(s_store[u], (i + 1) * 32)
                nc.scalar.activation(out[:, u, :], o_ps[:, :], ACT.Copy, scale=rden[:, u:u + 1]).then_inc(s_out, 1)
                nc.scalar.activation(mout[:, u, :], mo_ps[0:MROWS, 0:MEM], ACT.Copy,
                                     scale=mrden[:, u:u + 1]).then_inc(s_mout, 1)

            keys(0, 0, 0)
            streams(act, body)

        @block.vector
        def _(dve):
            V = nc.vector
            dve.sem_inc(s_read[0], 1)
            dve.sem_inc(s_pread2, 1)
            for t in (vn, dec, qblk[0], qblk[1], mqblk[0], mqblk[1], ptn):
                last = V.memset(t[tuple(slice(None) for _ in t.shape)], 0.0)
            last.then_inc(s_zero, 1)
            dve.wait_ge(s_turn0, 1)
            V.tensor_copy(qt[:, :, :].rearrange("p h t -> p (h t)"), s_ps[:, :]).then_inc(s_qt, 1)
            V.tensor_copy(knt[:, :, :].rearrange("p h t -> p (h t)"), n_ps[:, :]).then_inc(s_qt, 1)
            V.tensor_copy(mqt[:, :, :].rearrange("p h t -> p (h t)"), m_ps[:, 0:MP * P]).then_inc(s_qt, 1)
            dve.wait_ge(s_qt, 3)
            dve.wait_ge(s_zero, 1)

            def keys(b, u, i):
                for f, bank, before in fills(b, u, i):
                    if bank == 0:
                        dve.wait_ge(s_turn, b * 5 + (f + 1))
                        dst = kt[:, u, f, :] if f < HP else mkt[:, u, :, :].rearrange("p h k -> p (h k)")
                        V.tensor_copy(dst, t_ps[0][:, :]).then_inc(s_read[0], 1)

            def blocks(b, u):
                for r in range(2):
                    rows = slice(r * HD, (r + 1) * HD)
                    V.tensor_copy(qblk[u][rows, r * T:r * T + HP * (P + 32)].rearrange("p (h w) -> p h w", h=HP)[:, :, 0:T],
                                  qt[rows, :, bass.ts(b, T)])
                    last = V.tensor_copy(mqblk[u][rows, r * T:r * T + MP * (MROWS + 32)]
                                         .rearrange("p (h w) -> p h w", h=MP)[:, :, 0:T], mqt[rows, :, bass.ts(b, T)])
                last.then_inc(s_blk, 1)

            def body(b, u, i):
                dve.wait_ge(s_score, b * 3 + 1)
                V.tensor_reduce(top[:, 0:1], s_ps[:, 0:PAST], AX.X, ALU.max).then_inc(s_top, 1)
                dve.wait_ge(s_score, b * 3 + 2)
                V.tensor_reduce(top[:, 1:2], n_ps[:, 0:T], AX.X, ALU.max).then_inc(s_top, 1)
                dve.wait_ge(s_top, b * 2 + 2)
                V.tensor_reduce(negmax[:, u:u + 1], top[:, 0:2], AX.X, ALU.max, negate=True).then_inc(s_neg, 1)
                dve.wait_ge(s_score, b * 3 + 3)
                V.tensor_reduce(mneg[:, u:u + 1], m_ps[0:MROWS, 0:N_MEM], AX.X, ALU.max, negate=True).then_inc(s_neg, 1)
                if not isinstance(b, int) or b + 1 < B:
                    keys(b + 1, 1 - u, i + u)
                    blocks(b + 1, 1 - u)
                dve.wait_ge(s_exp, b * 2 + 3)
                V.tensor_reduce(den[:, u:u + 1], probs[:, :], AX.X, ALU.add).then_inc(s_den, 1)
                dve.wait_ge(s_mexp, b + 2)
                V.tensor_reduce(mden[:, u:u + 1], mprobs[:, :], AX.X, ALU.add).then_inc(s_den, 1)
                dve.wait_ge(s_den, b * 2 + 2)
                V.reciprocal(rden[:, u:u + 1], den[:, u:u + 1]).then_inc(s_rden, 1)
                V.reciprocal(mrden[:, u:u + 1], mden[:, u:u + 1]).then_inc(s_rden, 1)
                dve.wait_ge(s_pturn, b * 2 + 2)
                V.tensor_copy(ptn[0:T, :], p_ps[0:T, 0:P])
                V.tensor_copy(mpt[:, :, :].rearrange("p k q -> p (k q)"), p_ps[:, P:P + 2 * MROWS]).then_inc(s_pread2, 2)

            keys(0, 0, 0)
            blocks(0, 0)
            streams(dve, body)


def output_phase(nc, K, D, w_out):
    KF, KS = FOX // P, SSM // P
    with ExitStack() as stack:
        a = Place(nc, stack, "out")
        wh, wl = a.sb("wh", [P, KC, D_MODEL], F32R), a.sb("wl", [P, KC, D_MODEL], F32R)
        raw = a.sb("raw", [P, 2, D_MODEL])
        x, ssm = a.sb("x", [P, 2, D_MODEL]), a.sb("ssm", [P, 2, KS, P])
        fox, mem = a.sb("fox", [P, 2, 2, FOX]), a.sb("mem", [P, 2, 2, MEM])
        mix = a.sb("mix", [P, 2, FOX + MEM])
        mh, ml = a.sb("mh", [P, 2, KC, P], F32R), a.sb("ml", [P, 2, KC, P], F32R)
        y = a.sb("y", [P, 2, D_MODEL])
        xt_ps = [a.ps(f"xt{i}", [P, 4, P]) for i in range(2)]
        y_ps = [a.ps(f"y{i}", [P, 512]) for i in range(2)]
        s_w, s_in, s_store = ([a.sem(f"{k}{i}") for i in range(2)] for k in ("w", "in", "stored"))
        s_wh, s_wl, s_mix, s_xt, s_mh, s_ml = (a.sem(k) for k in ("wh", "wl", "mix", "turned", "mh", "ml"))
        s_g, s_y = ([a.sem(f"{k}{i}") for i in range(2)] for k in ("g", "y"))
        LOADS = 6
        block = stack.enter_context(nc.Block())
        PARTS = ((0, 4), (6, 8), (4, 6))

        def tiles(eng, body):
            for t in range(2):
                body(t, t)
            with eng.Fori(1, PROMPT_TILES // 2 - 1) as i:
                for u in range(2):
                    body(i * 2 + u, u)
            for t in range(PROMPT_TILES - 2, TILES):
                body(t, t % 2)

        def rows(array, sample, t):
            if isinstance(t, int) and t == PROMPT_TILES:
                return sample
            return array[bass.ts(t, P), :]

        @block.sync
        def _(sp):
            def load(t, u):
                def one(dst, src):
                    sp.dma_start(dst, src).then_inc(s_in[u], 16)
                one(fox[:, u, 0, :], D.fox[bass.ts(t, P), :])
                one(fox[:, u, 1, :], D.fox_gate[bass.ts(t, P), :])
                one(mem[:, u, 0, :], D.mem[bass.ts(t, P), :])
                one(mem[:, u, 1, :], D.mem_gate[bass.ts(t, P), :])
                one(ssm[:, u, :, :], D.ssm[:, bass.ts(t, P)].rearrange("(c p) t -> p c t", p=P))
                one(x[:, u, :], rows(D.x, D.xs, t))

            load(0, 0)
            load(1, 1)
            for c in range(KC):
                if c >= 2:
                    sp.wait_ge(s_wh, c - 1)
                    sp.wait_ge(s_wl, c - 1)
                sp.dma_start(raw[:, c % 2, :], w_out[c * P:(c + 1) * P, :]).then_inc(s_w[c % 2], 16)
            for u in range(2):
                sp.sem_inc(s_store[u], 16)

            def body(t, u):
                for h in range(2):
                    sp.wait_ge(s_y[h], t + 1)
                sp.dma_start(rows(D.y, D.ys, t), y[:, u, :]).then_inc(s_store[u], 16)
                if not isinstance(t, int) or t + 2 < TILES:
                    sp.wait_ge(s_ml, t * 3 + 3)
                    load(t + 2, u)

            tiles(sp, body)
            for u in range(2):
                sp.wait_ge(s_store[u], 16 * (1 + (TILES + 1 - u) // 2))

        @block.gpsimd
        def _(pool):
            def body(t, u):
                pool.wait_ge(s_in[u], (t - u) * (8 * LOADS) + 16 * LOADS)
                pool.wait_ge(s_xt, t * 2 + 2)
                nc.gpsimd.tensor_tensor(mix[:, u, 0:FOX], fox[:, u, 0, :], fox[:, u, 1, :], ALU.mult).then_inc(s_mix, 1)
                nc.gpsimd.tensor_tensor(mix[:, u, FOX:], mem[:, u, 0, :], mem[:, u, 1, :], ALU.mult).then_inc(s_mix, 1)

            tiles(pool, body)

        @block.tensor
        def _(pe):
            pe.sem_inc(s_xt, 4)

            def turn(t, u):
                pe.wait_ge(s_mix, t * 2 + 2)
                pe.wait_ge(s_ml, t * 3)
                for h, n in ((0, KF), (1, MEM // P)):
                    for c in range(n):
                        at = h * FOX + c * P
                        last = nc.tensor.transpose(xt_ps[h][:, c, :], mix[:, u, at:at + P], K.ident[:, :])
                    last.then_inc(s_xt, 1)

            def body(t, u):
                for h in range(2):
                    if h == 1 and not (isinstance(t, int) and t == TILES - 1):
                        turn(t + 1, 1 - u)
                    pe.wait_ge(s_ml, t * 3 + 3)
                    pe.wait_ge(s_y[h], t)
                    for c in range(KC):
                        for k, (ms, ws) in enumerate(((mh, wh), (ml, wh), (mh, wl))):
                            last = nc.tensor.matmul(y_ps[h][:, :], ms[:, u, c, :], ws[:, c, h * 512:(h + 1) * 512],
                                                    start=(c == 0 and k == 0), stop=(c == KC - 1 and k == 2))
                    last.then_inc(s_g[h], 1)

            turn(0, 0)
            pe.wait_ge(s_wl, KC)
            tiles(pe, body)

        @block.scalar
        def _(act):
            for c in range(KC):
                act.wait_ge(s_w[c % 2], 16 * (c // 2 + 1))
                nc.scalar.activation(wh[:, c, :], raw[:, c % 2, :], ACT.Copy).then_inc(s_wh, 1)

            def split(t, u):
                for k, (lo, hi) in enumerate(PARTS):
                    if k < 2:
                        act.wait_ge(s_xt, t * 2 + k + 5)
                        src = xt_ps[k][:, 0:hi - lo, :]
                    else:
                        act.wait_ge(s_in[u], (t - u) * (8 * LOADS) + 16 * LOADS)
                        src = ssm[:, u, :, :]
                    nc.scalar.activation(mh[:, u, lo:hi, :], src, ACT.Copy).then_inc(s_mh, 1)

            def body(t, u):
                if not (isinstance(t, int) and t == TILES - 1):
                    split(t + 1, 1 - u)

            split(0, 0)
            tiles(act, body)

        @block.vector
        def _(dve):
            for c in range(KC):
                dve.wait_ge(s_wh, c + 1)
                nc.vector.tensor_tensor(wl[:, c, :], raw[:, c % 2, :], fl(wh[:, c, :]), ALU.subtract).then_inc(s_wl, 1)

            def split(t, u):
                for k, (lo, hi) in enumerate(PARTS):
                    dve.wait_ge(s_mh, t * 3 + (k + 1))
                    src = xt_ps[k][:, 0:hi - lo, :] if k < 2 else ssm[:, u, :, :]
                    nc.vector.tensor_tensor(ml[:, u, lo:hi, :], src, fl(mh[:, u, lo:hi, :]), ALU.subtract).then_inc(s_ml, 1)

            def body(t, u):
                for h in range(2):
                    if h == 1 and not (isinstance(t, int) and t == TILES - 1):
                        split(t + 1, 1 - u)
                    dve.wait_ge(s_g[h], t + 1)
                    if h == 0:
                        dve.wait_ge(s_store[u], (t - u) * 8 + 16)
                    cols = slice(h * 512, (h + 1) * 512)
                    nc.vector.tensor_tensor(y[:, u, cols], y_ps[h][:, :], x[:, u, cols], ALU.add).then_inc(s_y[h], 1)

            split(0, 0)
            tiles(dve, body)


class Names:
    pass


def build(nc, I, O):
    K, D = Names(), Names()
    with ExitStack() as stack:
        a = Place(nc, stack, "all")

        def scratch(name, shape):
            return nc.dram_tensor("scratch_" + name, shape, F32).ap()

        D.q, D.k = scratch("q", (FOX_HEADS, P, TOKENS)), scratch("k", (FOX_HEADS, P, TOKENS))
        D.mq, D.mk = scratch("mq", (MEM_HEADS, P, TOKENS)), scratch("mk", (MEM_HEADS, P, N_MEM))
        D.q_s, D.mq_s = scratch("q_s", (P, FOX)), scratch("mq_s", (P, MEM))
        D.decay, D.decay_s = scratch("decay", (FOX_HEADS, 2, SEQ)), scratch("decay_s", (DEC_BATCH, FOX_HEADS, PAST + DEC_SEQ))
        D.fox_gate, D.mem_gate = scratch("fox_gate", (TOKENS, FOX)), scratch("mem_gate", (TOKENS, MEM))
        D.fox, D.mem = scratch("fox", (TOKENS, FOX)), scratch("mem", (TOKENS, MEM))
        D.wide, D.mwide = scratch("wide", (DEC_BATCH, P, FOX)), scratch("mwide", (DEC_BATCH, MEM_HEADS * DEC_SEQ, MEM))
        D.ssm = scratch("ssm", (SSM, TOKENS))
        x, xs = I["x_prompt"].rearrange("b s d -> (b s) d"), I["x_sample"].rearrange("b s d -> (b s) d")
        D.x, D.xs = x, xs
        D.y = O["y_prompt"].rearrange("b s d -> (b s) d")
        D.ys = O["y_sample"].rearrange("b s d -> (b s) d")
        D.cache_k = I["cache_fox_k"][0].rearrange("b t h d -> b t (h d)")
        D.cache_v = I["cache_fox_v"][0].rearrange("b t h d -> b t (h d)")
        D.cache_mk = I["cache_mem_k"][0].rearrange("b t h d -> b t (h d)")
        D.cache_mv = I["cache_mem_v"][0].rearrange("b t h d -> b t (h d)")
        w_in, norm_g = I["w_in"][0], I["norm_g"][0]
        D.cache_logf = I["cache_fox_logf"][0]
        D.o_k = O["fox_k_prompt"].rearrange("l b t h d -> (l b t) (h d)")
        D.o_v = O["fox_v_prompt"].rearrange("l b t h d -> (l b t) (h d)")
        D.o_k_s = O["fox_k_sample"].rearrange("l b t h d -> (l b t) (h d)")
        D.o_v_s = O["fox_v_sample"].rearrange("l b t h d -> (l b t) (h d)")
        D.o_logf = O["fox_logf_prompt"].rearrange("l b t h -> (l b t) h")
        D.o_logf_s = O["fox_logf_sample"].rearrange("l b t h -> (l b t) h")
        D.o_mk = O["mem_k_prompt"].rearrange("l b t h d -> (l b t) (h d)")
        D.o_mv = O["mem_v_prompt"].rearrange("l b t h d -> (l b t) (h d)")

        def tile_rows(prompt, sample=None):
            def rows(t):
                if sample is not None and isinstance(t, int) and t == PROMPT_TILES:
                    return sample
                return prompt[bass.ts(t, P), :]
            return rows

        K.ident, K.identb, K.causal = a.sb("ident", [P, P]), a.sb("identb", [P, P], BF16), a.sb("causal", [P, P], BF16)
        K.neghalf, K.one = a.sb("neghalf", [P, FOX_HEADS]), a.sb("one", [P, 1])
        K.logits = a.sb("logits", [P, TILES * FOX_HEADS])
        constants_phase(nc, K)
        mem = I["mem_prompt"].rearrange("b s d -> (b s) d")
        project(nc, K, "m", [(mem, N_MEM // P)], [(0, 2 * MEM)], I["w_mem_kv"][0], I["mem_norm"][0],
                [[Piece("heads", MEM, nat=tile_rows(D.o_mk), gain=I["mem_k_norm"][0], scratch=D.mk),
                  Piece("plain", MEM, nat=tile_rows(D.o_mv))]],
                [("X",), ("G", 0), ("T", 0)], 1)
        with ExitStack() as inner:
            b = Place(nc, inner, "s5io")
            K.su = b.sb("su", [P, 2, 8, TOKENS // 8])
            K.sg = b.sb("sg", [P, 2, 8, TOKENS // 8])
            project(nc, K, "g", [(x, PROMPT_TILES), (xs, 1)], [(C_MQ, 2 * MEM), (C_SU, 2 * SSM), (C_FG, FOX)],
                    w_in, norm_g,
                    [[Piece("heads", MEM, last=D.mq_s, gain=I["mem_q_norm"][0], scratch=D.mq, scale=HD ** -0.5),
                      Piece("gate", MEM, nat=tile_rows(D.mem_gate))],
                     [Piece("turned", 2 * SSM)],
                     [Piece("gate", FOX, nat=tile_rows(D.fox_gate))]],
                    [("G", 0), ("G", 1), ("T", 0), ("X",), ("G", 2), ("T", 1)], 2)
            ssm_phase(nc, K, D, I, O)
        project(nc, K, "k", [(x, PROMPT_TILES), (xs, 1)], [(C_FQ, 3 * FOX), (C_FF, FOX_HEADS)], w_in, norm_g,
                [[Piece("heads", FOX, last=D.q_s, gain=I["fox_q_norm"][0], scratch=D.q, scale=HD ** -0.5)],
                 [Piece("heads", FOX, nat=tile_rows(D.o_k, D.o_k_s), gain=I["fox_k_norm"][0], scratch=D.k)],
                 [Piece("plain", FOX, nat=tile_rows(D.o_v, D.o_v_s))],
                 [Piece("logits", FOX_HEADS, bias=I["b_forget"][0])]],
                [("G", 0), ("G", 1), ("T", 0), ("X",), ("G", 2), ("T", 1), ("G", 3)], 4)
        decay_phase(nc, K, D)
        prompt_attention(nc, K, D)
        sample_attention(nc, K, D)
        output_phase(nc, K, D, I["w_out"][0])


_INS = ["x_prompt", "x_sample", "mem_prompt", "cache_fox_k", "cache_fox_v", "cache_fox_logf",
        "state_ssm_re", "state_ssm_im", "cache_mem_k", "cache_mem_v", "norm_g", "w_in", "b_forget",
        "fox_q_norm", "fox_k_norm", "ssm_a_re", "ssm_a_im", "ssm_log_dt", "ssm_b_re", "ssm_b_im",
        "ssm_c_re", "ssm_c_im", "ssm_d", "w_glu", "b_glu", "mem_norm", "w_mem_kv", "mem_q_norm",
        "mem_k_norm", "w_out"]
_OUTS = [("y_prompt", (1, SEQ, D_MODEL)), ("y_sample", (DEC_BATCH, DEC_SEQ, D_MODEL)),
         ("fox_k_prompt", (1, 1, SEQ, FOX_HEADS, HD)), ("fox_v_prompt", (1, 1, SEQ, FOX_HEADS, HD)),
         ("fox_logf_prompt", (1, 1, SEQ, FOX_HEADS)),
         ("ssm_re_prompt", (1, 1, GROUPS, STATE)), ("ssm_im_prompt", (1, 1, GROUPS, STATE)),
         ("mem_k_prompt", (1, 1, N_MEM, MEM_HEADS, HD)), ("mem_v_prompt", (1, 1, N_MEM, MEM_HEADS, HD)),
         ("fox_k_sample", (1, DEC_BATCH, DEC_SEQ, FOX_HEADS, HD)),
         ("fox_v_sample", (1, DEC_BATCH, DEC_SEQ, FOX_HEADS, HD)),
         ("fox_logf_sample", (1, DEC_BATCH, DEC_SEQ, FOX_HEADS)),
         ("ssm_re_sample", (1, DEC_BATCH, GROUPS, STATE)), ("ssm_im_sample", (1, DEC_BATCH, GROUPS, STATE))]


def kernel(**inputs):
    import concourse.bacc as bacc
    from concourse.bass_utils import run_bass_kernel_spmd

    nc = bacc.Bacc("TRN2", target_bir_lowering=False, num_devices=1)
    arrays = {f"in_{n}": np.ascontiguousarray(inputs[n]) for n in _INS}
    ins = {n: nc.dram_tensor(f"in_{n}", arrays[f"in_{n}"].shape, F32, kind="ExternalInput").ap() for n in _INS}
    outs = {n: nc.dram_tensor(f"out_{n}", shape, F32, kind="ExternalOutput").ap() for n, shape in _OUTS}
    build(nc, ins, outs)
    r = run_bass_kernel_spmd(nc, [arrays], core_ids=[0])
    return tuple(r.results[0][f"out_{n}"] for n, _ in _OUTS)
```

```python
from contextlib import ExitStack

import numpy as np

import concourse.bass as bass
from concourse import mybir

P = 128
D_MODEL = 1024
KC = D_MODEL // P
SEQ = 2048
DEC_BATCH = 8
DEC_SEQ = 16
TOKENS = SEQ + DEC_BATCH * DEC_SEQ
TILES = TOKENS // P
PROMPT_TILES = SEQ // P
PAST = 512
HD = 64
FOX_HEADS = 8
FOX = FOX_HEADS * HD
GROUPS = 16
CH = 16
SSM = GROUPS * CH
STATE = 64
MEM_HEADS = 4
MEM = MEM_HEADS * HD
N_MEM = 256
EPS = 1e-6
MASKED = -1e30

C_FQ, C_FK, C_FV, C_FG = 0, FOX, 2 * FOX, 3 * FOX
C_FF = 4 * FOX
C_SU = C_FF + FOX_HEADS
C_SG = C_SU + SSM
C_MQ = C_SG + SSM
C_MG = C_MQ + MEM
C_END = C_MG + MEM

F32 = mybir.dt.float32
F32R = mybir.dt.float32r
BF16 = mybir.dt.bfloat16
ALU = mybir.AluOpType
ACT = mybir.ActivationFunctionType
AX = mybir.AxisListType


class Place:

    def __init__(self, nc, stack, prefix):
        self.nc, self.stack, self.prefix, self.sems = nc, stack, prefix, []
        stack.callback(self.clear)

    def clear(self):
        if self.sems:
            self.nc.clear_and_free_semaphores(self.sems)
            self.nc.all_engine_barrier()

    def sb(self, name, shape, dt=F32):
        return self.stack.enter_context(self.nc.sbuf_tensor(f"{self.prefix}_{name}", shape, dt))

    def ps(self, name, shape, dt=F32):
        return self.stack.enter_context(self.nc.psum_tensor(f"{self.prefix}_{name}", shape, dt))

    def sem(self, name):
        self.sems.append(self.nc.alloc_semaphore(name=f"{self.prefix}_{name}"))
        return self.sems[-1]


def fl(ap):
    return ap.bitcast(F32)


def hold(eng, sem, value, s_held):
    eng.wait_ge(sem, value)
    eng.sem_inc(s_held, 1)


def constants_phase(nc, K):
    with ExitStack() as stack:
        a = Place(nc, stack, "cst")
        s_set = a.sem("set")
        block = stack.enter_context(nc.Block())

        @block.gpsimd
        def _(pool):
            nc.gpsimd.memset(K.ident[:, :], 0.0).then_inc(s_set, 1)
            nc.gpsimd.memset(K.identb[:, :], 0.0).then_inc(s_set, 1)
            nc.gpsimd.memset(K.causal[:, :], 0.0).then_inc(s_set, 1)
            nc.gpsimd.memset(K.neghalf[:, :], -0.5).then_inc(s_set, 1)
            nc.gpsimd.memset(K.one[:, :], 1.0).then_inc(s_set, 1)
            pool.wait_ge(s_set, 5)
            nc.gpsimd.affine_select(out=K.ident[:, :], in_=K.ident[:, :], compare_op=ALU.not_equal, fill=1.0,
                                    base=0, pattern=[[-1, P]], channel_multiplier=1).then_inc(s_set, 1)
            nc.gpsimd.affine_select(out=K.identb[:, :], in_=K.identb[:, :], compare_op=ALU.not_equal, fill=1.0,
                                    base=0, pattern=[[-1, P]], channel_multiplier=1).then_inc(s_set, 1)
            nc.gpsimd.affine_select(out=K.causal[:, :], in_=K.causal[:, :], compare_op=ALU.is_ge, fill=MASKED,
                                    base=0, pattern=[[-1, P]], channel_multiplier=1).then_inc(s_set, 1)


class Piece:

    def __init__(self, kind, n, nat=None, last=None, gain=None, scale=1.0, scratch=None, bias=None):
        self.kind, self.n, self.nat, self.last = kind, n, nat, last
        self.gain, self.scale, self.scratch, self.bias = gain, scale, scratch, bias
        self.heads = n // HD


def project(nc, K, name, sources, w_runs, w_dram, gain_dram, groups, schedule, banks_turned):
    ntiles = sum(n for _, n in sources)
    ncols = sum(n for _, n in w_runs)
    nruns = len(w_runs)
    looped = (sources[0][1] - 2) // 2 * 2 if ntiles > 4 else 0
    KT = banks_turned
    with ExitStack() as stack:
        a = Place(nc, stack, name)
        wh, wl = a.sb("wh", [P, KC, ncols], F32R), a.sb("wl", [P, KC, ncols], F32R)
        RAW = 3
        raw, gain = a.sb("raw", [P, RAW, ncols]), a.sb("gain", [P, KC])
        x = a.sb("x", [P, 2, D_MODEL])
        xth, xtl = a.sb("xth", [P, 2, KC, P], F32R), a.sb("xtl", [P, 2, KC, P], F32R)
        ssq, var = a.sb("ssq", [P, 2]), a.sb("var", [P, 2])
        rstd, half = a.sb("rstd", [P, 2]), a.sb("half", [P, 2])
        squares = a.sb("squares", [P, D_MODEL])
        xt_ps = [a.ps(f"xt{i}", [P, 4, P]) for i in range(2)]
        g_ps = [a.ps(f"g{i}", [P, 512]) for i in range(len(groups))]
        tr_ps = [a.ps(f"tr{i}", [P, 4, P]) for i in range(2)]
        s_held_sp, s_held_pool = a.sem("held_sp"), a.sem("held_pool")
        s_w = [a.sem(f"w{c}") for c in range(KC)]
        s_x = [a.sem(f"x{i}") for i in range(2)]
        s_wh, s_wl, s_gain = a.sem("w_hi"), a.sem("w_lo"), a.sem("gain")
        s_xt, s_xth, s_xtl = a.sem("x_turned"), a.sem("x_hi"), a.sem("x_lo")
        s_ssq, s_pool, s_rstd = a.sem("ssq"), a.sem("pool_chain"), a.sem("rstd")
        s_g = [a.sem(f"g{i}") for i in range(len(groups))]
        s_tr, s_tev = a.sem("turned"), a.sem("turned_read")
        act_reads, dve_reads = [[] for _ in groups], [[] for _ in groups]
        parts_gain = []
        for g, pieces in enumerate(groups):
            at = 0
            for i, p in enumerate(pieces):
                tag = f"{g}{i}"
                p.at, at = at, at + p.n
                p.s_stage = a.sem("stage" + tag)
                p.s_out = [a.sem(f"stored{tag}{b}") for b in range(2)]
                if p.kind in ("gate", "turned"):
                    m = p.n if p.kind == "gate" else p.n // 2
                    p.th, p.z = a.sb("th" + tag, [P, m]), a.sb("z" + tag, [P, m])
                    p.s_th, p.s_z = a.sem("tanh" + tag), a.sem("z" + tag)
                    act_reads[g].append(p.s_th)
                    dve_reads[g].append(p.s_z)
                if p.kind == "turned":
                    p.stage, p.s_su = a.sb("stage" + tag, [P, 4, P]), a.sem("su" + tag)
                if p.kind in ("gate", "plain", "heads"):
                    p.stage = a.sb("stage" + tag, [P, 2, p.n])
                if p.kind == "plain":
                    act_reads[g].append(p.s_stage)
                if p.kind == "heads":
                    p.sq, p.qn = a.sb("sq" + tag, [P, p.n]), a.sb("qn" + tag, [P, p.n])
                    p.hs, p.hv, p.hr = (a.sb(k + tag, [P, p.heads]) for k in ("hs", "hv", "hr"))
                    p.parts = a.sb("parts" + tag, [P, p.heads, 2 * HD])
                    p.turned = a.sb("turned" + tag, [P, 2, p.heads, P])
                    p.s_tout = [a.sem(f"tstored{tag}{b}") for b in range(2)]
                    p.s_sq, p.s_hs, p.s_hr, p.s_qn, p.s_hi, p.s_lo = (
                        a.sem(k + tag) for k in ("sq", "hsum", "hrstd", "qn", "hi", "lo"))
                    act_reads[g].append(p.s_sq)
                    dve_reads[g].append(p.s_qn)
                    p.gain_sb = a.sb("hgain" + tag, [P, HD])
                    parts_gain.append((p.gain_sb, p.gain))
                if p.kind == "logits":
                    p.bias_sb = a.sb("bias" + tag, [P, p.n])
                    dve_reads[g].append(p.s_stage)
                    parts_gain.append((p.bias_sb, p.bias))
        first, nbanks = {}, {}
        for step in schedule:
            if step[0] == "T":
                first[step[1]] = sum(nbanks.values())
                nbanks[step[1]] = sum(2 * p.n if p.kind == "heads" else p.n for p in groups[step[1]]
                                      if p.kind in ("heads", "turned")) // 512
        assert sum(nbanks.values()) == KT

        def rows(t):
            if isinstance(t, int) and t >= sources[0][1]:
                return sources[1][0]
            return sources[0][0][bass.ts(t, P), :]

        def tiles(eng, body):
            for t in range(2):
                body(t, t)
            if looped:
                with eng.Fori(1, looped // 2) as i:
                    for u in range(2):
                        body(i * 2 + u, u)
            for t in range(max(looped, 2), ntiles):
                body(t, t % 2)

        def last_tile(t):
            return isinstance(t, int) and t == ntiles - 1

        def bank(t, k):
            return k % 2 if KT % 2 == 0 else (t * KT + k) % 2

        def turned_pieces(g):
            return [p for p in groups[g] if p.kind in ("heads", "turned")]

        block = stack.enter_context(nc.Block())

        @block.sync
        def _(sp):
            sp.dma_start(gain[:, :], gain_dram.rearrange("(c p) -> p c", p=P), allow_slow_non_contiguous=True).then_inc(s_gain, 16)
            for dst, src in parts_gain:
                sp.dma_start(dst[:, :], src.partition_broadcast(P)).then_inc(s_gain, 16)
            for t in range(2):
                sp.dma_start(x[:, t, :], rows(t)).then_inc(s_x[t], 16)
            for c in range(KC):
                if c >= RAW:
                    sp.wait_ge(s_wh, c - RAW + 1)
                    sp.wait_ge(s_wl, c - RAW + 1)
                at = 0
                for c0, n in w_runs:
                    sp.dma_start(raw[:, c % RAW, at:at + n],
                                 w_dram[c * P:(c + 1) * P, c0:c0 + n]).then_inc(s_w[c], 16)
                    at += n
            for pieces in groups:
                for p in pieces:
                    for b in range(2):
                        if p.nat:
                            sp.sem_inc(p.s_out[b], 16)
                        if p.kind == "heads":
                            sp.sem_inc(p.s_tout[b], 16)

            def body(t, u):
                if not isinstance(t, int) or t + 2 < ntiles:
                    sp.wait_ge(s_xt, (t + 1) * 2)
                    sp.wait_ge(s_ssq, t + 1)
                    sp.dma_start(x[:, u, :], rows(t + 2)).then_inc(s_x[u], 16)
                for step in schedule:
                    if step[0] == "G":
                        for p in groups[step[1]]:
                            if p.nat:
                                sp.wait_ge(p.s_stage, t + 1)
                                sp.dma_start(p.nat(t), p.stage[:, u, :]).then_inc(p.s_out[u], 16)
                            if p.last is not None and last_tile(t):
                                sp.wait_ge(p.s_stage, t + 1)
                                sp.dma_start(p.last, p.stage[:, u, :]).then_inc(p.s_out[u], 16)
                    if step[0] == "T":
                        for p in groups[step[1]]:
                            if p.kind == "heads":
                                hold(sp, s_tev, t * KT + first[step[1]] + nbanks[step[1]] + 1, s_held_sp)
                                sp.dma_start(p.scratch[:, :, bass.ts(t, P)].rearrange("h p t -> p h t"),
                                             p.turned[:, u, :, :]).then_inc(p.s_tout[u], 16)

            tiles(sp, body)
            for pieces in groups:
                for p in pieces:
                    for b in range(2):
                        if p.nat:
                            sp.wait_ge(p.s_out[b], 16 * (1 + (ntiles + 1 - b) // 2))
                        if p.kind == "heads":
                            sp.wait_ge(p.s_tout[b], 16 * (1 + (ntiles + 1 - b) // 2))
                    if p.last is not None:
                        sp.wait_ge(p.s_out[(ntiles - 1) % 2], 16)

        @block.tensor
        def _(pe):
            def turn_x(t, u):
                pe.wait_ge(s_x[u], (t - u) * 8 + 16)
                pe.wait_ge(s_xtl, t * 2)
                for h in range(2):
                    for c in range(4):
                        at = (4 * h + c) * P
                        last = nc.tensor.transpose(xt_ps[h][:, c, :], x[:, u, at:at + P], K.ident[:, :])
                    last.then_inc(s_xt, 1)

            def products_as_weights_come():
                for c in range(KC):
                    pe.wait_ge(s_wl, c + 1)
                    at = 0
                    for g, pieces in enumerate(groups):
                        n = sum(p.n for p in pieces)
                        for k, (xs, ws) in enumerate(((xth, wh), (xtl, wh), (xth, wl))):
                            last = nc.tensor.matmul(g_ps[g][:, 0:n], xs[:, 0, c, :], ws[:, c, at:at + n],
                                                    start=(c == 0 and k == 0), stop=(c == KC - 1 and k == 2))
                        if c == KC - 1:
                            last.then_inc(s_g[g], 1)
                        at += n

            first_product = next(step for step in schedule if step[0] == "G")

            def body(t, u):
                for step in schedule:
                    if step[0] == "X" and not last_tile(t):
                        turn_x(t + 1, 1 - u)
                    if step[0] == "G":
                        g = step[1]
                        at = sum(p.n for ps in groups[:g] for p in ps)
                        n = sum(p.n for p in groups[g])
                        pe.wait_ge(s_xtl, (t + 1) * 2)
                        if isinstance(t, int) and t == 0:
                            if step == first_product:
                                products_as_weights_come()
                            continue
                        for s in act_reads[g] + dve_reads[g]:
                            pe.wait_ge(s, t)
                        for c in range(KC):
                            for k, (xs, ws) in enumerate(((xth, wh), (xtl, wh), (xth, wl))):
                                last = nc.tensor.matmul(g_ps[g][:, 0:n], xs[:, u, c, :], ws[:, c, at:at + n],
                                                        start=(c == 0 and k == 0), stop=(c == KC - 1 and k == 2))
                        last.then_inc(s_g[g], 1)
                    if step[0] == "T":
                        g = step[1]
                        k = first[g]
                        for p in turned_pieces(g):
                            if p.kind == "heads":
                                pe.wait_ge(p.s_lo, t + 1)
                                blocks = [p.parts[:, j, :] for j in range(p.heads)]
                            else:
                                pe.wait_ge(p.s_su, t + 1)
                                pe.wait_ge(p.s_stage, t + 1)
                                blocks = [p.stage[:, j, :] for j in range(4)]
                            for j, b in enumerate(blocks):
                                if j % 4 == 0:
                                    pe.wait_ge(s_tev, t * KT + k)
                                last = nc.tensor.transpose(tr_ps[bank(t, k)][:, j % 4, :], b, K.ident[:, :])
                                if j % 4 == 3:
                                    last.then_inc(s_tr, 1)
                                    k += 1

            pe.sem_inc(s_tr, KT)
            turn_x(0, 0)
            tiles(pe, body)

        @block.scalar
        def _(act):
            act.sem_inc(s_tev, 1)

            def split_x(t, u):
                for h in range(2):
                    act.wait_ge(s_xt, t * 2 + h + 1)
                    nc.scalar.activation(xth[:, u, 4 * h:4 * h + 4, :], xt_ps[h][:, :, :], ACT.Copy).then_inc(s_xth, 1)
                act.wait_ge(s_x[u], (t - u) * 8 + 16)
                act.wait_ge(s_ssq, t)
                nc.scalar.activation(squares[:, :], x[:, u, :], ACT.Square, accum_out=ssq[:, u:u + 1]).then_inc(s_ssq, 1)

            split_x(0, 0)
            act.wait_ge(s_gain, 16 * (1 + len(parts_gain)))
            for c in range(KC):
                act.wait_ge(s_w[c], 16 * nruns)
                nc.scalar.activation(wh[:, c, :], raw[:, c % RAW, :], ACT.Copy, scale=gain[:, c:c + 1]).then_inc(s_wh, 1)

            def body(t, u):
                for step in schedule:
                    if step[0] == "X" and not last_tile(t):
                        split_x(t + 1, 1 - u)
                    if step[0] == "G":
                        g = step[1]
                        act.wait_ge(s_g[g], t + 1)
                        act.wait_ge(s_rstd, t + 1)
                        for p in groups[g]:
                            src = g_ps[g][:, p.at:p.at + p.n]
                            if p.kind in ("gate", "turned"):
                                act.wait_ge(p.s_stage, t)
                                nc.scalar.activation(p.th[:, :], src[:, p.n // 2:] if p.kind == "turned" else src,
                                                     ACT.Tanh, scale=half[:, u:u + 1]).then_inc(p.s_th, 1)
                            if p.kind == "plain":
                                act.wait_ge(p.s_out[u], (t - u) * 8 + 16)
                                nc.scalar.activation(p.stage[:, u, :], src, ACT.Copy,
                                                     scale=rstd[:, u:u + 1]).then_inc(p.s_stage, 1)
                            if p.kind == "heads":
                                act.wait_ge(p.s_hs, t)
                                nc.scalar.activation(p.sq[:, :], src, ACT.Square,
                                                     scale=rstd[:, u:u + 1]).then_inc(p.s_sq, 1)
                    if step[0] == "H":
                        g = step[1]
                        for p in groups[g]:
                            if p.kind == "heads":
                                act.wait_ge(p.s_stage, t + 1)
                                act.wait_ge(s_tr, t * KT + first[g] + nbanks[g])
                                nc.scalar.activation(p.parts[:, :, 0:HD].bitcast(F32R),
                                                     p.stage[:, u, :].rearrange("p (h d) -> p h d", d=HD),
                                                     ACT.Copy).then_inc(p.s_hi, 1)
                    if step[0] == "T":
                        g = step[1]
                        k = first[g]
                        for p in turned_pieces(g):
                            if p.kind == "heads":
                                act.wait_ge(p.s_tout[u], (t - u) * 8 + 16)
                                for j in range(p.heads // 4):
                                    act.wait_ge(s_tr, t * KT + KT + k + 1)
                                    nc.scalar.activation(p.turned[:, u, 4 * j:4 * j + 4, :], tr_ps[bank(t, k)][:, :, :],
                                                         ACT.Copy).then_inc(s_tev, 1)
                                    k += 1
                            else:
                                act.wait_ge(s_tr, t * KT + KT + k + 1)
                                for c in range(2):
                                    nc.scalar.activation(
                                        K.su[:, c, :, bass.ts(t, P // 8)],
                                        tr_ps[bank(t, k)][:, c, :].rearrange("p (j s) -> p s j", s=8), ACT.Copy)
                                nc.scalar.activation(K.sg[:, :, :, bass.ts(t, P // 8)].rearrange("p c s j -> p c j s"),
                                                     tr_ps[bank(t, k)][:, 2:4, :].rearrange("p c (j s) -> p c j s", s=8),
                                                     ACT.Copy).then_inc(s_tev, 1)
                                k += 1

            tiles(act, body)

        @block.vector
        def _(dve):
            def split_x(t, u):
                for h in range(2):
                    dve.wait_ge(s_xth, t * 2 + h + 1)
                    nc.vector.tensor_tensor(xtl[:, u, 4 * h:4 * h + 4, :], xt_ps[h][:, :, :],
                                            fl(xth[:, u, 4 * h:4 * h + 4, :]), ALU.subtract).then_inc(s_xtl, 1)

            split_x(0, 0)
            dve.wait_ge(s_gain, 16 * (1 + len(parts_gain)))
            for c in range(KC):
                dve.wait_ge(s_wh, c + 1)
                nc.vector.scalar_tensor_tensor(wl[:, c, :], raw[:, c % RAW, :], gain[:, c:c + 1], fl(wh[:, c, :]),
                                               ALU.mult, ALU.subtract).then_inc(s_wl, 1)

            def normalise_heads(g, t, u):
                by_head = "p (h d) -> p h d"
                for p in groups[g]:
                    if p.kind == "heads":
                        src = g_ps[g][:, p.at:p.at + p.n]
                        dve.wait_ge(p.s_hr, t + 1)
                        nc.vector.tensor_tensor(p.qn[:, :].rearrange(by_head, d=HD), src.rearrange(by_head, d=HD),
                                                p.hr[:, :, None].to_broadcast([P, p.heads, HD]),
                                                ALU.mult).then_inc(p.s_qn, 1)
                        dve.wait_ge(p.s_qn, t + 1)
                        if p.nat:
                            dve.wait_ge(p.s_out[u], (t - u) * 8 + 16)
                        nc.vector.tensor_tensor(p.stage[:, u, :].rearrange(by_head, d=HD),
                                                p.qn[:, :].rearrange(by_head, d=HD),
                                                p.gain_sb[:, None, :].to_broadcast([P, p.heads, HD]),
                                                ALU.mult).then_inc(p.s_stage, 1)
                        dve.wait_ge(p.s_hi, t + 1)
                        nc.vector.tensor_tensor(p.parts[:, :, HD:2 * HD].bitcast(F32R),
                                                p.stage[:, u, :].rearrange(by_head, d=HD), p.parts[:, :, 0:HD],
                                                ALU.subtract).then_inc(p.s_lo, 1)

            def body(t, u):
                for step in schedule:
                    if step[0] == "X" and not last_tile(t):
                        split_x(t + 1, 1 - u)
                    if step[0] == "H":
                        normalise_heads(step[1], t, u)
                    if step[0] != "G" or all(p.kind == "plain" for p in groups[step[1]]):
                        continue
                    g = step[1]
                    dve.wait_ge(s_g[g], t + 1)
                    dve.wait_ge(s_rstd, t + 1)
                    for s in act_reads[g]:
                        dve.wait_ge(s, t + 1)
                    for p in groups[g]:
                        src = g_ps[g][:, p.at:p.at + p.n]
                        if p.kind == "gate":
                            nc.vector.tensor_scalar(p.z[:, :], src, half[:, u:u + 1], None, ALU.mult).then_inc(p.s_z, 1)
                            dve.wait_ge(p.s_z, t + 1)
                            dve.wait_ge(p.s_th, t + 1)
                            dve.wait_ge(p.s_out[u], (t - u) * 8 + 16)
                            nc.vector.scalar_tensor_tensor(p.stage[:, u, :], p.th[:, :], 1.0, p.z[:, :],
                                                           ALU.add, ALU.mult).then_inc(p.s_stage, 1)
                        if p.kind == "turned":
                            dve.wait_ge(s_tr, t * KT + first[g] + nbanks[g])
                            n = p.n // 2
                            nc.vector.tensor_scalar(p.stage[:, 0:2, :], src[:, 0:n].rearrange("p (c n) -> p c n", c=2),
                                                    rstd[:, u:u + 1], None, ALU.mult).then_inc(p.s_su, 1)
                            nc.vector.tensor_scalar(p.z[:, :], src[:, n:], half[:, u:u + 1], None,
                                                    ALU.mult).then_inc(p.s_z, 1)
                            dve.wait_ge(p.s_z, t + 1)
                            dve.wait_ge(p.s_th, t + 1)
                            nc.vector.scalar_tensor_tensor(p.stage[:, 2:4, :],
                                                           p.th[:, :].rearrange("p (c n) -> p c n", c=2), 1.0,
                                                           p.z[:, :].rearrange("p (c n) -> p c n", c=2),
                                                           ALU.add, ALU.mult).then_inc(p.s_stage, 1)
                        if p.kind == "logits":
                            nc.vector.scalar_tensor_tensor(K.logits[:, bass.ts(t, FOX_HEADS)], src, rstd[:, u:u + 1],
                                                           p.bias_sb[:, :], ALU.mult, ALU.add).then_inc(p.s_stage, 1)
                        if p.kind == "heads":
                            by_head = "p (h d) -> p h d"
                            dve.wait_ge(p.s_sq, t + 1)
                            dve.wait_ge(p.s_hr, t)
                            nc.vector.tensor_reduce(p.hs[:, :], p.sq[:, :].rearrange(by_head, d=HD), AX.X,
                                                    ALU.add).then_inc(p.s_hs, 1)

            tiles(dve, body)

        @block.gpsimd
        def _(pool):
            heads = [p for ps in groups for p in ps if p.kind == "heads"]
            per_tile = 2 + 2 * len(heads)

            def row_rms(t, u, base):
                hold(pool, s_ssq, t + 1, s_held_pool)
                nc.gpsimd.tensor_scalar(var[:, 0:1], ssq[:, u:u + 1], 1.0 / D_MODEL, EPS, ALU.mult,
                                        ALU.add).then_inc(s_pool, 1)
                pool.wait_ge(s_pool, base + 1)
                nc.gpsimd.tensor_tensor(rstd[:, u:u + 1], var[:, 0:1], K.neghalf[:, 0:1], ALU.pow).then_inc(s_pool, 1)
                hold(pool, s_pool, base + 2, s_held_pool)
                nc.gpsimd.tensor_scalar(half[:, u:u + 1], rstd[:, u:u + 1], 0.5, None, ALU.mult).then_inc(s_rstd, 1)

            def body(t, u):
                n = 0
                for step in schedule:
                    base = t * per_tile + 2 + n
                    if step[0] == "X" and not last_tile(t):
                        for s in sum(dve_reads, []):
                            pool.wait_ge(s, t)
                        row_rms(t + 1, 1 - u, base)
                        n += 2
                    if step[0] == "G":
                        for p in groups[step[1]]:
                            if p.kind != "heads":
                                continue
                            base = t * per_tile + 2 + n
                            hold(pool, p.s_hs, t + 1, s_held_pool)
                            nc.gpsimd.tensor_scalar(p.hs[:, :], p.hs[:, :], 1.0 / HD, EPS, ALU.mult,
                                                    ALU.add).then_inc(s_pool, 1)
                            pool.wait_ge(s_pool, base + 1)
                            nc.gpsimd.tensor_tensor(p.hv[:, :], p.hs[:, :], K.neghalf[:, 0:p.heads],
                                                    ALU.pow).then_inc(s_pool, 1)
                            pool.wait_ge(p.s_qn, t)
                            hold(pool, s_pool, base + 2, s_held_pool)
                            nc.gpsimd.tensor_scalar(p.hr[:, :], p.hv[:, :], rstd[:, u:u + 1], p.scale,
                                                    ALU.mult, ALU.mult).then_inc(p.s_hr, 1)
                            n += 2

            row_rms(0, 0, 0)
            tiles(pool, body)


def decay_phase(nc, K, D):
    NG = TILES * FOX_HEADS
    with ExitStack() as stack:
        a = Place(nc, stack, "decay")
        e, ab, lf = a.sb("exp", [P, NG]), a.sb("abs", [P, NG]), a.sb("logf", [P, NG])
        cache = a.sb("cache", [P, PAST // P, DEC_BATCH, FOX_HEADS])
        rows = a.sb("rows", [FOX_HEADS, SEQ])
        csum = a.sb("csum", [FOX_HEADS, SEQ])
        ones = a.sb("ones", [DEC_BATCH * FOX_HEADS, SEQ])
        hi, lo = a.sb("hi", [FOX_HEADS, SEQ], F32R), a.sb("lo", [FOX_HEADS, SEQ], F32R)
        srows = a.sb("srows", [DEC_BATCH * FOX_HEADS, PAST + DEC_SEQ])
        ssum = a.sb("ssum", [DEC_BATCH * FOX_HEADS, PAST + DEC_SEQ])
        ps = [a.ps(f"t{i}", [P, 4, P]) for i in range(5)]
        s_cache, s_abs, s_e, s_ln, s_lf = (a.sem(k) for k in ("cache", "abs", "exp", "ln", "logf"))
        s_out, s_back, s_t, s_rows, s_ones = (a.sem(k) for k in ("stored", "back", "turned", "rows", "ones"))
        s_sum, s_hi, s_parts, s_end = (a.sem(k) for k in ("sum", "hi", "parts", "end"))
        block = stack.enter_context(nc.Block())
        C = FOX_HEADS
        NS = DEC_BATCH * C

        @block.sync
        def _(sp):
            for k in range(PAST // P):
                sp.dma_start(cache[:, k, :, :], D.cache_logf[:, k * P:(k + 1) * P, :].rearrange("b p h -> p b h"))\
                    .then_inc(s_cache, 16)
            sp.wait_ge(s_lf, 1)
            sp.dma_start(D.o_logf.rearrange("(t p) h -> p t h", p=P),
                         lf[:, 0:PROMPT_TILES * C].rearrange("p (t h) -> p t h", h=C)).then_inc(s_out, 16)
            sp.dma_start(D.o_logf_s, lf[:, PROMPT_TILES * C:NG]).then_inc(s_back, 16)
            sp.wait_ge(s_back, 16)
            for b in range(DEC_BATCH):
                sp.dma_start(srows[b * C:(b + 1) * C, PAST:],
                             D.o_logf_s[b * DEC_SEQ:(b + 1) * DEC_SEQ, :].rearrange("t h -> h t"),
                             allow_slow_non_contiguous=True).then_inc(s_back, 16)
            sp.wait_ge(s_parts, 1)
            for part, src in ((0, hi), (1, lo)):
                sp.dma_start(D.decay[:, part, :], fl(src[:, :])).then_inc(s_out, 16)
            sp.wait_ge(s_sum, 2)
            sp.dma_start(D.decay_s.rearrange("b h t -> (b h) t"), ssum[:, :]).then_inc(s_out, 16)
            sp.wait_ge(s_out, 64)

        @block.gpsimd
        def _(pool):
            nc.gpsimd.memset(ones[:, :], 1.0).then_inc(s_ones, 1)

        @block.scalar
        def _(act):
            act.wait_ge(s_abs, 1)
            nc.scalar.activation(e[:, :], ab[:, :], ACT.Exp, scale=-1.0).then_inc(s_e, 1)
            act.wait_ge(s_e, 1)
            nc.scalar.activation(ab[:, :], e[:, :], ACT.Ln, bias=K.one[:, 0:1]).then_inc(s_ln, 1)
            act.wait_ge(s_sum, 1)
            nc.scalar.activation(hi[:, :], csum[:, :], ACT.Copy).then_inc(s_hi, 1)

        @block.vector
        def _(dve):
            nc.vector.scalar_tensor_tensor(ab[:, :], K.logits[:, :], -1.0, K.logits[:, :], ALU.mult, ALU.max).then_inc(s_abs, 1)
            dve.wait_ge(s_ln, 1)
            nc.vector.scalar_tensor_tensor(lf[:, :], K.logits[:, :], 0.0, ab[:, :], ALU.min,
                                           ALU.subtract).then_inc(s_lf, 1)
            for i in range(4):
                dve.wait_ge(s_t, i + 1)
                nc.vector.tensor_copy(rows[:, i * 512:(i + 1) * 512], ps[i][0:C, :, :].rearrange("p a b -> p (a b)"))\
                    .then_inc(s_rows, 1)
            dve.wait_ge(s_ones, 1)
            dve.wait_ge(s_rows, 4)
            nc.vector.tensor_tensor_scan(csum[:, :], ones[0:C, :], rows[:, :], 0.0, ALU.mult,
                                         ALU.subtract).then_inc(s_sum, 1)
            dve.wait_ge(s_t, 5)
            nc.vector.tensor_copy(srows[:, 0:PAST], ps[4][0:NS, :, :].rearrange("p a b -> p (a b)")).then_inc(s_rows, 1)
            dve.wait_ge(s_rows, 5)
            dve.wait_ge(s_back, 16 * (1 + DEC_BATCH))
            nc.vector.tensor_tensor_scan(ssum[:, :], ones[0:NS, 0:PAST + DEC_SEQ], srows[:, :], 0.0, ALU.mult,
                                         ALU.subtract).then_inc(s_sum, 1)
            dve.wait_ge(s_hi, 1)
            nc.vector.tensor_tensor(lo[:, :], csum[:, :], fl(hi[:, :]), ALU.subtract).then_inc(s_parts, 1)

        @block.tensor
        def _(pe):
            pe.wait_ge(s_lf, 1)
            for i in range(4):
                for j in range(4):
                    last = nc.tensor.transpose(ps[i][0:C, j, :], lf[:, (4 * i + j) * C:(4 * i + j + 1) * C],
                                               K.ident[:, :])
                last.then_inc(s_t, 1)
            pe.wait_ge(s_cache, 16 * (PAST // P))
            for k in range(PAST // P):
                last = nc.tensor.transpose(ps[4][0:NS, k, :], cache[:, k, :, :].rearrange("p b h -> p (b h)"),
                                           K.ident[:, :])
            last.then_inc(s_t, 1)


def ssm_phase(nc, K, D, I, O):
    L = 16
    PAIRS = GROUPS // 2
    NB = SEQ // L
    NBS = NB + DEC_BATCH
    J = TOKENS // 8
    PAD = 7 * CH
    LEVELS = NB.bit_length() - 1
    NS = PAIRS * DEC_BATCH
    c1 = 6.28125
    c2 = round((2 * np.pi - c1) * 2 ** 21) / 2 ** 21
    c3 = 2 * np.pi - c1 - c2
    ROUND = 12582912.0
    RE, IM = 0, 1

    with ExitStack() as stack:
        a = Place(nc, stack, "ssm")
        prm = a.sb("prm", [P, 3, PAIRS])
        are, aim, log_dt = (prm[:, k, :] for k in range(3))
        dt, decay, theta, turns, ang, ang2, mag, cos, sin, den, rden, am1, zr, zi, x1, x2 = (
            a.sb(k, [P, PAIRS])[:, :] for k in ("dt", "decay", "theta", "turns", "ang", "ang2", "mag", "cos", "sin",
                                                "den", "rden", "am1", "zr", "zi", "x1", "x2"))
        braw = a.sb("braw", [P, 2, PAIRS, CH])
        craw = a.sb("craw", [P, 2, P])
        ct = a.sb("ct", [P, 2, PAIRS, CH])
        bbar = a.sb("bbar", [P, 2, PAIRS, CH])
        pw, pw_rev = a.sb("pw", [P, 2, L + 1, PAIRS]), a.sb("pw_rev", [P, 2, L, PAIRS])
        lvl = a.sb("lvl", [P, 2, LEVELS, PAIRS])
        wb = a.sb("wb", [P, 2, PAIRS, L, CH])
        wbt = a.sb("wbt", [P, PAIRS, 2, 2, P])
        ca = a.sb("ca", [P, 2, PAIRS, L + 1, CH])
        t1, t2 = a.sb("t1", [P, PAIRS * (L + 1) * CH]), a.sb("t2", [P, PAIRS * (L + 1) * CH])
        kern_mem = a.sb("kern", [P, GROUPS * (PAD + L * CH)])
        kern = kern_mem[0:CH, :].rearrange("p (g n) -> p g n", g=GROUPS)
        final = kern_mem[:, 0:2 * 8 * J].rearrange("p (m j s) -> p m j s", m=2, s=8)
        skip = a.sb("skip", [CH, GROUPS, CH])
        toep = a.sb("toep", [P, GROUPS, L * CH])
        u = a.sb("u", [P, GROUPS, J])
        hraw = a.sb("hraw", [NS, 2, P])
        scan = a.sb("scan", [P, 2, PAIRS, NBS])
        before = a.sb("before", [P, 2, PAIRS, NBS])
        end_p, end_s = a.sb("end_p", [P, 2, PAIRS]), a.sb("end_s", [P, 2, NS])
        out_p, out_s = a.sb("out_p", [PAIRS, 2, P]), a.sb("out_s", [NS, 2, P])
        wglu, bglu, bhalf = a.sb("wglu", [P, 2, SSM]), a.sb("bglu", [P, 2]), a.sb("bhalf", [P, 2])
        gt = a.sb("gt", [P, 2, J])
        ps = [a.ps(f"p{i}", [P, 512]) for i in range(8)]
        (s_load, s_exp, s_prm, s_trig, s_wb, s_wbt, s_mats, s_ct, s_bc, s_kern, s_kread, s_kdone, s_toep, s_uin, s_h0,
         s_drive, s_dread, s_before, s_y, s_yread, s_sq, s_poly, s_tanh, s_gelu, s_yt, s_glu, s_gtanh, s_final, s_ends,
         s_eread, s_state, s_stored, s_dve, s_bounce, s_yout, s_aload) = (a.sem(k) for k in (
             "load exp prm trig wb wbt mats ct bc kern kread kdone toep uin h0 drive dread before y yread sq poly "
             "tanh gelu yt glu gtanh final ends eread state stored dve bounce yout aload").split())
        NA, NLOAD = 2 + 2, 1 + 2 + 2 * PAIRS + 1 + 2 * PAIRS + 2
        CHUNK = GROUPS // 4 * J
        block = stack.enter_context(nc.Block())

        def ys(k):
            return u[:, 4 * k:4 * k + 4, :].rearrange("p g j -> p (g j)")

        @block.sync
        def _(sp):
            def load(dst, src, sem=None):
                sp.dma_start(dst, src).then_inc(sem or s_load, 16)

            with nc.allow_non_contiguous_dma(reason="parameters: a thousand words each"):
                load(are, I["ssm_a_re"][0].rearrange("(g r) n -> (r n) g", r=2), s_aload)
                load(aim, I["ssm_a_im"][0].rearrange("(g r) n -> (r n) g", r=2), s_aload)
                for r in range(2):
                    load(prm[r * STATE:(r + 1) * STATE, 2, :],
                         I["ssm_log_dt"][0].rearrange("(g r) -> r g", r=2)[r, :].partition_broadcast(STATE), s_aload)
                load(bglu[:, :], I["b_glu"][0].rearrange("(c p) -> p c", p=P))
            for k, b in enumerate((I["ssm_b_re"], I["ssm_b_im"])):
                load(braw[:, k, :, :], b[0].rearrange("(g r) n q -> (r n) g q", r=2))
            for k, c in enumerate((I["ssm_c_re"], I["ssm_c_im"])):
                for g in range(PAIRS):
                    load(craw[g * CH:(g + 1) * CH, k, :].rearrange("p (r n) -> p r n", r=2),
                         c[0, 2 * g:2 * g + 2, :, :].rearrange("r p n -> p r n"))
            load(skip[:, :, :].rearrange("q g p -> q (g p)"),
                 I["ssm_d"][0].rearrange("g p -> (g p)").partition_broadcast(CH))
            for k, h in enumerate((I["state_ssm_re"], I["state_ssm_im"])):
                for g in range(PAIRS):
                    load(hraw[g * DEC_BATCH:(g + 1) * DEC_BATCH, k, :],
                         h[0, :, 2 * g:2 * g + 2, :].rearrange("b r n -> b (r n)"))
            for c in range(2):
                load(wglu[:, c, :], I["w_glu"][0, c * P:(c + 1) * P, :])
            sp.wait_ge(s_bounce, 32)
            for s in range(8):
                sp.dma_start(u[s * CH:(s + 1) * CH, :, :], D.ssm_in[s, :, :].rearrange("(g q) j -> q g j", q=CH))\
                    .then_inc(s_uin, 16)
            sp.wait_ge(s_kdone, 1)
            for s in range(8):
                sp.dma_start(toep[s * CH:(s + 1) * CH, :, :],
                             kern[:, :, PAD - s * CH:PAD - s * CH + L * CH]).then_inc(s_toep, 16)
            sp.wait_ge(s_uin, 16 * 8)
            sp.wait_ge(s_gelu, 4)
            for s in range(8):
                sp.dma_start(D.ssm_out[s, :, :].rearrange("(g q) j -> q g j", q=CH), u[s * CH:(s + 1) * CH, :, :])\
                    .then_inc(s_yout, 16)
            sp.wait_ge(s_yout, 16 * 8)
            for c in range(2):
                sp.dma_start(K.su[:, c, :, :], D.ssm_out[:, c * P:(c + 1) * P, :].rearrange("s p j -> p s j"))\
                    .then_inc(s_yt, 16)
            sp.wait_ge(s_eread, 4)
            for k, (po, so) in enumerate((("ssm_re_prompt", "ssm_re_sample"), ("ssm_im_prompt", "ssm_im_sample"))):
                sp.dma_start(O[po][0, 0].rearrange("(g r) n -> g (r n)", r=2), out_p[:, k, :]).then_inc(s_stored, 16)
                for g in range(PAIRS):
                    sp.dma_start(O[so][0, :, 2 * g:2 * g + 2, :].rearrange("b r n -> b (r n)"),
                                 out_s[g * DEC_BATCH:(g + 1) * DEC_BATCH, k, :]).then_inc(s_stored, 16)
            for m in range(2):
                sp.wait_ge(s_final, 8 * (m + 1))
                sp.dma_start(D.ssm[m * P:(m + 1) * P, :], final[:, m, :, :].rearrange("p j s -> p (j s)"))\
                    .then_inc(s_stored, 16)
            sp.wait_ge(s_stored, 16 * (2 * (1 + PAIRS) + 2))

        @block.scalar
        def _(act):
            for c in range(2):
                act.dma_start(D.ssm_in[:, c * P:(c + 1) * P, :].rearrange("s p j -> p s j"), K.su[:, c, :, :])\
                    .then_inc(s_bounce, 16)
            act.wait_ge(s_aload, 16 * NA)
            nc.scalar.activation(dt, log_dt, ACT.Exp).then_inc(s_exp, 1)
            act.wait_ge(s_prm, 1)
            nc.scalar.activation(mag, decay, ACT.Exp).then_inc(s_trig, 1)
            nc.scalar.activation(sin, ang, ACT.Sin).then_inc(s_trig, 1)
            nc.scalar.activation(cos, ang2, ACT.Sin).then_inc(s_trig, 1)
            for g in range(PAIRS):
                act.wait_ge(s_wbt, g + 1)
                nc.scalar.activation(wbt[:, g, :, :, :].rearrange("p a b c -> p (a b c)"), ps[g % 2][:, :],
                                     ACT.Copy).then_inc(s_mats, 1)
            for k in range(4):
                act.wait_ge(s_yread, 4 * (k + 1))
                act.wait_ge(s_gelu, k)
                nc.scalar.activation(t1[:, 0:CHUNK], ys(k), ACT.Square).then_inc(s_sq, 1)
                act.wait_ge(s_poly, k + 1)
                nc.scalar.activation(t1[:, 0:CHUNK], t2[:, 0:CHUNK], ACT.Tanh,
                                     scale=float(np.sqrt(2 / np.pi))).then_inc(s_tanh, 1)
            for n in range(16):
                act.wait_ge(s_glu, n + 1)
                if n >= 2:
                    act.wait_ge(s_final, n - 1)
                nc.scalar.activation(gt[:, n % 2, :], ps[n % 2][:, 0:J], ACT.Tanh, scale=0.25,
                                     bias=bhalf[:, n // 8:n // 8 + 1]).then_inc(s_gtanh, 1)

        @block.vector
        def _(dve):
            steps = [0]

            def do(ins):
                steps[0] += 1
                ins.then_inc(s_dve, 1)
                dve.wait_ge(s_dve, steps[0])

            V = nc.vector

            def mul(o, x, y):
                do(V.tensor_tensor(o, x, y, ALU.mult))

            def cmul(o_re, o_im, x_re, x_im, y_re, y_im, p, q):
                mul(p, x_re, y_re)
                mul(q, x_im, y_im)
                do(V.tensor_tensor(o_re, p, q, ALU.subtract))
                mul(p, x_re, y_im)
                mul(q, x_im, y_re)
                do(V.tensor_tensor(o_im, p, q, ALU.add))

            dve.wait_ge(s_exp, 1)
            mul(decay, dt, are)
            mul(theta, dt, aim)
            do(V.tensor_scalar(turns, theta, 1.0 / (2 * np.pi), ROUND, ALU.mult, ALU.add))
            do(V.tensor_scalar(turns, turns, ROUND, None, ALU.subtract))
            do(V.scalar_tensor_tensor(x1, turns, -c1, theta, ALU.mult, ALU.add))
            do(V.scalar_tensor_tensor(x2, turns, -c2, x1, ALU.mult, ALU.add))
            do(V.scalar_tensor_tensor(x1, turns, -c3, x2, ALU.mult, ALU.add))
            do(V.tensor_scalar(ang, x1, 3.1415925, -3.1415925, ALU.min, ALU.max))
            do(V.scalar_tensor_tensor(x2, ang, -1.0, ang, ALU.mult, ALU.max))
            V.tensor_scalar(ang2, x2, -1.0, np.pi / 2, ALU.mult, ALU.add).then_inc(s_prm, 1)
            dve.wait_ge(s_trig, 3)
            a_re, a_im = pw[:, RE, 1, :], pw[:, IM, 1, :]
            mul(a_re, mag, cos)
            mul(a_im, mag, sin)
            mul(x1, are, are)
            mul(x2, aim, aim)
            do(V.tensor_tensor(den, x1, x2, ALU.add))
            do(V.reciprocal(rden, den))
            do(V.tensor_scalar(am1, a_re, 1.0, None, ALU.subtract))
            mul(x1, am1, are)
            mul(x2, a_im, aim)
            do(V.tensor_tensor(x1, x1, x2, ALU.add))
            mul(zr, x1, rden)
            mul(x1, a_im, are)
            mul(x2, am1, aim)
            do(V.tensor_tensor(x1, x1, x2, ALU.subtract))
            mul(zi, x1, rden)
            n = PAIRS * CH

            def by_pair(x):
                return x.rearrange("p (g q) -> p g q", g=PAIRS)

            dve.wait_ge(s_load, 16 * NLOAD)
            do(V.tensor_scalar(bhalf[:, :], bglu[:, :], 0.5, None, ALU.mult))
            z_re, z_im = (z[:, :, None].to_broadcast([P, PAIRS, CH]) for z in (zr, zi))
            cmul(bbar[:, RE, :, :], bbar[:, IM, :, :], braw[:, RE, :, :], braw[:, IM, :, :], z_re, z_im,
                 by_pair(t1[:, 0:n]), by_pair(t2[:, 0:n]))
            do(V.memset(pw[:, RE, 0, :], 1.0))
            do(V.memset(pw[:, IM, 0, :], 0.0))
            m = 1
            while m < L:
                bc = [pw[:, k, m:m + 1, :].to_broadcast([P, m, PAIRS]) for k in (RE, IM)]
                tt = [t[:, 0:m * PAIRS].rearrange("p (t g) -> p t g", g=PAIRS) for t in (t1, t2)]
                cmul(pw[:, RE, m + 1:2 * m + 1, :], pw[:, IM, m + 1:2 * m + 1, :],
                     pw[:, RE, 1:m + 1, :], pw[:, IM, 1:m + 1, :], bc[0], bc[1], tt[0], tt[1])
                m *= 2
            do(V.tensor_copy(lvl[:, :, 0, :], pw[:, :, L, :]))
            for k in range(1, LEVELS):
                cmul(lvl[:, RE, k, :], lvl[:, IM, k, :], lvl[:, RE, k - 1, :], lvl[:, IM, k - 1, :],
                     lvl[:, RE, k - 1, :], lvl[:, IM, k - 1, :], x1, x2)
            for s in range(L):
                do(V.tensor_copy(pw_rev[:, :, s, :], pw[:, :, L - 1 - s, :]))
            full = [P, PAIRS, L, CH]
            n = PAIRS * L * CH
            tt = [t[:, 0:n].rearrange("p (g s q) -> p g s q", g=PAIRS, s=L) for t in (t1, t2)]
            rev = [pw_rev[:, k, :, :].rearrange("p s g -> p g s")[:, :, :, None].to_broadcast(full) for k in (RE, IM)]
            bb = [bbar[:, k, :, None, :].to_broadcast(full) for k in (RE, IM)]
            cmul(wb[:, RE, :, :, :], wb[:, IM, :, :, :], rev[0], rev[1], bb[0], bb[1], tt[0], tt[1])
            dve.sem_inc(s_wb, 1)
            dve.wait_ge(s_ct, 1)
            do(V.tensor_copy(ct[:, :, :, :].rearrange("p k g q -> p (k g q)"), ps[7][:, 0:2 * P]))
            full = [P, PAIRS, L + 1, CH]
            tt = [t[:, :].rearrange("p (g s q) -> p g s q", g=PAIRS, s=L + 1) for t in (t1, t2)]
            fw = [pw[:, k, :, :].rearrange("p s g -> p g s")[:, :, :, None].to_broadcast(full) for k in (RE, IM)]
            cc = [ct[:, k, :, None, :].to_broadcast(full) for k in (RE, IM)]
            mul(tt[0], fw[0], cc[0])
            mul(tt[1], fw[1], cc[1])
            flat = "p g s q -> p (g s q)"
            do(V.tensor_tensor(ca[:, RE, :, :, :].rearrange(flat), t1[:, :], t2[:, :], ALU.subtract))
            mul(tt[0], fw[0], cc[1])
            mul(tt[1], fw[1], cc[0])
            V.scalar_tensor_tensor(ca[:, IM, :, :, :].rearrange(flat), t1[:, :], -1.0, t2[:, :], ALU.mult,
                                   ALU.subtract).then_inc(s_bc, 1)
            do(V.memset(kern[:, :, 0:PAD], 0.0))
            for k in range(PAIRS):
                dve.wait_ge(s_kern, k + 1)
                for r in range(2):
                    V.tensor_copy(kern[:, 2 * k + r, PAD:], ps[2 + 2 * r + k % 2][0:CH, 0:L * CH]).then_inc(s_kread, 1)
            tt16 = t1[0:CH, 0:GROUPS * CH].rearrange("p (g q) -> p g q", g=GROUPS)
            mul(tt16, skip[:, :, :], K.ident[0:CH, None, 0:CH].to_broadcast([CH, GROUPS, CH]))
            dve.wait_ge(s_kread, 2 * PAIRS)
            V.tensor_tensor(kern[:, :, PAD:PAD + CH], kern[:, :, PAD:PAD + CH], tt16, ALU.add).then_inc(s_kdone, 1)
            for g in range(PAIRS):
                dve.wait_ge(s_drive, g + 1)
                V.tensor_copy(scan[:, :, g, :], ps[2 + g % 2][:, 0:2 * NBS].rearrange("p (k c) -> p k c", k=2))\
                    .then_inc(s_dread, 1)
            dve.wait_ge(s_h0, 1)
            do(V.tensor_copy(before[:, :, :, NB:], ps[6][:, 0:2 * NS].rearrange("p (k g b) -> p k g b", k=2, b=DEC_BATCH)))
            do(V.memset(before[:, :, :, 0:1], 0.0))
            dve.wait_ge(s_dread, PAIRS)
            full = [P, PAIRS, DEC_BATCH]
            tt = [t[:, 0:NS].rearrange("p (g b) -> p g b", g=PAIRS) for t in (t1, t2)]
            lv = [lvl[:, k, 0, :, None].to_broadcast(full) for k in (RE, IM)]
            es = [end_s[:, k, :].rearrange("p (g b) -> p g b", g=PAIRS) for k in (RE, IM)]
            h0 = [before[:, k, :, NB:] for k in (RE, IM)]
            cmul(es[0], es[1], h0[0], h0[1], lv[0], lv[1], tt[0], tt[1])
            for k in (RE, IM):
                do(V.tensor_tensor(es[k], es[k], scan[:, k, :, NB:], ALU.add))
            for up, k in [(True, k) for k in range(LEVELS)] + [(False, k) for k in range(LEVELS - 2, -1, -1)]:
                d = 1 << k
                spans = [scan[:, r, :, 0:NB].rearrange("p g (c e) -> p g c e", e=2 * d) for r in (RE, IM)]
                w = NB // (2 * d) - (0 if up else 1)
                if up:
                    to = [x[:, :, :, 2 * d - 1] for x in spans]
                    h = [x[:, :, :, d - 1] for x in spans]
                else:
                    to = [x[:, :, 1:, d - 1] for x in spans]
                    h = [x[:, :, 0:w, 2 * d - 1] for x in spans]
                tt = [t[:, 0:PAIRS * w].rearrange("p (g c) -> p g c", g=PAIRS) for t in (t1, t2)]
                lv = [lvl[:, r, k, :, None].to_broadcast([P, PAIRS, w]) for r in (RE, IM)]
                for x, y, z, o, sign in ((h[0], lv[0], (h[1], lv[1]), to[0], ALU.subtract),
                                         (h[0], lv[1], (h[1], lv[0]), to[1], ALU.add)):
                    mul(tt[0], x, y)
                    mul(tt[1], z[0], z[1])
                    do(V.tensor_tensor(tt[0], tt[0], tt[1], sign))
                    do(V.tensor_tensor(o, o, tt[0], ALU.add))
            for r in (RE, IM):
                do(V.tensor_copy(before[:, r, :, 1:NB], scan[:, r, :, 0:NB - 1]))
            V.tensor_copy(end_p[:, :, :], scan[:, :, :, NB - 1]).then_inc(s_before, 1)
            for k in range(4):
                for g in range(4 * k, 4 * k + 4):
                    dve.wait_ge(s_y, g + 1)
                    V.tensor_copy(u[:, g, :].rearrange("p (c b) -> p b c", b=2),
                                  ps[g % 4][:, 0:2 * NBS].rearrange("p (b c) -> p b c", b=2)).then_inc(s_yread, 1)
                dve.wait_ge(s_yread, 4 * (k + 1))
                dve.wait_ge(s_sq, k + 1)
                do(V.tensor_scalar(t1[:, 0:CHUNK], t1[:, 0:CHUNK], 0.044715, 1.0, ALU.mult, ALU.add))
                V.tensor_tensor(t2[:, 0:CHUNK], t1[:, 0:CHUNK], ys(k), ALU.mult).then_inc(s_poly, 1)
                dve.wait_ge(s_tanh, k + 1)
                V.scalar_tensor_tensor(ys(k), t1[:, 0:CHUNK], 1.0, ys(k), ALU.add, ALU.mult).then_inc(s_gelu, 1)
            dve.wait_ge(s_ends, 1)
            for k in range(2):
                V.tensor_copy(out_p[:, k, :], ps[4][0:PAIRS, k * P:(k + 1) * P]).then_inc(s_eread, 1)
                V.tensor_copy(out_s[:, k, :], ps[5][0:NS, k * P:(k + 1) * P]).then_inc(s_eread, 1)
            dve.wait_ge(s_yt, 16 * 2)
            dve.wait_ge(s_toep, 16 * 8)
            for n in range(16):
                m, s = n // 8, n % 8
                w = t2[:, (n % 2) * J:(n % 2 + 1) * J]
                do(V.scalar_tensor_tensor(w, K.su[:, m, s, :], 0.25, K.sg[:, m, s, :], ALU.mult, ALU.mult))
                dve.wait_ge(s_gtanh, n + 1)
                V.scalar_tensor_tensor(final[:, m, :, s], gt[:, n % 2, :], 1.0, w, ALU.add, ALU.mult).then_inc(s_final, 1)

        @block.tensor
        def _(pe):
            T = nc.tensor
            pe.wait_ge(s_load, 16 * NLOAD)
            for k in range(2):
                last = T.transpose(ps[7][:, k * P:(k + 1) * P], craw[:, k, :], K.ident[:, :])
            last.then_inc(s_ct, 1)
            for k in range(2):
                last = T.transpose(ps[6][:, k * NS:(k + 1) * NS], hraw[:, k, :], K.ident[0:NS, 0:NS])
            last.then_inc(s_h0, 1)
            pe.wait_ge(s_wb, 1)
            for g in range(PAIRS):
                if g >= 2:
                    pe.wait_ge(s_mats, g - 1)
                for b in range(2):
                    for r in (RE, IM):
                        at = (2 * b + r) * P
                        last = T.transpose(ps[g % 2][:, at:at + P],
                                           wb[:, r, g, 8 * b:8 * b + 8, :].rearrange("p s q -> p (s q)"), K.ident[:, :])
                last.then_inc(s_wbt, 1)
            pe.wait_ge(s_bc, 1)
            for k in range(PAIRS):
                if k >= 2:
                    pe.wait_ge(s_kread, 2 * (k - 1))
                for r in range(2):
                    rows = slice(r * STATE, (r + 1) * STATE)
                    for c in (RE, IM):
                        last = T.matmul(ps[2 + 2 * r + k % 2][0:CH, 0:L * CH], bbar[rows, c, k, :],
                                        ca[rows, c, k, 0:L, :].rearrange("p t q -> p (t q)"),
                                        start=c == RE, stop=c == IM)
                last.then_inc(s_kern, 1)
            pe.wait_ge(s_kread, 2 * PAIRS)
            pe.wait_ge(s_uin, 16 * 8)
            pe.wait_ge(s_mats, PAIRS)
            for g in range(PAIRS):
                if g >= 2:
                    pe.wait_ge(s_dread, g - 1)
                for r in range(2):
                    for c in (RE, IM):
                        for b in range(2):
                            last = T.matmul(ps[2 + g % 2][r * STATE:(r + 1) * STATE, c * NBS:(c + 1) * NBS],
                                            wbt[:, g, b, c, r * STATE:(r + 1) * STATE],
                                            u[:, 2 * g + r, :].rearrange("p (c b) -> p b c", b=2)[:, b, :],
                                            start=b == 0, stop=b == 1)
                last.then_inc(s_drive, 1)
            pe.wait_ge(s_toep, 16 * 8)
            pe.wait_ge(s_dread, PAIRS)

            def from_inputs(g):
                halves = u[:, g, :].rearrange("p (c b) -> p b c", b=2)
                for b in range(2):
                    for k in range(b + 1):
                        T.matmul(ps[g % 4][:, b * NBS:(b + 1) * NBS], toep[:, g, (b - k) * P:(b - k + 1) * P],
                                 halves[:, k, :], start=b == 0, stop=False)

            for g in range(4):
                from_inputs(g)
            pe.wait_ge(s_before, 1)
            for g in range(GROUPS):
                if g >= 4:
                    pe.wait_ge(s_yread, g - 3)
                    from_inputs(g)
                rows = slice(g % 2 * STATE, (g % 2 + 1) * STATE)
                for b in range(2):
                    for c in (RE, IM):
                        last = T.matmul(ps[g % 4][:, b * NBS:(b + 1) * NBS],
                                        ca[rows, c, g // 2, 1 + 8 * b:9 + 8 * b, :].rearrange("p t q -> p (t q)"),
                                        before[rows, c, g // 2, :], start=False, stop=b == 1 and c == IM)
                last.then_inc(s_y, 1)
            for k in range(2):
                T.transpose(ps[4][0:PAIRS, k * P:(k + 1) * P], end_p[:, k, :], K.ident[:, :])
                last = T.transpose(ps[5][0:NS, k * P:(k + 1) * P], end_s[:, k, :], K.ident[:, :])
            last.then_inc(s_ends, 1)
            pe.wait_ge(s_yt, 16 * 2)
            for n in range(16):
                m, s = n // 8, n % 8
                if n >= 2:
                    pe.wait_ge(s_gtanh, n - 1)
                for c in range(2):
                    last = T.matmul(ps[n % 2][:, 0:J], wglu[:, c, m * P:(m + 1) * P], K.su[:, c, s, :],
                                    start=c == 0, stop=c == 1)
                last.then_inc(s_glu, 1)


class Block512:

    def __init__(self, h, kind, b, out):
        self.h, self.kind, self.b, self.out = h, kind, b, out
        fox = kind == "fox"
        self.key_blocks = 4 * (b + 1) if fox else N_MEM // P
        self.groups = []
        for r in range(4):
            keys = (4 * b + r + 1) * P if fox else N_MEM
            self.groups += [(r, k0, min(512, keys - k0)) for k0 in range(0, keys, 512)]
        self.tops = len(self.groups) // 4

    def first_query(self, k):
        return max(0, k - 4 * self.b) * P if self.kind == "fox" else 0

    def diagonal(self, k):
        return self.kind == "fox" and k >= 4 * self.b


LEAD = 4
LAG = 1


def attention_schedule(blocks):
    steps = [(s, k) for s, b in enumerate(blocks) for k in range(b.key_blocks)]
    start = [steps.index((s, 0)) for s in range(len(blocks))]
    todo = [(s, n) for s, b in enumerate(blocks) for n in range(len(b.groups))]
    width = [blocks[s].groups[n][2] for s, n in todo]
    total = [sum(len(b.groups) for b in blocks[:s + 1]) for s in range(len(blocks))]
    order, done, rows = [], 0, 0

    def maximum():
        nonlocal done
        s, n = todo[done]
        order.append(("max", s, n))
        done += 1

    def turn_rows():
        nonlocal rows
        while rows < len(blocks) and total[rows] <= done:
            order.append(("row", rows))
            rows += 1

    def value(v):
        order.append(("value",) + steps[v])
        if v + 1 == len(steps) or steps[v + 1][1] == 0:
            order.append(("copy", steps[v][0]))
        if v and steps[v][1] == 0:
            order.append(("turn", steps[v][0] - 1))

    while done < total[0]:
        maximum()
    turn_rows()
    for g in range(2):
        order.append(("keys",) + steps[g])
    order += [("low",) + steps[0], ("split", 0)]
    debt = 0
    for g in range(len(steps)):
        debt += max((sum(width[done:total[s]]) - debt) / (max(start[s] - LEAD, g) - g + 1)
                    for s in range(len(blocks))) if done < len(todo) else 0
        ready = rows < len(blocks) and total[rows] <= done
        if ready and g + 2 < len(steps) and steps[g + 2][0] == rows and steps[g + 2][1] == 0:
            turn_rows()
            ready = False
        if g + 2 < len(steps):
            order.append(("keys",) + steps[g + 2])
        if g + 2 + LEAD == start[len(blocks) // 2]:
            order.append(("split", len(blocks) // 2))
        if ready:
            turn_rows()
        must = max([total[s] for s in range(len(blocks)) if start[s] - LEAD <= g], default=0)
        while done < len(todo) and (done < must or debt >= width[done]):
            debt = max(0, debt - width[done])
            maximum()
        if g - LAG >= 2 and steps[g - LAG - 1][1] == 0:
            order.append(("norm", steps[g - LAG - 2][0]))
        if g + 1 < len(steps):
            order.append(("low",) + steps[g + 1])
        if g >= LAG:
            value(g - LAG)
    for v in range(len(steps) - LAG, len(steps)):
        value(v)
    last = len(blocks) - 1
    return order + [("turn", last), ("norm", last)]


def prompt_attention(nc, K, D):
    NPAIR = FOX_HEADS // 2
    MQ = SEQ // 2
    PB = 8
    blocks = [Block512(h, kind, b, out) for h in range(2) for kind, b, out in
              (("fox", 0, 0), ("fox", 1, 1), ("mem", 0, 4), ("fox", 2, 2), ("mem", 1, 5), ("fox", 3, 3))]
    order = attention_schedule(blocks)
    BLOCKS, HALF = len(blocks), len(blocks) // 2
    numbers = {e: m for m, e in enumerate(e for e in order if e[0] in ("max", "row"))}
    NMAX = len(numbers)
    STEPS = sum(b.key_blocks for b in blocks)
    step0 = [sum(b.key_blocks for b in blocks[:s]) for s in range(BLOCKS)]
    assert NMAX % 2 == 0 and STEPS % PB == 0
    ROW_C, ROW_MAX = HD, 96

    with ExitStack() as stack:
        a = Place(nc, stack, "attn")
        qa = [a.sb(f"qa{h}", [P, SEQ], F32R) for h in range(2)]
        qb = [a.sb(f"qb{h}", [ROW_MAX + 1, SEQ], F32R) for h in range(2)]
        ka = [a.sb(f"ka{h}", [P, SEQ], F32R) for h in range(2)]
        kb = [a.sb(f"kb{h}", [ROW_MAX + 1, SEQ], F32R) for h in range(2)]
        v = [a.sb(f"v{h}", [P, PROMPT_TILES, HD + 1]) for h in range(2)]
        mqa = [a.sb(f"mqa{h}", [P, MQ], F32R) for h in range(2)]
        mqb = [a.sb(f"mqb{h}", [HD + 1, MQ], F32R) for h in range(2)]
        mka = [a.sb(f"mka{h}", [P, N_MEM], F32R) for h in range(2)]
        mkb = [a.sb(f"mkb{h}", [HD + 1, N_MEM], F32R) for h in range(2)]
        mv = [a.sb(f"mv{h}", [P, N_MEM // P, HD + 1]) for h in range(2)]
        vh, vl = ([a.sb(f"{k}{h}", [P, PROMPT_TILES, HD + 1], F32R) for h in range(2)] for k in ("vh", "vl"))
        mvh, mvl = ([a.sb(f"{k}{h}", [P, N_MEM // P, HD + 1], F32R) for h in range(2)] for k in ("mvh", "mvl"))
        probs = a.sb("probs", [P, PB, 512])
        probs_h, probs_l = (a.sb(k, [P, PB, 512], F32R) for k in ("probs_h", "probs_l"))
        tops, negmax = a.sb("tops", [P, 2, 16]), a.sb("negmax", [P, 2, 4])
        rden = a.sb("rden", [P, 2, 4])
        out = a.sb("out", [P, 2, HALF, 4, HD])
        turned = a.sb("turned", [HD + 1, 512])
        m_ps = [a.ps(f"sm{i}", [P, 512]) for i in range(2)]
        k_ps = [a.ps(f"sk{i}", [P, 512]) for i in range(3)]
        v_ps = [a.ps(f"pv{i}", [HD + 1, 512]) for i in range(2)]
        o_ps = a.ps("o", [P, 4, HD + 1])
        s_zero, s_fill, s_load = a.sem("zero"), [a.sem(f"fill{h}") for h in range(2)], [a.sem(f"load{h}") for h in range(2)]
        s_max, s_top, s_negmax = a.sem("maxscores"), a.sem("top"), a.sem("negmax")
        s_keys, s_exp, s_value, s_rden, s_norm = (a.sem(k) for k in ("keyscores", "exp", "value", "rden", "norm"))
        s_vh, s_vl, s_low = a.sem("values_hi"), a.sem("values_lo"), a.sem("low")
        s_copy, s_back = a.sem("out_copied"), a.sem("out_turned")
        s_store = [a.sem(f"stored{h}") for h in range(2)]
        s_vload = [a.sem(f"values_loaded{h}") for h in range(2)]
        LOADS, VLOADS, STORES, FILLS = 6, 7, 2, 6
        block = stack.enter_context(nc.Block())

        def own(i, n, each):
            return i * each + (max(n, 0) + 1)

        @block.sync
        def _(sp):
            with sp.Fori(0, NPAIR) as i:
                for h in range(2):
                    head = i * 2 + h

                    def load(dst, src):
                        sp.dma_start(dst, src).then_inc(s_load[h], 16)

                    def vload(dst, src):
                        sp.dma_start(dst, src).then_inc(s_vload[h], 16)

                    def row(x, lo, hi):
                        return x[bass.ds(head, 1), lo:hi, 0:SEQ].rearrange("o p t -> (o p) t")

                    def mem_row(x, lo, hi, at, n):
                        return x[bass.ds(i, 1), lo:hi, at:at + n].rearrange("o p t -> (o p) t")

                    sp.wait_ge(s_norm, i * BLOCKS + (1 + h * HALF))
                    load(fl(qa[h][:, :]), row(D.q, 0, P))
                    load(fl(ka[h][0:HD, :]), row(D.k, 0, HD))
                    load(fl(ka[h][HD:P, :]), row(D.k, 0, HD))
                    load(fl(qb[h][0:HD, :]), row(D.q, 0, HD))
                    load(fl(kb[h][0:HD, :]), row(D.k, HD, P))
                    sp.wait_ge(s_fill[h], FILLS)
                    load(fl(kb[h][ROW_C:ROW_C + 2, :]), row(D.decay, 0, 2))
                    vload(v[h][:, :, 0:HD], D.o_v[:, bass.ds(head * HD, HD)].rearrange("(k p) d -> p k d", p=P))
                    vload(fl(mqa[h][:, :]), mem_row(D.mq, 0, P, h * MQ, MQ))
                    vload(fl(mqb[h][0:HD, :]), mem_row(D.mq, 0, HD, h * MQ, MQ))
                    vload(fl(mka[h][0:HD, :]), mem_row(D.mk, 0, HD, 0, N_MEM))
                    vload(fl(mka[h][HD:P, :]), mem_row(D.mk, 0, HD, 0, N_MEM))
                    vload(fl(mkb[h][0:HD, :]), mem_row(D.mk, HD, P, 0, N_MEM))
                    vload(mv[h][:, :, 0:HD], D.o_mv[:, bass.ds(i * HD, HD)].rearrange("(k p) d -> p k d", p=P))

        @block.tensor
        def _(pe):
            for s in (s_keys, s_value, s_max, s_back):
                pe.sem_inc(s, 1)
            with pe.Fori(0, NPAIR) as i:
                for what, s, *n in order:
                    b = blocks[s]
                    fox, h = b.kind == "fox", b.h
                    q0 = b.b * 512
                    if what == "max":
                        r, k0, width = b.groups[n[0]]
                        m = numbers[what, s, n[0]]
                        bank, q = m_ps[m % 2], slice(q0 + r * P, q0 + (r + 1) * P)
                        if n[0] == 0 and s % HALF == 0:
                            pe.wait_ge(s_fill[h], FILLS)
                            pe.wait_ge(s_load[h], (i + 1) * (16 * LOADS))
                        if n[0] == 0 and s % HALF == 2:
                            pe.wait_ge(s_vload[h], (i + 1) * (16 * VLOADS))
                        pe.wait_ge(s_top, own(i, m - 1, NMAX))
                        if fox:
                            nc.tensor.matmul(bank[:, 0:width], qa[h][:, q], ka[h][:, k0:k0 + width], start=True, stop=False)
                            if k0 + width == q.stop:
                                nc.tensor.matmul(bank[:, width - P:width], K.identb[:, :], K.causal[:, :],
                                                 start=False, stop=False)
                            nc.tensor.matmul(bank[:, 0:width], qb[h][0:ROW_C + 2, q], kb[h][0:ROW_C + 2, k0:k0 + width],
                                             start=False, stop=True).then_inc(s_max, 1)
                        else:
                            nc.tensor.matmul(bank[:, 0:width], mqa[h][:, q], mka[h][:, 0:width], start=True, stop=False)
                            nc.tensor.matmul(bank[:, 0:width], mqb[h][0:HD, q], mkb[h][0:HD, 0:width],
                                             start=False, stop=True).then_inc(s_max, 1)
                    if what == "row":
                        m = numbers[what, s]
                        pe.wait_ge(s_negmax, own(i, s + 1, BLOCKS))
                        pe.wait_ge(s_top, own(i, m - 1, NMAX))
                        for r in range(4):
                            last = nc.tensor.transpose(m_ps[m % 2][0:1, r * P:(r + 1) * P], negmax[:, s % 2, r:r + 1],
                                                       K.ident[:, :])
                        last.then_inc(s_max, 1)
                    if what == "keys":
                        k, g = n[0], step0[s] + n[0]
                        at = b.first_query(k)
                        bank, keys, q = k_ps[g % 3], slice(k * P, (k + 1) * P), slice(q0 + at, q0 + 512)
                        if k == 0:
                            pe.wait_ge(s_top, own(i, numbers["row", s] + 1, NMAX))
                        pe.wait_ge(s_exp, own(i, 2 * (g - 2), 2 * STEPS))
                        if fox:
                            nc.tensor.matmul(bank[:, at:512], ka[h][:, keys], qa[h][:, q], start=True, stop=False)
                            if b.diagonal(k):
                                nc.tensor.matmul(bank[:, at:at + P], K.causal[:, :], K.identb[:, :], start=False, stop=False)
                            nc.tensor.matmul(bank[:, at:512], kb[h][:, keys], qb[h][:, q],
                                             start=False, stop=True).then_inc(s_keys, 1)
                        else:
                            nc.tensor.matmul(bank[:, :], mka[h][:, keys], mqa[h][:, q], start=True, stop=False)
                            nc.tensor.matmul(bank[:, :], mkb[h][:, keys], mqb[h][:, q],
                                             start=False, stop=True).then_inc(s_keys, 1)
                    if what == "value":
                        k, g = n[0], step0[s] + n[0]
                        pe.wait_ge(s_low, own(i, g + 1, STEPS))
                        if k == 0 and s % HALF == 0:
                            pe.wait_ge(s_vl, own(i, 2 * (h + 1), 4))
                        if k == 0:
                            pe.wait_ge(s_copy, own(i, s - 1, BLOCKS))
                        at = b.first_query(k)
                        hi, lo = (vh[h], vl[h]) if fox else (mvh[h], mvl[h])
                        for j, (vals, part) in enumerate(((hi, probs_h), (hi, probs_l), (lo, probs_h))):
                            last = nc.tensor.matmul(v_ps[s % 2][:, at:512], vals[:, k, :], part[:, g % PB, at:512],
                                                    start=(k == 0 and j == 0), stop=(k == b.key_blocks - 1 and j == 2))
                        last.then_inc(s_value, 1)
                    if what == "turn":
                        pe.wait_ge(s_copy, own(i, s + 1, BLOCKS))
                        pe.wait_ge(s_norm, own(i, s, BLOCKS) + HALF)
                        for r in range(4):
                            last = nc.tensor.transpose(o_ps[:, r, :], turned[:, r * P:(r + 1) * P], K.ident[0:HD + 1, 0:HD + 1])
                        last.then_inc(s_back, 1)

        @block.scalar
        def _(act):
            act.sem_inc(s_exp, 1)
            act.sem_inc(s_copy, 1)
            act.sem_inc(s_vh, 1)
            for h in range(2):
                act.sem_inc(s_store[h], 16 * STORES)
            with act.Fori(0, NPAIR) as i:

                def store(h):
                    head = i * 2 + h
                    act.wait_ge(s_norm, own(i, (h + 1) * HALF, BLOCKS) + HALF)
                    act.dma_start(D.fox[0:SEQ, bass.ds(head * HD, HD)].rearrange("(t p) d -> p t d", p=P),
                                  out[:, h, 0:4, :, :].rearrange("p b t d -> p (b t) d")).then_inc(s_store[h], 16)
                    act.dma_start(D.mem[h * MQ:(h + 1) * MQ, bass.ds(i * HD, HD)].rearrange("(t p) d -> p t d", p=P),
                                  out[:, h, 4:6, :, :].rearrange("p b t d -> p (b t) d")).then_inc(s_store[h], 16)

                for what, s, *n in order:
                    if what == "copy":
                        act.wait_ge(s_value, own(i, step0[s] + blocks[s].key_blocks, STEPS))
                        act.wait_ge(s_back, own(i, s, BLOCKS))
                        nc.scalar.activation(turned[:, :], v_ps[s % 2][:, :], ACT.Copy).then_inc(s_copy, 1)
                    if what == "split":
                        h = blocks[s].h
                        act.wait_ge(s_vload[h], (i + 1) * (16 * VLOADS))
                        nc.scalar.activation(vh[h][:, :, :], v[h][:, :, :], ACT.Copy).then_inc(s_vh, 1)
                        nc.scalar.activation(mvh[h][:, :, :], mv[h][:, :, :], ACT.Copy).then_inc(s_vh, 1)
                    if what != "keys":
                        continue
                    g, at = step0[s] + n[0], blocks[s].first_query(n[0])
                    act.wait_ge(s_keys, own(i, g + 1, STEPS))
                    act.wait_ge(s_low, own(i, g - PB + 1, STEPS))
                    nc.scalar.activation(probs[:, g % PB, at:512], k_ps[g % 3][:, at:512], ACT.Exp).then_inc(s_exp, 1)
                    act.wait_ge(s_value, own(i, g - PB + 1, STEPS))
                    nc.scalar.activation(probs_h[:, g % PB, at:512], k_ps[g % 3][:, at:512], ACT.Exp).then_inc(s_exp, 1)
                    if s == HALF + 1 and n[0] == 4:
                        store(0)
                store(1)
            for h in range(2):
                act.wait_ge(s_store[h], 16 * STORES * (1 + NPAIR))

        @block.gpsimd
        def _(pool):
            for h in range(2):
                nc.gpsimd.memset(fl(kb[h][ROW_C:ROW_MAX, :]), 0.0).then_inc(s_fill[h], 1)
                nc.gpsimd.memset(fl(kb[h][ROW_MAX:ROW_MAX + 1, :]), 1.0).then_inc(s_fill[h], 1)
                nc.gpsimd.memset(fl(mkb[h][HD:HD + 1, :]), 1.0).then_inc(s_fill[h], 1)
            pool.sem_inc(s_vl, 1)
            for h in range(2):
                pool.wait_ge(s_fill[h], FILLS)
            with pool.Fori(0, NPAIR) as i:
                for h in range(2):
                    for j, (x, hi, lo) in enumerate(((v, vh, vl), (mv, mvh, mvl))):
                        pool.wait_ge(s_vl, own(i, 2 * h + j, 4))
                        pool.wait_ge(s_vh, own(i, 2 * h + j + 1, 4))
                        nc.gpsimd.tensor_tensor(lo[h][:, :, :], x[h][:, :, :], fl(hi[h][:, :, :]),
                                                ALU.subtract).then_inc(s_vl, 1)

        @block.vector
        def _(dve):
            for h in range(2):
                nc.vector.memset(fl(qb[h][ROW_C:ROW_MAX, :]), 0.0).then_inc(s_zero, 1)
                dve.wait_ge(s_zero, h + 1)
                nc.vector.memset(fl(qb[h][ROW_C:ROW_C + 2, :]), 1.0).then_inc(s_fill[h], 1)
                nc.vector.memset(v[h][:, :, HD:HD + 1], 1.0).then_inc(s_fill[h], 1)
                nc.vector.memset(mv[h][:, :, HD:HD + 1], 1.0).then_inc(s_fill[h], 1)
            for s in (s_top, s_negmax, s_rden, s_low):
                dve.sem_inc(s, 1)
            dve.sem_inc(s_norm, 1 + HALF)
            with dve.Fori(0, NPAIR) as i:
                for what, s, *n in order:
                    b = blocks[s]
                    if what == "max":
                        r, k0, width = b.groups[n[0]]
                        m = numbers[what, s, n[0]]
                        top = tops[:, s % 2, n[0]:n[0] + 1]
                        if n[0] == 0:
                            dve.wait_ge(s_negmax, own(i, s - 1, BLOCKS))
                        dve.wait_ge(s_max, own(i, m + 1, NMAX))
                        nc.vector.tensor_reduce(top, m_ps[m % 2][:, 0:width], AX.X, ALU.max).then_inc(s_top, 1)
                        if n[0] == len(b.groups) - 1:
                            dve.wait_ge(s_top, own(i, m + 1, NMAX))
                            if s >= 2:
                                dve.wait_ge(s_max, own(i, numbers["row", s - 2] + 1, NMAX))
                            nc.vector.tensor_reduce(negmax[:, s % 2, :],
                                                    tops[:, s % 2, 0:4 * b.tops].rearrange("p (r n) -> p r n", n=b.tops),
                                                    AX.X, ALU.max, negate=True).then_inc(s_negmax, 1)
                    if what == "low":
                        g, at = step0[s] + n[0], b.first_query(n[0])
                        dve.wait_ge(s_exp, own(i, 2 * g + 2, 2 * STEPS))
                        dve.wait_ge(s_value, own(i, g - PB + 1, STEPS))
                        nc.vector.tensor_tensor(probs_l[:, g % PB, at:512], probs[:, g % PB, at:512],
                                                fl(probs_h[:, g % PB, at:512]), ALU.subtract).then_inc(s_low, 1)
                    if what == "row":
                        m = numbers[what, s]
                        dve.wait_ge(s_max, own(i, m + 1, NMAX))
                        q = slice(b.b * 512, (b.b + 1) * 512)
                        row = qb[b.h][ROW_MAX:ROW_MAX + 1, q] if b.kind == "fox" else mqb[b.h][HD:HD + 1, q]
                        nc.vector.tensor_copy(row, m_ps[m % 2][0:1, :]).then_inc(s_top, 1)
                    if what == "norm":
                        dve.wait_ge(s_back, own(i, s + 1, BLOCKS))
                        dve.wait_ge(s_norm, own(i, s - 1, BLOCKS) + HALF)
                        nc.vector.reciprocal(rden[:, s % 2, :], o_ps[:, :, HD]).then_inc(s_rden, 1)
                        dve.wait_ge(s_rden, own(i, s + 1, BLOCKS))
                        if s % HALF == 0:
                            dve.wait_ge(s_store[b.h], (i + 1) * (16 * STORES))
                        nc.vector.tensor_tensor(out[:, b.h, b.out, :, :], o_ps[:, :, 0:HD],
                                                rden[:, s % 2, :, None].to_broadcast([P, 4, HD]), ALU.mult).then_inc(s_norm, 1)


def sample_attention(nc, K, D, w_out):
    B, T = DEC_BATCH, DEC_SEQ
    KT = PAST // P
    HP, MP = FOX_HEADS // 2, MEM_HEADS // 2
    MROWS = MEM_HEADS * T
    KEYS = PAST + T
    with ExitStack() as stack:
        a = Place(nc, stack, "smp")
        qn, kn, mqn = a.sb("qn", [P, FOX]), a.sb("kn", [P, FOX]), a.sb("mqn", [P, MEM])
        qt, knt, mqt = a.sb("qt", [P, HP, P]), a.sb("knt", [P, HP, P]), a.sb("mqt", [P, MP, P])
        qblk = [a.sb(f"qblk{u}", [P, 32 + HP * (P + 32)]) for u in range(2)]
        mqblk = [a.sb(f"mqblk{u}", [P, 32 + MP * (MROWS + 32)]) for u in range(2)]
        kc, vc = a.sb("kc", [P, 2, KT, FOX]), a.sb("vc", [P, 2, KT, FOX])
        mk, mv = a.sb("mk", [P, 2, N_MEM // P, MEM]), a.sb("mv", [P, 2, N_MEM // P, MEM])
        vn, dec = a.sb("vn", [P, 2, FOX]), a.sb("dec", [P, 2, KEYS])
        kt, mkt = a.sb("kt", [P, 2, HP, PAST]), a.sb("mkt", [P, 2, MP, N_MEM])
        sel, rep = a.sb("sel", [P, FOX_HEADS, T]), a.sb("rep", [P, FOX_HEADS, T], BF16)
        top, negmax, den, rden = (a.sb(k, [P, 2]) for k in ("top", "negmax", "den", "rden"))
        mneg, mden, mrden = (a.sb(k, [MROWS, 2]) for k in ("mneg", "mden", "mrden"))
        probs, mprobs = a.sb("probs", [P, KEYS]), a.sb("mprobs", [MROWS, N_MEM])
        pt, ptn, mpt = a.sb("pt", [P, KT, P]), a.sb("ptn", [P, P]), a.sb("mpt", [P, 2, MROWS])
        out, mout = a.sb("out", [P, 2, FOX]), a.sb("mout", [MROWS, 2, MEM])
        t_ps = [a.ps(f"t{i}", [P, 512]) for i in range(2)]
        p_ps, s_ps, n_ps, m_ps, o_ps, mo_ps = (a.ps(k, [P, 512]) for k in ("p", "s", "n", "m", "o", "mo"))
        wide, mwide = D.wide, D.mwide
        (s_q, s_turn0, s_qt, s_zero, s_sel, s_blk, s_turn, s_score, s_top, s_neg, s_exp, s_mexp, s_den, s_rden, s_pturn,
         s_pread, s_pread2, s_pv, s_out, s_mout, s_gather) = (a.sem(k) for k in (
             "q turn0 qt zero sel blk turn score top neg exp mexp den rden pturn pread pread2 pv out mout gather").split())
        s_w, s_wh, s_wl = [a.sem(f"w{c}") for c in range(KC)], a.sem("w_hi"), a.sem("w_lo")
        s_load = [a.sem(f"load{u}") for u in range(2)]
        s_store = [a.sem(f"store{u}") for u in range(2)]
        s_read = [a.sem("read_dve"), a.sem("read_act")]
        s_kload = [a.sem(f"kload{u}") for u in range(2)]
        KLOADS, LOADS = 2, 4
        block = stack.enter_context(nc.Block())

        def streams(eng, body):
            for b in range(2):
                body(b, b, 0)
            with eng.Fori(1, B // 2 - 1) as i:
                for u in range(2):
                    body(i * 2 + u, u, i)
            for b in range(B - 2, B):
                body(b, b % 2, b // 2)

        def fills(b, u, i):
            return [(f, (5 * u + f) % 2, i * 5 + (5 * u + f) // 2) for f in range(5)]

        @block.sync
        def _(sp):
            sp.dma_start(qn[:, :], D.q_s).then_inc(s_q, 16)
            sp.dma_start(kn[:, :], D.o_k_s).then_inc(s_q, 16)
            sp.dma_start(mqn[:, :], D.mq_s).then_inc(s_q, 16)
            for u in range(2):
                sp.sem_inc(s_store[u], 32)
            sp.dma_start(kc[:, 0, :, :], D.cache_k[0, :, :].rearrange("(k p) c -> p k c", p=P)).then_inc(s_kload[0], 16)
            sp.dma_start(mk[:, 0, :, :], D.cache_mk[0, :, :].rearrange("(k p) c -> p k c", p=P)).then_inc(s_kload[0], 16)
            sp.wait_ge(s_zero, 1)

            def one_of(b):
                return slice(b, b + 1) if isinstance(b, int) else bass.ds(b, 1)

            def load_keys(b, u):
                sp.dma_start(kc[:, u, :, :], D.cache_k[one_of(b), :, :].rearrange("o (k p) c -> p (o k) c", p=P))\
                    .then_inc(s_kload[u], 16)
                sp.dma_start(mk[:, u, :, :], D.cache_mk[one_of(b), :, :].rearrange("o (k p) c -> p (o k) c", p=P))\
                    .then_inc(s_kload[u], 16)

            def load(b, u):
                def one(dst, src):
                    sp.dma_start(dst, src).then_inc(s_load[u], 16)
                bb = one_of(b)
                one(dec[0:FOX_HEADS, u, :], D.decay_s[bb, :, :].rearrange("o h c -> (o h) c"))
                one(vc[:, u, :, :], D.cache_v[bb, :, :].rearrange("o (k p) c -> p (o k) c", p=P))
                one(mv[:, u, :, :], D.cache_mv[bb, :, :].rearrange("o (k p) c -> p (o k) c", p=P))
                one(vn[0:T, u, :], D.o_v_s.rearrange("(b t) c -> b t c", t=T)[bb, :, :].rearrange("o t c -> (o t) c"))

            load_keys(1, 1)
            load(0, 0)
            load(1, 1)
            for c in range(KC):
                sp.dma_start(K.w_raw[:, c, :], w_out[c * P:(c + 1) * P, :]).then_inc(s_w[c], 16)

            def body(b, u, i):
                bb = one_of(b)
                if not isinstance(b, int) or b + 2 < B:
                    sp.wait_ge(s_turn, b * 5 + 5)
                    load_keys(b + 2, u)
                sp.wait_ge(s_out, b + 2)
                sp.dma_start(wide[bb, :, :].rearrange("o r c -> (o r) c"), out[:, u, :]).then_inc(s_store[u], 16)
                sp.wait_ge(s_mout, b + 2)
                sp.dma_start(mwide[bb, :, :].rearrange("o r c -> (o r) c"), mout[:, u, :]).then_inc(s_store[u], 16)
                if not isinstance(b, int) or b + 2 < B:
                    load(b + 2, u)

            streams(sp, body)
            for u in range(2):
                sp.wait_ge(s_store[u], 32 * (1 + B // 2))
            for h in range(FOX_HEADS):
                sp.dma_start(D.fox[SEQ:, h * HD:(h + 1) * HD].rearrange("(b t) d -> b t d", t=T),
                             wide[:, h * T:(h + 1) * T, h * HD:(h + 1) * HD]).then_inc(s_gather, 16)
            for h in range(MEM_HEADS):
                sp.dma_start(D.mem[SEQ:, h * HD:(h + 1) * HD].rearrange("(b t) d -> b t d", t=T),
                             mwide[:, h * T:(h + 1) * T, h * HD:(h + 1) * HD]).then_inc(s_gather, 16)
            sp.wait_ge(s_gather, 16 * (FOX_HEADS + MEM_HEADS))

        @block.gpsimd
        def _(pool):
            nc.gpsimd.memset(sel[:, :, :], 0.0).then_inc(s_sel, 1)
            nc.gpsimd.memset(rep[:, :, :], 0.0).then_inc(s_sel, 1)
            pool.wait_ge(s_sel, 2)
            nc.gpsimd.affine_select(out=sel[:, :, :], in_=sel[:, :, :], compare_op=ALU.not_equal, fill=1.0, base=0,
                                    pattern=[[-1, FOX_HEADS], [0, T]], channel_multiplier=1).then_inc(s_sel, 1)
            nc.gpsimd.affine_select(out=rep[:, :, :], in_=rep[:, :, :], compare_op=ALU.not_equal, fill=1.0, base=0,
                                    pattern=[[0, FOX_HEADS], [-1, T]], channel_multiplier=1).then_inc(s_sel, 1)

        @block.tensor
        def _(pe):
            X = nc.tensor
            pe.wait_ge(s_q, 48)
            for dst, src, n in ((s_ps, qn, HP), (n_ps, kn, HP), (m_ps, mqn, MP)):
                for j in range(n):
                    last = X.transpose(dst[:, j * P:(j + 1) * P], src[:, j * P:(j + 1) * P], K.ident[:, :])
            last.then_inc(s_turn0, 1)
            pe.wait_ge(s_sel, 4)
            pe.wait_ge(s_zero, 1)
            pe.wait_ge(s_qt, 3)

            def turn_keys(b, u, i):
                pe.wait_ge(s_kload[u], (i + 1) * (16 * KLOADS))
                for f, bank, before in fills(b, u, i):
                    pe.wait_ge(s_read[bank], before + 1)
                    for j in range(4):
                        src = (kc[:, u, j, f * P:(f + 1) * P] if f < HP else mk[:, u, j % 2, (j // 2) * P:(j // 2 + 1) * P])
                        last = X.transpose(t_ps[bank][:, j * P:(j + 1) * P], src, K.ident[:, :])
                    last.then_inc(s_turn, 1)

            def body(b, u, i):
                pe.wait_ge(s_load[u], (i + 1) * (16 * LOADS))
                for bank in range(2):
                    pe.wait_ge(s_read[bank], i * 5 + ((5 * (u + 1) + 1 - bank) // 2 + 1))
                pe.wait_ge(s_blk, b + 1)
                pe.wait_ge(s_exp, b * 2 + 1)
                pe.wait_ge(s_mexp, b + 1)
                q = [qblk[u][:, h * P:(h + 1) * P] for h in range(HP)]
                sel_h = sel[:, :, :].rearrange("p h t -> p (h t)")
                for h in range(HP):
                    X.matmul(s_ps[:, 0:PAST], q[h], kt[:, u, h, :], start=h == 0, stop=False)
                X.matmul(s_ps[:, 0:PAST], sel_h, dec[:, u, 0:PAST], start=False, stop=True).then_inc(s_score, 1)
                for h in range(HP):
                    X.matmul(n_ps[:, 0:T], q[h], knt[:, h, bass.ts(b, T)], start=h == 0, stop=False)
                X.matmul(n_ps[:, 0:T], rep[:, :, :].rearrange("p h t -> p (h t)"), K.causal[:, 0:T],
                         start=False, stop=False)
                X.matmul(n_ps[:, 0:T], sel_h, dec[:, u, PAST:KEYS], start=False, stop=True).then_inc(s_score, 1)
                for h in range(MP):
                    last = X.matmul(m_ps[0:MROWS, 0:N_MEM], mqblk[u][:, h * MROWS:(h + 1) * MROWS], mkt[:, u, h, :],
                                    start=h == 0, stop=h == MP - 1)
                last.then_inc(s_score, 1)
                if not isinstance(b, int) or b + 1 < B:
                    turn_keys(b + 1, 1 - u, i + u)
                pe.wait_ge(s_exp, b * 2 + 3)
                pe.wait_ge(s_pread2, b * 2 + 1)
                for j in range(KT):
                    last = X.transpose(p_ps[:, j * P:(j + 1) * P], probs[:, j * P:(j + 1) * P], K.ident[:, :])
                last.then_inc(s_pturn, 1)
                pe.wait_ge(s_mexp, b + 2)
                pe.wait_ge(s_pread, b + 2)
                X.transpose(p_ps[0:T, 0:P], probs[:, PAST:KEYS], K.ident[:, :])
                for j in range(2):
                    last = X.transpose(p_ps[:, P + j * MROWS:P + (j + 1) * MROWS], mprobs[:, j * P:(j + 1) * P],
                                       K.ident[0:MROWS, 0:MROWS])
                last.then_inc(s_pturn, 1)
                pe.wait_ge(s_mout, b + 1)
                pe.wait_ge(s_out, b + 1)
                for j in range(KT):
                    X.matmul(o_ps[:, :], pt[:, j, :], vc[:, u, j, :], start=j == 0, stop=False)
                pe.wait_ge(s_pread2, b * 2 + 3)
                X.matmul(o_ps[:, :], ptn[:, :], vn[:, u, :], start=False, stop=True).then_inc(s_pv, 1)
                for j in range(2):
                    last = X.matmul(mo_ps[0:MROWS, 0:MEM], mpt[:, j, :], mv[:, u, j, :], start=j == 0, stop=j == 1)
                last.then_inc(s_pv, 1)

            turn_keys(0, 0, 0)
            streams(pe, body)

        @block.scalar
        def _(act):
            act.sem_inc(s_read[1], 1)
            act.sem_inc(s_pread, 1)
            act.sem_inc(s_exp, 1)
            act.sem_inc(s_mexp, 1)
            act.sem_inc(s_out, 1)
            act.sem_inc(s_mout, 1)

            def keys(b, u, i):
                for f, bank, before in fills(b, u, i):
                    if bank == 1:
                        act.wait_ge(s_turn, b * 5 + (f + 1))
                        dst = kt[:, u, f, :] if f < HP else mkt[:, u, :, :].rearrange("p h k -> p (h k)")
                        nc.scalar.activation(dst, t_ps[1][:, :], ACT.Copy).then_inc(s_read[1], 1)

            def body(b, u, i):
                act.wait_ge(s_neg, b * 2 + 1)
                act.wait_ge(s_pturn, b * 2)
                nc.scalar.activation(probs[:, 0:PAST], s_ps[:, 0:PAST], ACT.Exp, bias=negmax[:, u:u + 1])
                nc.scalar.activation(probs[:, PAST:KEYS], n_ps[:, 0:T], ACT.Exp, bias=negmax[:, u:u + 1]).then_inc(s_exp, 2)
                act.wait_ge(s_neg, b * 2 + 2)
                nc.scalar.activation(mprobs[:, :], m_ps[0:MROWS, 0:N_MEM], ACT.Exp, bias=mneg[:, u:u + 1]).then_inc(s_mexp, 1)
                if not isinstance(b, int) or b + 1 < B:
                    keys(b + 1, 1 - u, i + u)
                act.wait_ge(s_pturn, b * 2 + 1)
                nc.scalar.activation(pt[:, :, :].rearrange("p k q -> p (k q)"), p_ps[:, :], ACT.Copy).then_inc(s_pread, 1)
                act.wait_ge(s_pv, b * 2 + 2)
                act.wait_ge(s_rden, b * 2 + 2)
                act.wait_ge(s_store[u], (i + 1) * 32)
                nc.scalar.activation(out[:, u, :], o_ps[:, :], ACT.Copy, scale=rden[:, u:u + 1]).then_inc(s_out, 1)
                nc.scalar.activation(mout[:, u, :], mo_ps[0:MROWS, 0:MEM], ACT.Copy,
                                     scale=mrden[:, u:u + 1]).then_inc(s_mout, 1)

            keys(0, 0, 0)
            streams(act, body)
            for c in range(KC):
                act.wait_ge(s_w[c], 16)
                nc.scalar.activation(K.w_hi[:, c, :], K.w_raw[:, c, :], ACT.Copy).then_inc(s_wh, 1)

        @block.vector
        def _(dve):
            V = nc.vector
            dve.sem_inc(s_read[0], 1)
            dve.sem_inc(s_pread2, 1)
            for t in (vn, dec, qblk[0], qblk[1], mqblk[0], mqblk[1], ptn):
                last = V.memset(t[tuple(slice(None) for _ in t.shape)], 0.0)
            last.then_inc(s_zero, 1)
            dve.wait_ge(s_turn0, 1)
            V.tensor_copy(qt[:, :, :].rearrange("p h t -> p (h t)"), s_ps[:, :]).then_inc(s_qt, 1)
            V.tensor_copy(knt[:, :, :].rearrange("p h t -> p (h t)"), n_ps[:, :]).then_inc(s_qt, 1)
            V.tensor_copy(mqt[:, :, :].rearrange("p h t -> p (h t)"), m_ps[:, 0:MP * P]).then_inc(s_qt, 1)
            dve.wait_ge(s_qt, 3)
            dve.wait_ge(s_zero, 1)

            def keys(b, u, i):
                for f, bank, before in fills(b, u, i):
                    if bank == 0:
                        dve.wait_ge(s_turn, b * 5 + (f + 1))
                        dst = kt[:, u, f, :] if f < HP else mkt[:, u, :, :].rearrange("p h k -> p (h k)")
                        V.tensor_copy(dst, t_ps[0][:, :]).then_inc(s_read[0], 1)

            def blocks(b, u):
                for r in range(2):
                    rows = slice(r * HD, (r + 1) * HD)
                    V.tensor_copy(qblk[u][rows, r * T:r * T + HP * (P + 32)].rearrange("p (h w) -> p h w", h=HP)[:, :, 0:T],
                                  qt[rows, :, bass.ts(b, T)])
                    last = V.tensor_copy(mqblk[u][rows, r * T:r * T + MP * (MROWS + 32)]
                                         .rearrange("p (h w) -> p h w", h=MP)[:, :, 0:T], mqt[rows, :, bass.ts(b, T)])
                last.then_inc(s_blk, 1)

            def body(b, u, i):
                dve.wait_ge(s_score, b * 3 + 1)
                V.tensor_reduce(top[:, 0:1], s_ps[:, 0:PAST], AX.X, ALU.max).then_inc(s_top, 1)
                dve.wait_ge(s_score, b * 3 + 2)
                V.tensor_reduce(top[:, 1:2], n_ps[:, 0:T], AX.X, ALU.max).then_inc(s_top, 1)
                dve.wait_ge(s_top, b * 2 + 2)
                V.tensor_reduce(negmax[:, u:u + 1], top[:, 0:2], AX.X, ALU.max, negate=True).then_inc(s_neg, 1)
                dve.wait_ge(s_score, b * 3 + 3)
                V.tensor_reduce(mneg[:, u:u + 1], m_ps[0:MROWS, 0:N_MEM], AX.X, ALU.max, negate=True).then_inc(s_neg, 1)
                if not isinstance(b, int) or b + 1 < B:
                    keys(b + 1, 1 - u, i + u)
                    blocks(b + 1, 1 - u)
                dve.wait_ge(s_exp, b * 2 + 3)
                V.tensor_reduce(den[:, u:u + 1], probs[:, :], AX.X, ALU.add).then_inc(s_den, 1)
                dve.wait_ge(s_mexp, b + 2)
                V.tensor_reduce(mden[:, u:u + 1], mprobs[:, :], AX.X, ALU.add).then_inc(s_den, 1)
                dve.wait_ge(s_den, b * 2 + 2)
                V.reciprocal(rden[:, u:u + 1], den[:, u:u + 1]).then_inc(s_rden, 1)
                V.reciprocal(mrden[:, u:u + 1], mden[:, u:u + 1]).then_inc(s_rden, 1)
                dve.wait_ge(s_pturn, b * 2 + 2)
                V.tensor_copy(ptn[0:T, :], p_ps[0:T, 0:P])
                V.tensor_copy(mpt[:, :, :].rearrange("p k q -> p (k q)"), p_ps[:, P:P + 2 * MROWS]).then_inc(s_pread2, 2)

            keys(0, 0, 0)
            blocks(0, 0)
            streams(dve, body)
            for c in range(KC):
                dve.wait_ge(s_wh, c + 1)
                V.tensor_tensor(K.w_lo[:, c, :], K.w_raw[:, c, :], fl(K.w_hi[:, c, :]), ALU.subtract).then_inc(s_wl, 1)


def output_phase(nc, K, D):
    KF, KS = FOX // P, SSM // P
    with ExitStack() as stack:
        a = Place(nc, stack, "out")
        x, ssm = a.sb("x", [P, 2, D_MODEL]), a.sb("ssm", [P, 2, KS, P])
        fox, mem = a.sb("fox", [P, 2, 2, FOX]), a.sb("mem", [P, 2, 2, MEM])
        mix = a.sb("mix", [P, 2, FOX + MEM])
        mh, ml = a.sb("mh", [P, 2, KC, P], F32R), a.sb("ml", [P, 2, KC, P], F32R)
        y = a.sb("y", [P, 2, D_MODEL])
        xt_ps = [a.ps(f"xt{i}", [P, 4, P]) for i in range(2)]
        y_ps = [a.ps(f"y{i}", [P, 512]) for i in range(2)]
        s_in, s_store = ([a.sem(f"{k}{i}") for i in range(2)] for k in ("in", "stored"))
        s_mix, s_xt, s_mh, s_ml = (a.sem(k) for k in ("mix", "turned", "mh", "ml"))
        s_g, s_y = ([a.sem(f"{k}{i}") for i in range(2)] for k in ("g", "y"))
        s_xin = [a.sem(f"x{i}") for i in range(2)]
        LOADS = 5
        block = stack.enter_context(nc.Block())
        PARTS = ((0, 4), (6, 8), (4, 6))

        def tiles(eng, body):
            for t in range(2):
                body(t, t)
            with eng.Fori(1, PROMPT_TILES // 2 - 1) as i:
                for u in range(2):
                    body(i * 2 + u, u)
            for t in range(PROMPT_TILES - 2, TILES):
                body(t, t % 2)

        def rows(array, sample, t):
            if isinstance(t, int) and t == PROMPT_TILES:
                return sample
            return array[bass.ts(t, P), :]

        @block.sync
        def _(sp):
            def load(t, u):
                def one(dst, src):
                    sp.dma_start(dst, src).then_inc(s_in[u], 16)
                one(fox[:, u, 0, :], D.fox[bass.ts(t, P), :])
                one(fox[:, u, 1, :], D.fox_gate[bass.ts(t, P), :])
                one(mem[:, u, 0, :], D.mem[bass.ts(t, P), :])
                one(mem[:, u, 1, :], D.mem_gate[bass.ts(t, P), :])
                one(ssm[:, u, :, :], D.ssm[:, bass.ts(t, P)].rearrange("(c p) t -> p c t", p=P))

            def load_x(t, u):
                sp.dma_start(x[:, u, :], rows(D.x, D.xs, t)).then_inc(s_xin[u], 16)

            for t in range(2):
                load(t, t)
                load_x(t, t)
            for u in range(2):
                sp.sem_inc(s_store[u], 16)

            def body(t, u):
                more = not isinstance(t, int) or t + 2 < TILES
                if more:
                    sp.wait_ge(s_ml, t * 3 + 3)
                    load(t + 2, u)
                for h in range(2):
                    sp.wait_ge(s_y[h], t + 1)
                sp.dma_start(rows(D.y, D.ys, t), y[:, u, :]).then_inc(s_store[u], 16)
                if more:
                    load_x(t + 2, u)

            tiles(sp, body)
            for u in range(2):
                sp.wait_ge(s_store[u], 16 * (1 + (TILES + 1 - u) // 2))

        @block.gpsimd
        def _(pool):
            def body(t, u):
                pool.wait_ge(s_in[u], (t - u) * (8 * LOADS) + 16 * LOADS)
                pool.wait_ge(s_xt, t * 2 + 2)
                nc.gpsimd.tensor_tensor(mix[:, u, 0:FOX], fox[:, u, 0, :], fox[:, u, 1, :], ALU.mult).then_inc(s_mix, 1)
                nc.gpsimd.tensor_tensor(mix[:, u, FOX:], mem[:, u, 0, :], mem[:, u, 1, :], ALU.mult).then_inc(s_mix, 1)

            tiles(pool, body)

        @block.tensor
        def _(pe):
            pe.sem_inc(s_xt, 4)

            def turn(t, u):
                pe.wait_ge(s_mix, t * 2 + 2)
                pe.wait_ge(s_ml, t * 3)
                for h, n in ((0, KF), (1, MEM // P)):
                    for c in range(n):
                        at = h * FOX + c * P
                        last = nc.tensor.transpose(xt_ps[h][:, c, :], mix[:, u, at:at + P], K.ident[:, :])
                    last.then_inc(s_xt, 1)

            def body(t, u):
                for h in range(2):
                    if h == 1 and not (isinstance(t, int) and t == TILES - 1):
                        turn(t + 1, 1 - u)
                    pe.wait_ge(s_ml, t * 3 + 3)
                    pe.wait_ge(s_y[h], t)
                    for c in range(KC):
                        for k, (ms, ws) in enumerate(((mh, K.w_hi), (ml, K.w_hi), (mh, K.w_lo))):
                            last = nc.tensor.matmul(y_ps[h][:, :], ms[:, u, c, :], ws[:, c, h * 512:(h + 1) * 512],
                                                    start=(c == 0 and k == 0), stop=(c == KC - 1 and k == 2))
                    last.then_inc(s_g[h], 1)

            turn(0, 0)
            tiles(pe, body)

        @block.scalar
        def _(act):
            def split(t, u):
                for k, (lo, hi) in enumerate(PARTS):
                    if k < 2:
                        act.wait_ge(s_xt, t * 2 + k + 5)
                        src = xt_ps[k][:, 0:hi - lo, :]
                    else:
                        act.wait_ge(s_in[u], (t - u) * (8 * LOADS) + 16 * LOADS)
                        src = ssm[:, u, :, :]
                    nc.scalar.activation(mh[:, u, lo:hi, :], src, ACT.Copy).then_inc(s_mh, 1)

            def body(t, u):
                if not (isinstance(t, int) and t == TILES - 1):
                    split(t + 1, 1 - u)

            split(0, 0)
            tiles(act, body)

        @block.vector
        def _(dve):
            def split(t, u):
                for k, (lo, hi) in enumerate(PARTS):
                    dve.wait_ge(s_mh, t * 3 + (k + 1))
                    src = xt_ps[k][:, 0:hi - lo, :] if k < 2 else ssm[:, u, :, :]
                    nc.vector.tensor_tensor(ml[:, u, lo:hi, :], src, fl(mh[:, u, lo:hi, :]), ALU.subtract).then_inc(s_ml, 1)

            def body(t, u):
                for h in range(2):
                    if h == 1 and not (isinstance(t, int) and t == TILES - 1):
                        split(t + 1, 1 - u)
                    dve.wait_ge(s_g[h], t + 1)
                    if h == 0:
                        dve.wait_ge(s_store[u], (t - u) * 8 + 16)
                        dve.wait_ge(s_xin[u], (t - u) * 8 + 16)
                    cols = slice(h * 512, (h + 1) * 512)
                    nc.vector.tensor_tensor(y[:, u, cols], y_ps[h][:, :], x[:, u, cols], ALU.add).then_inc(s_y[h], 1)

            split(0, 0)
            tiles(dve, body)


class Names:
    pass


def build(nc, I, O):
    K, D = Names(), Names()
    with ExitStack() as stack:
        a = Place(nc, stack, "all")

        def scratch(name, shape):
            return nc.dram_tensor("scratch_" + name, shape, F32).ap()

        D.q, D.k = scratch("q", (FOX_HEADS, P, TOKENS)), scratch("k", (FOX_HEADS, P, TOKENS))
        D.mq, D.mk = scratch("mq", (MEM_HEADS, P, TOKENS)), scratch("mk", (MEM_HEADS, P, N_MEM))
        D.q_s, D.mq_s = scratch("q_s", (P, FOX)), scratch("mq_s", (P, MEM))
        D.decay, D.decay_s = scratch("decay", (FOX_HEADS, 2, SEQ)), scratch("decay_s", (DEC_BATCH, FOX_HEADS, PAST + DEC_SEQ))
        D.fox_gate, D.mem_gate = scratch("fox_gate", (TOKENS, FOX)), scratch("mem_gate", (TOKENS, MEM))
        D.fox, D.mem = scratch("fox", (TOKENS, FOX)), scratch("mem", (TOKENS, MEM))
        D.wide, D.mwide = scratch("wide", (DEC_BATCH, P, FOX)), scratch("mwide", (DEC_BATCH, MEM_HEADS * DEC_SEQ, MEM))
        D.ssm = scratch("ssm", (SSM, TOKENS))
        D.ssm_in, D.ssm_out = scratch("ssm_in", (8, SSM, TOKENS // 8)), scratch("ssm_out", (8, SSM, TOKENS // 8))
        x, xs = I["x_prompt"].rearrange("b s d -> (b s) d"), I["x_sample"].rearrange("b s d -> (b s) d")
        D.x, D.xs = x, xs
        D.y = O["y_prompt"].rearrange("b s d -> (b s) d")
        D.ys = O["y_sample"].rearrange("b s d -> (b s) d")
        D.cache_k = I["cache_fox_k"][0].rearrange("b t h d -> b t (h d)")
        D.cache_v = I["cache_fox_v"][0].rearrange("b t h d -> b t (h d)")
        D.cache_mk = I["cache_mem_k"][0].rearrange("b t h d -> b t (h d)")
        D.cache_mv = I["cache_mem_v"][0].rearrange("b t h d -> b t (h d)")
        w_in, norm_g = I["w_in"][0], I["norm_g"][0]
        D.cache_logf = I["cache_fox_logf"][0]
        D.o_k = O["fox_k_prompt"].rearrange("l b t h d -> (l b t) (h d)")
        D.o_v = O["fox_v_prompt"].rearrange("l b t h d -> (l b t) (h d)")
        D.o_k_s = O["fox_k_sample"].rearrange("l b t h d -> (l b t) (h d)")
        D.o_v_s = O["fox_v_sample"].rearrange("l b t h d -> (l b t) (h d)")
        D.o_logf = O["fox_logf_prompt"].rearrange("l b t h -> (l b t) h")
        D.o_logf_s = O["fox_logf_sample"].rearrange("l b t h -> (l b t) h")
        D.o_mk = O["mem_k_prompt"].rearrange("l b t h d -> (l b t) (h d)")
        D.o_mv = O["mem_v_prompt"].rearrange("l b t h d -> (l b t) (h d)")

        def tile_rows(prompt, sample=None):
            def rows(t):
                if sample is not None and isinstance(t, int) and t == PROMPT_TILES:
                    return sample
                return prompt[bass.ts(t, P), :]
            return rows

        K.ident, K.identb, K.causal = a.sb("ident", [P, P]), a.sb("identb", [P, P], BF16), a.sb("causal", [P, P], BF16)
        K.neghalf, K.one = a.sb("neghalf", [P, FOX_HEADS]), a.sb("one", [P, 1])
        K.logits = a.sb("logits", [P, TILES * FOX_HEADS])
        constants_phase(nc, K)
        mem = I["mem_prompt"].rearrange("b s d -> (b s) d")
        project(nc, K, "m", [(mem, N_MEM // P)], [(0, 2 * MEM)], I["w_mem_kv"][0], I["mem_norm"][0],
                [[Piece("heads", MEM, nat=tile_rows(D.o_mk), gain=I["mem_k_norm"][0], scratch=D.mk),
                  Piece("plain", MEM, nat=tile_rows(D.o_mv))]],
                [("X",), ("G", 0), ("H", 0), ("T", 0)], 1)
        with ExitStack() as inner:
            b = Place(nc, inner, "s5io")
            K.su = b.sb("su", [P, 2, 8, TOKENS // 8])
            K.sg = b.sb("sg", [P, 2, 8, TOKENS // 8])
            project(nc, K, "g", [(x, PROMPT_TILES), (xs, 1)], [(C_MQ, 2 * MEM), (C_SU, 2 * SSM), (C_FG, FOX)],
                    w_in, norm_g,
                    [[Piece("heads", MEM, last=D.mq_s, gain=I["mem_q_norm"][0], scratch=D.mq, scale=HD ** -0.5),
                      Piece("gate", MEM, nat=tile_rows(D.mem_gate))],
                     [Piece("turned", 2 * SSM)],
                     [Piece("gate", FOX, nat=tile_rows(D.fox_gate))]],
                    [("G", 0), ("H", 0), ("G", 1), ("T", 0), ("X",), ("G", 2), ("T", 1)], 2)
            ssm_phase(nc, K, D, I, O)
        project(nc, K, "k", [(x, PROMPT_TILES), (xs, 1)], [(C_FQ, 3 * FOX), (C_FF, FOX_HEADS)], w_in, norm_g,
                [[Piece("heads", FOX, last=D.q_s, gain=I["fox_q_norm"][0], scratch=D.q, scale=HD ** -0.5)],
                 [Piece("heads", FOX, nat=tile_rows(D.o_k, D.o_k_s), gain=I["fox_k_norm"][0], scratch=D.k)],
                 [Piece("plain", FOX // 2, nat=tile_rows(D.o_v[:, 0:FOX // 2], D.o_v_s[:, 0:FOX // 2]))],
                 [Piece("plain", FOX // 2, nat=tile_rows(D.o_v[:, FOX // 2:], D.o_v_s[:, FOX // 2:])),
                  Piece("logits", FOX_HEADS, bias=I["b_forget"][0])]],
                [("G", 0), ("H", 0), ("G", 1), ("X",), ("G", 2), ("T", 0), ("H", 1), ("G", 3), ("T", 1)], 4)
        decay_phase(nc, K, D)
        prompt_attention(nc, K, D)
        K.w_raw = a.sb("w_raw", [P, KC, D_MODEL])
        K.w_hi, K.w_lo = a.sb("w_hi", [P, KC, D_MODEL], F32R), a.sb("w_lo", [P, KC, D_MODEL], F32R)
        sample_attention(nc, K, D, I["w_out"][0])
        output_phase(nc, K, D)


_INS = ["x_prompt", "x_sample", "mem_prompt", "cache_fox_k", "cache_fox_v", "cache_fox_logf",
        "state_ssm_re", "state_ssm_im", "cache_mem_k", "cache_mem_v", "norm_g", "w_in", "b_forget",
        "fox_q_norm", "fox_k_norm", "ssm_a_re", "ssm_a_im", "ssm_log_dt", "ssm_b_re", "ssm_b_im",
        "ssm_c_re", "ssm_c_im", "ssm_d", "w_glu", "b_glu", "mem_norm", "w_mem_kv", "mem_q_norm",
        "mem_k_norm", "w_out"]
_OUTS = [("y_prompt", (1, SEQ, D_MODEL)), ("y_sample", (DEC_BATCH, DEC_SEQ, D_MODEL)),
         ("fox_k_prompt", (1, 1, SEQ, FOX_HEADS, HD)), ("fox_v_prompt", (1, 1, SEQ, FOX_HEADS, HD)),
         ("fox_logf_prompt", (1, 1, SEQ, FOX_HEADS)),
         ("ssm_re_prompt", (1, 1, GROUPS, STATE)), ("ssm_im_prompt", (1, 1, GROUPS, STATE)),
         ("mem_k_prompt", (1, 1, N_MEM, MEM_HEADS, HD)), ("mem_v_prompt", (1, 1, N_MEM, MEM_HEADS, HD)),
         ("fox_k_sample", (1, DEC_BATCH, DEC_SEQ, FOX_HEADS, HD)),
         ("fox_v_sample", (1, DEC_BATCH, DEC_SEQ, FOX_HEADS, HD)),
         ("fox_logf_sample", (1, DEC_BATCH, DEC_SEQ, FOX_HEADS)),
         ("ssm_re_sample", (1, DEC_BATCH, GROUPS, STATE)), ("ssm_im_sample", (1, DEC_BATCH, GROUPS, STATE))]


def kernel(**inputs):
    import concourse.bacc as bacc
    from concourse.bass_utils import run_bass_kernel_spmd

    nc = bacc.Bacc("TRN2", target_bir_lowering=False, num_devices=1)
    arrays = {f"in_{n}": np.ascontiguousarray(inputs[n]) for n in _INS}
    ins = {n: nc.dram_tensor(f"in_{n}", arrays[f"in_{n}"].shape, F32, kind="ExternalInput").ap() for n in _INS}
    outs = {n: nc.dram_tensor(f"out_{n}", shape, F32, kind="ExternalOutput").ap() for n, shape in _OUTS}
    build(nc, ins, outs)
    r = run_bass_kernel_spmd(nc, [arrays], core_ids=[0])
    return tuple(r.results[0][f"out_{n}"] for n, _ in _OUTS)
```
